# Optimizing a Trainium2 kernel written in Bass

```python
import jax, jax.numpy as jnp
from jax import lax
import numpy as np

D_MODEL = 1024
BATCH = 1
SEQ = 512
DEPTH = 1

HEAD_DIM = 64
N_ATT_HEADS = (D_MODEL // 2) // HEAD_DIM
N_RWKV_HEADS = (D_MODEL // 2) // HEAD_DIM
ATT_W = N_ATT_HEADS * HEAD_DIM
RWKV_W = N_RWKV_HEADS * HEAD_DIM
MIX_W = ATT_W + RWKV_W
GRID_W = 64
WIN_H = 8
WIN_W = 16
ROWS_PER_BLOCK = 2
D_DECAY_LORA = 64
D_AAA_LORA = 64
D_GATE_LORA = 128
N_DIR = 2
SHIFT_W = 3 * RWKV_W + N_DIR * D_DECAY_LORA + N_DIR * D_AAA_LORA + D_GATE_LORA
IN_PROJ_W = 3 * ATT_W + SHIFT_W
N_EXPERTS = 32
TOP_K = 4
D_EXPERT = D_MODEL
SWIGLU_ALPHA = 1.702
SWIGLU_LIMIT = 7.0
EXPERT_BLOCK = 128
RMS_EPS = 1e-5
GN_EPS = 64e-5

kernel_name = "hybrid_na2d_birwkv7_moe_block"

def rmsnorm(x, w):
    xf = x.astype(jnp.float32)
    y = xf * lax.rsqrt(jnp.mean(xf * xf, axis=-1, keepdims=True) + RMS_EPS)
    return (y * w.astype(jnp.float32)).astype(x.dtype)

def neighbourhood_attention(q, k, v, rpb):
    B, T, H, dh = q.shape
    rows = T // GRID_W
    kh = min(WIN_H, rows)
    kw = WIN_W
    qg = q.reshape(B, rows, GRID_W, H, dh)
    kg = k.reshape(B, rows, GRID_W, H, dh)
    vg = v.reshape(B, rows, GRID_W, H, dh)
    cols = np.arange(GRID_W)
    col_start = np.clip(cols - kw // 2, 0, GRID_W - kw)
    col_idx = col_start[:, None] + np.arange(kw)[None, :]
    dc = col_idx - cols[:, None] + (WIN_W - 1)
    n_blocks = rows // ROWS_PER_BLOCK
    scale = dh ** -0.5

    def block(bi):
        r = bi * ROWS_PER_BLOCK + jnp.arange(ROWS_PER_BLOCK)
        r_start = jnp.clip(r - kh // 2, 0, rows - kh)
        row_idx = r_start[:, None] + jnp.arange(kh)[None, :]
        q_blk = lax.dynamic_slice_in_dim(qg, bi * ROWS_PER_BLOCK, ROWS_PER_BLOCK, axis=1)
        k_win = kg[:, row_idx][:, :, :, col_idx]
        v_win = vg[:, row_idx][:, :, :, col_idx]
        s = jnp.einsum('brchd,bricjhd->bhrcij', q_blk, k_win).astype(jnp.float32) * scale
        dr = row_idx - r[:, None] + (WIN_H - 1)
        bias = rpb[:, dr[:, None, :, None], dc[None, :, None, :]]
        s = s + bias.astype(jnp.float32)[None]
        p = jax.nn.softmax(s.reshape(s.shape[:4] + (kh * kw,)), axis=-1).reshape(s.shape)
        return jnp.einsum('bhrcij,bricjhd->brchd', p.astype(v.dtype), v_win)

    out = lax.map(block, jnp.arange(n_blocks))
    return jnp.moveaxis(out, 0, 1).reshape(B, T, H, dh)

def rwkv7_bidir(p, mu_prev, mu_next, w0, w2, a0, a2, g2, k_k, k_a, r_k, ln_w, ln_b):
    B, T, _ = p.shape
    H, N, C = N_RWKV_HEADS, HEAD_DIM, RWKV_W
    p_prev = jnp.pad(p, ((0, 0), (1, 0), (0, 0)))[:, :-1]
    p_next = jnp.pad(p, ((0, 0), (0, 1), (0, 0)))[:, 1:]
    p = p + mu_prev * (p_prev - p) + mu_next * (p_next - p)
    split_at = list(np.cumsum([C, C, C, N_DIR * D_DECAY_LORA, N_DIR * D_AAA_LORA]))
    r, k, v, dw, da, dg = jnp.split(p, split_at, axis=-1)
    dw = dw.reshape(B, T, N_DIR, D_DECAY_LORA)
    da = da.reshape(B, T, N_DIR, D_AAA_LORA)
    w_log = -jax.nn.softplus(-(w0[:, None, None, :] + jnp.einsum('btzr,zrc->zbtc', jnp.tanh(dw), w2))) - 0.5
    decay = jnp.exp(-jnp.exp(w_log.astype(jnp.float32)))
    a = jax.nn.sigmoid(a0[:, None, None, :] + jnp.einsum('btzr,zrc->zbtc', da, a2))
    g = jax.nn.sigmoid(dg) @ g2
    heads = lambda u: u.reshape(u.shape[:-1] + (H, N))
    kk = heads((k * k_k).astype(jnp.float32))
    kk = kk / jnp.maximum(jnp.sqrt(jnp.sum(kk * kk, axis=-1, keepdims=True)), 1e-12)
    kk_c = kk.reshape(B, T, C)
    k_dir = k[None] * (1.0 + (a - 1.0) * k_a)
    a_kk = a.astype(jnp.float32) * kk_c[None]
    both = lambda u: jnp.broadcast_to(u[None], (N_DIR,) + u.shape)

    def orient(u):
        return jnp.stack([u[0], jnp.flip(u[1], axis=1)])

    to_scan = lambda u: jnp.moveaxis(orient(heads(u.astype(jnp.float32))), 2, 0)
    xs = (to_scan(both(r)), to_scan(decay), to_scan(k_dir), to_scan(both(v)),
          to_scan(both(kk_c)), to_scan(a_kk))

    def step(S, inp):
        r_t, w_t, k_t, v_t, kk_t, akk_t = inp
        sa = jnp.einsum('zbhij,zbhj->zbhi', S, kk_t)
        S = S * w_t[..., None, :] - sa[..., :, None] * akk_t[..., None, :] + v_t[..., :, None] * k_t[..., None, :]
        return S, jnp.einsum('zbhij,zbhj->zbhi', S, r_t)

    S0 = jnp.zeros((N_DIR, B, H, N, N), jnp.float32)
    _, ys = lax.scan(step, S0, xs)
    y = orient(jnp.moveaxis(ys, 0, 2)).sum(axis=0)
    mean = jnp.mean(y, axis=-1, keepdims=True)
    var = jnp.mean((y - mean) ** 2, axis=-1, keepdims=True)
    yn = ((y - mean) * lax.rsqrt(var + GN_EPS)).reshape(B, T, C) * ln_w.astype(jnp.float32) + ln_b.astype(jnp.float32)
    coef = jnp.einsum('bthn,zbthn,hn->bth', heads(r.astype(jnp.float32)), heads(k_dir.astype(jnp.float32)),
                      r_k.astype(jnp.float32))
    bonus = (coef[..., None] * heads(v.astype(jnp.float32))).reshape(B, T, C)
    return ((yn + bonus) * g.astype(jnp.float32)).astype(p.dtype)

def clamped_swiglu(hcat):
    gate, lin = hcat[:, :D_EXPERT], hcat[:, D_EXPERT:]
    gate = jnp.minimum(gate, SWIGLU_LIMIT)
    lin = jnp.clip(lin, -SWIGLU_LIMIT, SWIGLU_LIMIT)
    return (lin + 1.0) * (gate * jax.nn.sigmoid(SWIGLU_ALPHA * gate))

def moe(x2d, router_w, router_b, w_up, b_up, w_down, b_down):
    M, D = x2d.shape
    logits = (x2d @ router_w + router_b).astype(jnp.float32)
    top_val, top_idx = lax.top_k(logits, TOP_K)
    gates = jax.nn.softmax(top_val, axis=-1)
    A = M * TOP_K
    e_flat = top_idx.reshape(A)
    tok_flat = jnp.arange(A, dtype=jnp.int32) // TOP_K
    g_flat = gates.reshape(A)
    order = jnp.argsort(e_flat)
    e_s, tok_s, g_s = e_flat[order], tok_flat[order], g_flat[order]
    counts = jnp.bincount(e_flat, length=N_EXPERTS)
    padded = (counts + EXPERT_BLOCK - 1) // EXPERT_BLOCK * EXPERT_BLOCK
    start = jnp.cumsum(counts) - counts
    pend = jnp.cumsum(padded)
    pstart = pend - padded
    dest = pstart[e_s] + (jnp.arange(A) - start[e_s])
    P = -(-(A + N_EXPERTS * EXPERT_BLOCK) // EXPERT_BLOCK) * EXPERT_BLOCK
    n_blk = P // EXPERT_BLOCK
    row_tok = jnp.zeros((P,), jnp.int32).at[dest].set(tok_s)
    x_buf = x2d[row_tok].reshape(n_blk, EXPERT_BLOCK, D)
    blk_expert = jnp.searchsorted(pend, jnp.arange(n_blk) * EXPERT_BLOCK, side='right')
    blk_expert = jnp.minimum(blk_expert, N_EXPERTS - 1)

    def expert_block(args):
        xb, e = args
        hcat = xb @ w_up[e] + b_up[e]
        return clamped_swiglu(hcat) @ w_down[e] + b_down[e]

    y_buf = lax.map(expert_block, (x_buf, blk_expert)).reshape(P, D)
    contrib = g_s[:, None].astype(x2d.dtype) * y_buf[dest]
    return jax.ops.segment_sum(contrib, tok_s, num_segments=M)

def setup_inputs(seed: int = 0) -> dict:
    key = jax.random.key(seed)
    ks = jax.random.split(key, 32)
    L, D, C = DEPTH, D_MODEL, RWKV_W
    nrm = lambda k, s, sc: jax.random.normal(k, s, jnp.float32) * sc
    return {
        "x": nrm(ks[0], (BATCH, SEQ, D), 1.0),
        "norm1_w": 1.0 + nrm(ks[1], (L, D), 0.05),
        "w_in": nrm(ks[2], (L, D, IN_PROJ_W), D ** -0.5),
        "attn_rpb": nrm(ks[3], (L, N_ATT_HEADS, 2 * WIN_H - 1, 2 * WIN_W - 1), 0.1),
        "attn_norm_w": 1.0 + nrm(ks[4], (L, ATT_W), 0.05),
        "rwkv_mu_prev": jax.random.uniform(ks[5], (L, SHIFT_W), jnp.float32, 0.0, 0.5),
        "rwkv_mu_next": jax.random.uniform(ks[6], (L, SHIFT_W), jnp.float32, 0.0, 0.5),
        "rwkv_w0": nrm(ks[7], (L, N_DIR, C), 0.5),
        "rwkv_w2": nrm(ks[8], (L, N_DIR, D_DECAY_LORA, C), 0.1),
        "rwkv_a0": nrm(ks[9], (L, N_DIR, C), 0.5),
        "rwkv_a2": nrm(ks[10], (L, N_DIR, D_AAA_LORA, C), 0.1),
        "rwkv_g2": nrm(ks[11], (L, D_GATE_LORA, C), D_GATE_LORA ** -0.5),
        "rwkv_k_k": 0.85 + nrm(ks[12], (L, C), 0.05),
        "rwkv_k_a": 1.0 + nrm(ks[13], (L, C), 0.05),
        "rwkv_r_k": nrm(ks[14], (L, N_RWKV_HEADS, HEAD_DIM), 0.1),
        "rwkv_ln_w": 1.0 + nrm(ks[15], (L, C), 0.05),
        "rwkv_ln_b": nrm(ks[16], (L, C), 0.01),
        "w_o": nrm(ks[17], (L, MIX_W, D), MIX_W ** -0.5),
        "norm2_w": 1.0 + nrm(ks[18], (L, D), 0.05),
        "router_w": nrm(ks[19], (L, D, N_EXPERTS), D ** -0.5),
        "router_b": nrm(ks[20], (L, N_EXPERTS), 0.01),
        "expert_w_up": nrm(ks[21], (L, N_EXPERTS, D, 2 * D_EXPERT), D ** -0.5),
        "expert_b_up": nrm(ks[22], (L, N_EXPERTS, 2 * D_EXPERT), 0.01),
        "expert_w_down": nrm(ks[23], (L, N_EXPERTS, D_EXPERT, D), D_EXPERT ** -0.5),
        "expert_b_down": nrm(ks[24], (L, N_EXPERTS, D), 0.01),
        "final_norm_w": 1.0 + nrm(ks[25], (D,), 0.05),
    }

def reference(x, norm1_w, w_in, attn_rpb, attn_norm_w, rwkv_mu_prev, rwkv_mu_next, rwkv_w0, rwkv_w2,
              rwkv_a0, rwkv_a2, rwkv_g2, rwkv_k_k, rwkv_k_a, rwkv_r_k, rwkv_ln_w, rwkv_ln_b, w_o,
              norm2_w, router_w, router_b, expert_w_up, expert_b_up, expert_w_down, expert_b_down,
              final_norm_w):
    B, T, D = x.shape
    h = x
    for l in range(DEPTH):
        hn = rmsnorm(h, norm1_w[l])
        proj = hn @ w_in[l]
        q = proj[..., :ATT_W].reshape(B, T, N_ATT_HEADS, HEAD_DIM)
        k = proj[..., ATT_W:2 * ATT_W].reshape(B, T, N_ATT_HEADS, HEAD_DIM)
        v = proj[..., 2 * ATT_W:3 * ATT_W].reshape(B, T, N_ATT_HEADS, HEAD_DIM)
        att = neighbourhood_attention(q, k, v, attn_rpb[l]).reshape(B, T, ATT_W)
        att = rmsnorm(att, attn_norm_w[l])
        rk = rwkv7_bidir(proj[..., 3 * ATT_W:], rwkv_mu_prev[l], rwkv_mu_next[l], rwkv_w0[l], rwkv_w2[l],
                         rwkv_a0[l], rwkv_a2[l], rwkv_g2[l], rwkv_k_k[l], rwkv_k_a[l], rwkv_r_k[l],
                         rwkv_ln_w[l], rwkv_ln_b[l])
        h = h + jnp.concatenate([att, rk], axis=-1) @ w_o[l]
        hn = rmsnorm(h, norm2_w[l])
        h = h + moe(hn.reshape(B * T, D), router_w[l], router_b[l], expert_w_up[l], expert_b_up[l],
                    expert_w_down[l], expert_b_down[l]).reshape(B, T, D)
    return rmsnorm(h, final_norm_w)


_drawn_inputs = setup_inputs


def setup_inputs(seed=0):
    import zlib

    import numpy as np

    out = dict(_drawn_inputs(seed))
    spreads = {}
    factors = {'rwkv_ln_b': 7.773, 'expert_b_up': 8.0, 'expert_b_down': 8.0}
    for name, (base, spread) in spreads.items():
        noise = np.random.default_rng([zlib.crc32(name.encode()), seed]).standard_normal(out[name].shape)
        drawn = base * np.exp(spread * noise) if base else spread * noise
        out[name] = __import__('jax').numpy.asarray(drawn.astype(out[name].dtype))
    for name, factor in factors.items():
        out[name] = (out[name] * factor).astype(out[name].dtype)
    return out
```

```python
from contextlib import ExitStack

import numpy as np

import concourse.bass as bass
from concourse import mybir

ALU = mybir.AluOpType
ACT = mybir.ActivationFunctionType
AX = mybir.AxisListType
F32 = mybir.dt.float32
F32R = mybir.dt.float32r
BF16 = mybir.dt.bfloat16
I32 = mybir.dt.int32
U32 = mybir.dt.uint32

P = 128
D = 1024
T = 512
NT = T // P
KD = D // P
HD = 64
NH = 8
C = NH * HD
NPAIR = NH // 2
GRID = 64
ROWS = T // GRID
WIN = 16
LORA_TILES = 3
NTILE = 6 * NPAIR + LORA_TILES
TQ, TK, TV, TR, TRK, TRV, TDW, TDA, TDG = 0, 4, 8, 12, 16, 20, 24, 25, 26
N_ATT_TILES = 12
E = 32
F = 1024
TOPK = 4
RMS_EPS = 1e-5
GN_EPS = 64e-5
KAPPA = float(np.exp(-0.5))
ds = bass.ds


class Banks:

    def __init__(self, sem, name, psum, keys):
        n = len(psum)
        self.psum = psum
        self.at = {k: (i % n, i // n) for i, k in enumerate(keys)}
        assert len(self.at) == len(keys)
        self.per = [len([i for i in range(len(keys)) if i % n == b]) for b in range(n)]
        self.filled = [sem(f"{name}_filled{b}") for b in range(n)]
        self.freed = [sem(f"{name}_freed{b}") for b in range(n)]

    def tile(self, key):
        return self.psum[self.at[key][0]]

    def fill_sem(self, key):
        return self.filled[self.at[key][0]]

    def free_sem(self, key):
        return self.freed[self.at[key][0]]

    def count(self, it, key):
        b, o = self.at[key]
        return it * self.per[b] + (o + 1)

    def before(self, it, key):
        return self.count(it, key)

    def after(self, it, key):
        b, o = self.at[key]
        return it * self.per[b] + (o + 2)


def phase_semaphores(nc, ctx, phase):
    mine = []

    def finish():
        nc.clear_and_free_semaphores(mine)
        nc.all_engine_barrier(sem_only=True)

    ctx.callback(finish)

    def sem(name):
        mine.append(nc.alloc_semaphore(f"{phase}_{name}"))
        return mine[-1]

    return sem


def vec_rows():
    at, out = 0, {}
    for name, n in (("norm1_w", KD), ("norm2_w", KD), ("attn_norm_w", 4), ("mu_prev", 15), ("mu_next", 15),
                    ("w0", 8), ("a0", 8), ("k_k", 4), ("k_a", 4), ("r_k", 4)):
        out[name] = (at, n)
        at += n
    return out, at


def flat2(ap):
    return ap.rearrange("p a b -> p (a b)")


def in_projection(nc, psum, ext, keep):
    rows, nrows = vec_rows()
    with ExitStack() as ctx:
        sb = lambda name, shape, dt=F32: ctx.enter_context(nc.sbuf_tensor("proj_" + name, shape, dt))
        sem = phase_semaphores(nc, ctx, "proj")
        x, PTa, PTb, ident, vec = (keep[k] for k in ("x", "PTa", "PTb", "ident", "vec"))
        xn = sb("xn", [P, NT, D])
        x_hi = sb("x_hi", [P, KD, T], F32R)
        x_lo = sb("x_lo", [P, KD, T], F32R)
        ss = sb("ss", [P, NT])
        rs = sb("rs", [P, NT])
        vrow = sb("vrow", [nrows, P])
        keepw = sb("shift_keep", [P, NTILE])
        prevw = sb("shift_prev", [P, NTILE])
        nextw = sb("shift_next", [P, NTILE])
        NS = 4
        CW = 3 * P
        raw = sb("w_raw", [P, NS, 2 * CW])
        w_hi = sb("w_hi", [P, NS, 2 * CW], F32R)
        w_lo = sb("w_lo", [P, NS, 2 * CW], F32R)
        NCH = NTILE // 3
        OUTS = ((0, 2, PTa, 0), (2, 4, PTb, N_ATT_TILES))
        x_in = [sem(f"x_in{t}") for t in range(NT)]
        c_in = sem("consts_in")
        v_in = sem("vectors_in")
        sumsq = sem("sumsq_done")
        ms_done = sem("meansq_done")
        root = sem("root_done")
        rstd = sem("rstd_done")
        xn_done = sem("xn_done")
        turned = sem("x_turned")
        hi_x = sem("x_hi_done")
        lo_x = sem("x_lo_done")
        vt = sem("vectors_turned")
        vec_ok = sem("vec_done")
        shw = sem("shift_weights_done")
        raw_in = [sem(f"w_raw_in{s}") for s in range(NS)]
        hi_w = [sem(f"w_hi_done{s}") for s in range(NS)]
        lo_w = [sem(f"w_lo_done{s}") for s in range(NS)]
        used = [sem(f"w_used{s}") for s in range(NS)]
        kept = sem("own_part_done")
        prevd = sem("prev_part_done")
        nextd = sem("next_part_done")
        B = Banks(sem, "inproj", psum, [(h, j) for h in range(2) for j in range(3)])
        w_dram = ext["w_in"].rearrange("(k p) n -> p k n", p=P)

        block = ctx.enter_context(nc.Block())

        @block.sync
        def _(sp):
            for name, (r, n) in rows.items():
                sp.dma_start(vrow[r:r + n, :], ext[name]).then_inc(v_in, 16)
            sp.dma_start(ident[:, :], ext["c_ident"]).then_inc(c_in, 16)

            def load_chunk(c):
                for s in range(NS):
                    sp.wait_ge(lo_w[s], c + 1)
                    sp.dma_start(raw[:, s, :].rearrange("p (k n) -> p k n", k=2),
                                 w_dram[:, 2 * s:2 * s + 2, ds(CW * c, CW)]).then_inc(raw_in[s], 16)

            with sp.Fori(0, NCH) as c:
                load_chunk(c)

        @block.scalar
        def _(act):
            xd = ext["x"].rearrange("(t p) d -> p t d", p=P)
            for t in range(NT):
                act.dma_start(x[:, t, :], xd[:, t, :]).then_inc(x_in[t], 16)
            for t in range(NT):
                act.wait_ge(x_in[t], 16)
                act.activation(xn[:, t, :], x[:, t, :], ACT.Square, accum_out=ss[:, t:t + 1]).then_inc(sumsq, 1)
                act.wait_ge(ms_done, t + 1)
                act.activation(rs[:, t:t + 1], rs[:, t:t + 1], ACT.Sqrt).then_inc(root, 1)

            def split_w(c, s, it=None, h=None):
                act.wait_ge(raw_in[s], 16 * c + 16)
                if it is not None:
                    if s < NS - 1:
                        act.wait_ge(used[s], 2 * it + h + 1)
                    else:
                        act.wait_ge(B.fill_sem((h, 2)), B.count(it, (h, 2)))
                act.activation(w_hi[:, s, :], raw[:, s, :], ACT.Copy).then_inc(hi_w[s], 1)

            def own_part(it, h, j, PT, first):
                g = 6 * it + 3 * h + j
                key = (h, j)
                act.wait_ge(B.fill_sem(key), B.count(it, key))
                act.activation(flat2(PT[:, ds(g - first, 1), :]), B.tile(key)[:, :], ACT.Identity,
                               scale=keepw[:, ds(g, 1)]).then_inc(kept, 1)

            for s in range(NS):
                split_w(0, s)
            act.wait_ge(vec_ok, 1)
            for k in range(KD):
                act.wait_ge(turned, k + 1)
                act.activation(x_hi[:, k, :], psum[k][:, :], ACT.Identity,
                               scale=vec[:, rows["norm1_w"][0] + k:rows["norm1_w"][0] + k + 1]).then_inc(hi_x, 1)
            act.wait_ge(shw, 5)
            for i0, i1, PT, first in OUTS:
                with act.Fori(i0, i1) as it:
                    for h in range(2):
                        for s in range(NS):
                            split_w(2 * it + h + 1, s, it, h)
                        for j in range(3):
                            own_part(it, h, j, PT, first)
            for j in range(3):
                own_part(NCH // 2, 0, j, PT, first)

        @block.gpsimd
        def _(pool):
            for s in range(NS):
                pool.sem_inc(lo_w[s], 1)
            for b in range(len(psum)):
                pool.sem_inc(B.freed[b], 1)

        @block.vector
        def _(dve):
            for t in range(NT):
                dve.wait_ge(sumsq, t + 1)
                dve.tensor_scalar(rs[:, t:t + 1], ss[:, t:t + 1], 1.0 / D, RMS_EPS, ALU.mult, ALU.add).then_inc(ms_done, 1)
                dve.wait_ge(root, t + 1)
                dve.reciprocal(rs[:, t:t + 1], rs[:, t:t + 1]).then_inc(rstd, 1)
                dve.wait_ge(rstd, t + 1)
                dve.tensor_scalar(xn[:, t, :], x[:, t, :], rs[:, t:t + 1], None, ALU.mult).then_inc(xn_done, 1)
            dve.wait_ge(vt, 1)
            dve.tensor_copy(vec[:, :], psum[0][:, 0:nrows]).then_inc(vec_ok, 1)
            dve.wait_ge(vec_ok, 1)
            dve.memset(prevw[:, 0:N_ATT_TILES], 0.0)
            dve.memset(nextw[:, 0:N_ATT_TILES], 0.0)
            m0, m1 = rows["mu_prev"][0], rows["mu_next"][0]
            dve.tensor_copy(prevw[:, N_ATT_TILES:NTILE], vec[:, m0:m0 + 15]).then_inc(shw, 1)
            dve.tensor_copy(nextw[:, N_ATT_TILES:NTILE], vec[:, m1:m1 + 15]).then_inc(shw, 1)
            dve.wait_ge(shw, 2)
            dve.memset(keepw[:, 0:4], HD ** -0.5)
            dve.memset(keepw[:, 4:N_ATT_TILES], 1.0)
            dve.tensor_scalar(keepw[:, N_ATT_TILES:NTILE], prevw[:, N_ATT_TILES:NTILE], -1.0, 1.0,
                              ALU.mult, ALU.add).then_inc(shw, 1)
            dve.wait_ge(shw, 3)
            dve.tensor_tensor(keepw[:, N_ATT_TILES:NTILE], keepw[:, N_ATT_TILES:NTILE],
                              nextw[:, N_ATT_TILES:NTILE], ALU.subtract).then_inc(shw, 2)

            def split_w(c, s):
                dve.wait_ge(hi_w[s], c + 1)
                dve.tensor_tensor(w_lo[:, s, :], raw[:, s, :], w_hi[:, s, :].bitcast(F32), ALU.subtract).then_inc(lo_w[s], 1)

            def other_parts(it, h, j, PT, first):
                g = 6 * it + 3 * h + j
                key = (h, j)
                b = B.tile(key)
                dst = flat2(PT[:, ds(g - first, 1), :])
                dve.wait_ge(kept, g + 1)
                dve.scalar_tensor_tensor(out=dst[:, 1:T], in0=b[:, 0:T - 1], scalar=prevw[:, ds(g, 1)], in1=dst[:, 1:T],
                                         op0=ALU.mult, op1=ALU.add).then_inc(prevd, 1)
                dve.wait_ge(prevd, g + 1)
                dve.scalar_tensor_tensor(out=dst[:, 0:T - 1], in0=b[:, 1:T], scalar=nextw[:, ds(g, 1)],
                                         in1=dst[:, 0:T - 1], op0=ALU.mult, op1=ALU.add).then_inc(B.free_sem(key), 1)

            for s in range(NS):
                split_w(0, s)
            for k in range(KD):
                dve.wait_ge(hi_x, k + 1)
                ins = dve.scalar_tensor_tensor(out=x_lo[:, k, :], in0=psum[k][:, :],
                                               scalar=vec[:, rows["norm1_w"][0] + k:rows["norm1_w"][0] + k + 1],
                                               in1=x_hi[:, k, :].bitcast(F32), op0=ALU.mult, op1=ALU.subtract)
                ins.then_inc(lo_x, 1)
            for i0, i1, PT, first in OUTS:
                with dve.Fori(i0, i1) as it:
                    for h in range(2):
                        for s in range(NS):
                            split_w(2 * it + h + 1, s)
                        for j in range(3):
                            other_parts(it, h, j, PT, first)
            for j in range(3):
                other_parts(NCH // 2, 0, j, PT, first)

        @block.tensor
        def _(pe):
            pe.wait_ge(c_in, 16)
            pe.wait_ge(v_in, 16 * len(rows))
            pe.transpose(psum[0][:, 0:nrows], vrow[:, :], ident[0:nrows, 0:nrows]).then_inc(vt, 1)
            pe.wait_ge(vec_ok, 1)
            for t in range(NT):
                pe.wait_ge(xn_done, t + 1)
                for k in range(KD):
                    ins = pe.transpose(psum[k][:, P * t:P * t + P], xn[:, t, P * k:P * k + P], ident[:, :])
                    if t == NT - 1:
                        ins.then_inc(turned, 1)

            def chunk(it, h):
                c = 2 * it + h
                for s in range(NS):
                    pe.wait_ge(lo_w[s], c + 2)
                    for k2 in range(2):
                        k = 2 * s + k2
                        for j in range(3):
                            key = (h, j)
                            if k == 0:
                                pe.wait_ge(B.free_sem(key), B.before(it, key))
                            out = B.tile(key)[:, :]
                            w = slice(k2 * CW + j * P, k2 * CW + j * P + P)
                            pe.matmul(out, w_hi[:, s, w], x_hi[:, k, :], start=(k == 0), stop=False)
                            pe.matmul(out, w_hi[:, s, w], x_lo[:, k, :], start=False, stop=False)
                            ins = pe.matmul(out, w_lo[:, s, w], x_hi[:, k, :], start=False, stop=(k == KD - 1))
                            if k == KD - 1:
                                ins.then_inc(B.fill_sem(key), 1)
                    if s < NS - 1:
                        ins.then_inc(used[s], 1)

            pe.wait_ge(lo_x, KD)
            with pe.Fori(0, NCH // 2) as it:
                for h in range(2):
                    chunk(it, h)
            chunk(NCH // 2, 0)


PADC = 8
PGRID = GRID + 2 * PADC
QC = 16
KC = QC + WIN
RPBH = 15 * 31
RPB_PAD = 16


def attention(nc, psum, ext, keep, vpad):
    with ExitStack() as ctx:
        sb = lambda name, shape, dt=F32: ctx.enter_context(nc.sbuf_tensor("att_" + name, shape, dt))
        sem = phase_semaphores(nc, ctx, "att")
        PT, ident, att = keep["PTa"], keep["ident"], keep["att"]
        v_nat = sb("v_nat", [P, NT, C])
        zero = sb("zero", [P, C])
        kpad = sb("k_padded", [P, NPAIR, ROWS, PGRID])
        bias = sb("bias_table", [P, NH * ROWS, KC])
        mask = sb("mask_table", [P, NT, KC])
        tab = sb("bias_and_mask", [P, NH * ROWS, KC])
        vw = sb("v_windows", [P, NT, 2, C])
        qw = sb("q_window", [P, NPAIR, ROWS, QC])
        kw = sb("k_window", [P, NPAIR, ROWS, KC])
        sc = sb("scores", [P, 2, 2, ROWS * KC])
        pT = sb("probs_turned", [P, 2, 4, P])
        nmax = sb("neg_max", [P, NPAIR, 2])
        sums = sb("exp_sums", [P, NPAIR, 2])
        rec = sb("recip_sums", [P, NPAIR, 2])
        zeroed = sem("zeroed")
        bias_in = sem("bias_in")
        mask_in = sem("mask_in")
        v_out = sem("v_padded_out")
        pads_out = sem("pads_out")
        vw_in = sem("v_windows_in")
        kp_ok = sem("k_padded_done")
        win = sem("windows_done")
        tabd = sem("table_done")
        scd = sem("scores_biased")
        maxd = sem("max_done")
        expd = sem("exp_done")
        rcd = sem("recip_done")
        V = Banks(sem, "vturn", psum[:4], [(t,) for t in range(NT)])
        order = []
        for i in range(NPAIR + 2):
            order += [("S", i)] * (i < NPAIR) + [("T", i - 1)] * (1 <= i <= NPAIR) + [("O", i - 2)] * (i >= 2)
        A = Banks(sem, "att", psum, order)
        vp = vpad.rearrange("(r c) n -> r c n", c=PGRID)

        def heads(u):
            return 4 * (u // 2) + u % 2, 4 * (u // 2) + u % 2 + 2

        block = ctx.enter_context(nc.Block())

        @block.sync
        def _(sp):
            sp.dma_start(mask[:, :, :], ext["c_att_mask"].rearrange("p (t k) -> p t k", t=NT)).then_inc(mask_in, 16)
            for r in range(ROWS):
                sp.dma_start(bias[QC * r:QC * r + QC, :, :].rearrange("c (h k) x -> c h k x", h=NH),
                             ext["rpb"][:, :, ROWS - 1 - r:2 * ROWS - 1 - r, :]).then_inc(bias_in, 16)
            sp.wait_ge(zeroed, 1)
            sp.dma_start(vp[:, 0:PADC, :], zero[0:GRID, :]).then_inc(pads_out, 16)
            sp.dma_start(vp[:, PADC + GRID:PGRID, :], zero[0:GRID, :]).then_inc(pads_out, 16)
            for t in range(NT):
                sp.wait_ge(V.free_sem((t,)), V.after(0, (t,)))
                sp.dma_start(vp[2 * t:2 * t + 2, PADC:PADC + GRID, :], v_nat[:, t, :]).then_inc(v_out, 16)
            sp.wait_ge(v_out, 16 * NT)
            sp.wait_ge(pads_out, 32)
            for jt in range(NT):
                for hf in range(2):
                    sp.dma_start(vw[:, jt, hf, :], vp[4 * hf:4 * hf + 4, QC * jt:QC * jt + KC, :]).then_inc(vw_in, 16)

        @block.gpsimd
        def _(pool):
            for b in range(4):
                pool.sem_inc(V.freed[b], 1)
            for b in range(8):
                pool.sem_inc(A.freed[b], 1)
            pool.memset(zero[:, :], 0.0).then_inc(zeroed, 1)
            pool.memset(kpad[:, :, :, 0:PADC], 0.0)
            pool.memset(kpad[:, :, :, PADC + GRID:PGRID], 0.0)
            for p in range(NPAIR):
                pool.tensor_copy(kpad[:, p, :, PADC:PADC + GRID],
                                 PT[:, TK + p, :].rearrange("p (r c) -> p r c", c=GRID)).then_inc(kp_ok, 1)
            pool.wait_ge(kp_ok, NPAIR)
            pool.wait_ge(mask_in, 16)
            pool.wait_ge(bias_in, 16 * ROWS)
            with pool.Fori(0, NT) as jt:
                for p in range(NPAIR):
                    for u in (p // 2 * 2, p // 2 * 2 + 1):
                        pool.wait_ge(A.free_sem(("S", u)), A.before(jt, ("S", u)))
                    pool.tensor_copy(qw[:, p, :, :], PT[:, TQ + p, :].rearrange("p (r c) -> p r c", c=GRID)
                                     [:, :, ds(QC * jt, QC)])
                    pool.tensor_copy(kw[:, p, :, :], kpad[:, p, :, ds(QC * jt, KC)]).then_inc(win, 1)
                    rows = slice(2 * ROWS * p, 2 * ROWS * p + 2 * ROWS)
                    pool.tensor_tensor(tab[:, rows, :], bias[:, rows, :],
                                       mask[:, ds(jt, 1), :].to_broadcast([P, 2 * ROWS, KC]), ALU.add).then_inc(tabd, 1)

        @block.tensor
        def _(pe):
            for t in range(NT):
                for p in range(NPAIR):
                    ins = pe.transpose(V.tile((t,))[:, P * p:P * p + P], PT[:, TV + p, P * t:P * t + P], ident[:, :])
                ins.then_inc(V.fill_sem((t,)), 1)
            for t in range(NT):
                pe.wait_ge(V.free_sem((t,)), V.after(0, (t,)))

            def scores(jt, u):
                key = ("S", u)
                pe.wait_ge(win, 4 * jt + u // 2 * 2 + 2)
                pe.wait_ge(A.free_sem(key), A.before(jt, key))
                half = slice(HD * (u % 2), HD * (u % 2) + HD)
                for n in range(2):
                    pair = u // 2 * 2 + n
                    ins = pe.matmul(A.tile(key)[:, 256 * n:256 * n + 256],
                                    qw[half, pair, :, :].rearrange("p r c -> p (r c)"),
                                    kw[half, pair, :, :].rearrange("p r c -> p (r c)"), start=True, stop=True)
                ins.then_inc(A.fill_sem(key), 1)

            def turn(jt, p):
                key = ("T", p)
                pe.wait_ge(expd, 8 * jt + 2 * p + 2)
                pe.wait_ge(A.free_sem(key), A.before(jt, key))
                for h in range(2):
                    for hf in range(2):
                        q = 2 * h + hf
                        ins = pe.transpose(A.tile(key)[:, P * q:P * q + P], sc[:, p % 2, h, P * hf:P * hf + P], ident[:, :])
                ins.then_inc(A.fill_sem(key), 1)

            def values(jt, p):
                key = ("O", p)
                pe.wait_ge(A.free_sem(("T", p)), A.after(jt, ("T", p)))
                pe.wait_ge(A.free_sem(key), A.before(jt, key))
                for h in range(2):
                    for hf in range(2):
                        v = vw[:, ds(jt, 1), hf, HD * heads(p)[h]:HD * heads(p)[h] + HD].rearrange("p a b -> p (a b)")
                        ins = pe.matmul(A.tile(key)[:, HD * h:HD * h + HD], pT[:, p % 2, 2 * h + hf, :], v,
                                        start=(hf == 0), stop=(hf == 1))
                ins.then_inc(A.fill_sem(key), 1)

            pe.wait_ge(vw_in, 16 * 2 * NT)
            with pe.Fori(0, NT) as jt:
                for i in range(NPAIR + 2):
                    if i < NPAIR:
                        scores(jt, i)
                    if 1 <= i <= NPAIR:
                        turn(jt, i - 1)
                    if i >= 2:
                        values(jt, i - 2)

        @block.scalar
        def _(act):
            for t in range(NT):
                act.wait_ge(V.fill_sem((t,)), 1)
                act.activation(v_nat[:, t, :], V.tile((t,))[:, :], ACT.Copy).then_inc(V.free_sem((t,)), 1)

            def exps(jt, p):
                act.wait_ge(maxd, 4 * jt + p + 1)
                for h in range(2):
                    act.activation(sc[:, p % 2, h, :], sc[:, p % 2, h, :], ACT.Exp, bias=nmax[:, p, h:h + 1],
                                   accum_out=sums[:, p, h:h + 1]).then_inc(expd, 1)

            def probs(jt, p):
                key = ("T", p)
                act.wait_ge(A.fill_sem(key), A.count(jt, key))
                act.activation(pT[:, p % 2, :, :].rearrange("p a b -> p (a b)"), A.tile(key)[:, :], ACT.Copy)\
                   .then_inc(A.free_sem(key), 1)

            with act.Fori(0, NT) as jt:
                for i in range(NPAIR + 1):
                    if i < NPAIR:
                        exps(jt, i)
                    if i >= 1:
                        probs(jt, i - 1)

        @block.vector
        def _(dve):
            def biased(jt, p):
                key = ("S", p)
                dve.wait_ge(A.fill_sem(key), A.count(jt, key))
                dve.wait_ge(tabd, 4 * jt + p // 2 * 2 + 2)
                both = tab[:, :, :].rearrange("p (h r) k -> p h (r k)", h=NH)[:, heads(p)[0]:heads(p)[1] + 1:2, :]
                dve.tensor_tensor(sc[:, p % 2, :, :], A.tile(key).rearrange("p (h k) -> p h k", h=2), both,
                                  ALU.add).then_inc(A.free_sem(key), 1)
                dve.wait_ge(A.free_sem(key), A.after(jt, key))
                dve.tensor_reduce(nmax[:, p, :], sc[:, p % 2, :, :], AX.X, ALU.max, negate=True).then_inc(maxd, 1)

            def out(jt, p):
                key = ("O", p)
                dve.wait_ge(expd, 8 * jt + 2 * p + 2)
                dve.reciprocal(rec[:, p, :], sums[:, p, :]).then_inc(rcd, 1)
                dve.wait_ge(rcd, 4 * jt + p + 1)
                dve.wait_ge(A.fill_sem(key), A.count(jt, key))
                dst = att[:, ds(jt, 1), :].rearrange("p a (h d) -> p (a h) d", h=NH)[:, heads(p)[0]:heads(p)[1] + 1:2, :]
                dve.tensor_tensor(dst, A.tile(key)[:, 0:P].rearrange("p (h d) -> p h d", h=2),
                                  rec[:, p, :].unsqueeze(2).to_broadcast([P, 2, HD]), ALU.mult)\
                   .then_inc(A.free_sem(key), 1)

            with dve.Fori(0, NT) as jt:
                for i in range(NPAIR + 2):
                    if i < NPAIR:
                        biased(jt, i)
                    if i >= 2:
                        out(jt, i - 2)


class Chain:

    def __init__(self, eng, sem, it=0, per=0):
        self.eng, self.sem, self.base, self.n = eng, sem, it * per, 0

    def __call__(self, ins):
        self.n += 1
        ins.then_inc(self.sem, 1)
        self.eng.wait_ge(self.sem, self.base + self.n)


NLEV = 7
NCK = NT


def rwkv_keys():
    keys = [("L", what, z) for z in range(2) for what in "wa"]
    keys += [("N", z, a) for z in range(2) for a in range(3)]
    keys += [("X", z, c, h) for z in range(2) for c in range(NCK) for h in range(2)]
    keys += [("K",)]
    keys += [("T", 1, g) for g in range(4)]
    for lv in range(2, NLEV + 1):
        for s in "WZT" if lv < NLEV else "WZ":
            keys += [(s, lv, g) for g in range(4)]
    keys += [("U", g) for g in range(4)] + [("V", z) for z in range(2)]
    for n in range(NCK):
        keys += [("A", n, h) for h in range(2)]
        keys += [("S", n, h) for h in range(2)] if n < NCK - 1 else []
        keys += [("Y", n, h) for h in range(2)]
    return keys


def rwkv(nc, psum, ext, keep):
    rows, nrows = vec_rows()
    with ExitStack() as ctx:
        sb = lambda name, shape, dt=F32: ctx.enter_context(nc.sbuf_tensor("rwkv_" + name, shape, dt))
        sem = phase_semaphores(nc, ctx, "rwkv")
        PT, ident, vec, Y = keep["PTb"], keep["ident"], keep["vec"], keep["rk"]
        R0, K0, V0, DW, DA, DG = 0, 4, 8, 12, 13, 14
        VN, coef = keep["VN"], keep["coef"]
        KK = sb("kk", [P, NPAIR, T])
        w2 = sb("w2", [P, C])
        a2 = sb("a2", [P, C])
        consts = sb("rw_consts", [P, 2 * 512 + NLEV * P + P + 2])
        scmask = [consts[:, 512 * z:512 * z + 512] for z in range(2)]
        lvmask = [consts[:, 1024 + P * i:1024 + P * i + P] for i in range(NLEV)]
        headsum = consts[:, 1024 + NLEV * P:1024 + NLEV * P + P]
        headone = consts[:, 1024 + NLEV * P + P:1024 + NLEV * P + P + 2]
        reset = sb("scan_reset", [P, T])
        w2s = sb("w2_part", [P, P])
        a2s = sb("a2_part", [P, P])
        VS = sb("v_part", [P, NT, P])
        sg = sb("decay_sig", [P, 2, T])
        aa = sb("a_gate", [P, 2, T])
        Ps = sb("decay_sums", [P, T])
        D1 = sb("d_incl", [P, T])
        D2 = sb("d_excl", [P, T])
        E3 = sb("e_neg", [P, T])
        kds = sb("k_dirs", [P, T])
        tmp = sb("rw_tmp", [P, T])
        mid = sb("mids", [P, 2, 2 * NCK])
        G = sb("chunk_decay", [P, 2, NCK])
        QR = [sb(f"qr{z}", [P, NCK, 2 * P]) for z in range(2)]
        KD = [sb(f"kd{z}", [P, T]) for z in range(2)]
        AD = [sb(f"ad{z}", [P, T]) for z in range(2)]
        nat = [[sb(f"nat{z}{a}", [P, NCK, P]) for a in range(3)] for z in range(2)]
        SC = [sb(f"sc{g}", [P, NCK, 512]) for g in range(4)]
        X = [sb(f"x{g}", [P, NCK, P]) for g in range(4)]
        XT = [sb(f"xt{g}", [P, NCK, P]) for g in range(4)]
        W1 = [sb(f"w1{g}", [P, NCK, P]) for g in range(4)]
        WT = XT[0:2]
        U0 = [W1[g][:, :, 0:HD] for g in range(4)]
        SA = sb("sa", [P, 2, 2, HD])
        S = [sb(f"state{z}", [P, 2, HD]) for z in range(2)]
        PREP = 18

        c_in = sem("rw_consts_in")
        w_in = sem("lora_in")
        lora_act = sem("lora_activated")
        rst = sem("reset_done")
        kraw = sem("kk_scaled")
        ksq = sem("kk_squared")
        kroot = sem("kk_root")
        kch = sem("kk_chain")
        kkok = sem("kk_done")
        parts = sem("parts_done")
        sgd = sem("sigmoids_done")
        pch = sem("prep_chain")
        dd = sem("exponents_done")
        ed = sem("exps_done")
        prod = sem("products_done")
        csum = sem("coef_input_done")
        x1 = sem("x1_done")
        x1c = sem("x1_masked")
        gd = sem("decays_done")
        ymem = sem("y_cleared")
        keysC = [("v", t) for t in range(NT)] + [("k", p) for p in range(NPAIR)]
        Q = Banks(sem, "rwpre", psum, keysC)
        B = Banks(sem, "rw", psum, rwkv_keys())

        block = ctx.enter_context(nc.Block())

        @block.sync
        def _(sp):
            sp.dma_start(consts[:, :], ext["c_rwkv"]).then_inc(c_in, 16)
            sp.dma_start(w2[:, :], ext["w2"]).then_inc(w_in, 16)
            sp.dma_start(a2[:, :], ext["a2"]).then_inc(w_in, 16)

        @block.gpsimd
        def _(pool):
            for b in range(8):
                pool.sem_inc(Q.freed[b], 1)
                pool.sem_inc(B.freed[b], 1)
            pool.memset(Y[:, :, :], 0.0).then_inc(ymem, 1)
            pool.memset(reset[:, :], 1.0).then_inc(rst, 1)
            pool.wait_ge(rst, 1)
            pool.memset(reset[:, :].rearrange("p (c t) -> p c t", t=P)[:, :, 0:1], 0.0).then_inc(rst, 1)
            for p in range(NPAIR):
                pool.wait_ge(kraw, p + 1)
                pool.tensor_tensor(tmp[:, :] if p % 2 else D1[:, :], KK[:, p, :], KK[:, p, :], ALU.mult).then_inc(ksq, 1)
                if p + 2 < NPAIR:
                    pool.wait_ge(Q.fill_sem(("k", p)), Q.count(0, ("k", p)))
            pool.wait_ge(w_in, 32)
            pool.wait_ge(c_in, 16)
            for t in range(NT):
                pool.wait_ge(Q.free_sem(("v", t)), Q.after(0, ("v", t)))
            with pool.Fori(0, NPAIR) as it:
                for h in range(2):
                    key = ("Y", NCK - 1, h)
                    pool.wait_ge(B.free_sem(key), B.after(it, key) - B.per[B.at[key][0]])
                pool.tensor_copy(w2s[:, :], w2[:, ds(P * it, P)]).then_inc(parts, 1)
                pool.tensor_copy(a2s[:, :], a2[:, ds(P * it, P)]).then_inc(parts, 1)
                pool.tensor_copy(VS[:, :, :], VN[:, :, ds(P * it, P)]).then_inc(parts, 1)
                for g in range(4):
                    z, h = divmod(g, 2)
                    for c in range(NCK):
                        key = ("X", z, c, h)
                        pool.wait_ge(B.free_sem(key), B.after(it, key))
                    pool.tensor_tensor(X[g][:, :, :], SC[g][:, :, 0:P],
                                       lvmask[0].unsqueeze(1).to_broadcast([P, NCK, P]), ALU.mult).then_inc(x1c, 1)
                    pool.wait_ge(x1c, 4 * it + g + 1)
                    pool.tensor_tensor(X[g][:, :, :], X[g][:, :, :],
                                       ident[:, :].unsqueeze(1).to_broadcast([P, NCK, P]), ALU.add).then_inc(x1, 1)

        @block.tensor
        def _(pe):
            for t in range(NT):
                for p in range(NPAIR):
                    ins = pe.transpose(Q.tile(("v", t))[:, P * p:P * p + P], PT[:, V0 + p, P * t:P * t + P], ident[:, :])
                ins.then_inc(Q.fill_sem(("v", t)), 1)
            pe.wait_ge(c_in, 16)
            for p in range(NPAIR):
                pe.wait_ge(ksq, p + 1)
                pe.matmul(Q.tile(("k", p))[:, :], headsum, (tmp if p % 2 else D1)[:, :], start=True, stop=True)\
                  .then_inc(Q.fill_sem(("k", p)), 1)
            for k in keysC:
                pe.wait_ge(Q.free_sem(k), Q.after(0, k))
            pe.wait_ge(lora_act, 1)

            with pe.Fori(0, NPAIR) as it:
                def bank(key):
                    pe.wait_ge(B.free_sem(key), B.before(it, key))
                    return B.tile(key)

                def copied(key):
                    pe.wait_ge(B.free_sem(key), B.after(it, key))

                def done(ins, key):
                    ins.then_inc(B.fill_sem(key), 1)

                pe.wait_ge(parts, 3 * it + 3)
                for z in range(2):
                    zz = slice(HD * z, HD * z + HD)
                    done(pe.matmul(bank(("L", "w", z))[:, :], w2s[zz, :], PT[zz, DW, :], start=True, stop=True), ("L", "w", z))
                    done(pe.matmul(bank(("L", "a", z))[:, :], a2s[zz, :], PT[zz, DA, :], start=True, stop=True), ("L", "a", z))
                for z in range(2):
                    pe.wait_ge(prod, 4 * (2 * it + z) + 4)
                    for a in range(3):
                        dst = bank(("N", z, a))
                        for c in range(NCK):
                            src = (QR[z][:, c, 0:P], KD[z][:, P * c:P * c + P], AD[z][:, P * c:P * c + P])[a]
                            ins = pe.transpose(dst[:, P * c:P * c + P], src, ident[:, :])
                        done(ins, ("N", z, a))
                for z in range(2):
                    for c in range(NCK):
                        for h in range(2):
                            half = slice(HD * h, HD * h + HD)
                            dst = bank(("X", z, c, h))
                            pe.matmul(dst[:, 0:256], AD[z][half, P * c:P * c + P], QR[z][half, c, :], start=True, stop=True)
                            done(pe.matmul(dst[:, 256:512], KD[z][half, P * c:P * c + P], QR[z][half, c, :],
                                           start=True, stop=True), ("X", z, c, h))
                pe.wait_ge(csum, it + 1)
                dst = bank(("K",))
                for c in range(NCK):
                    ins = pe.matmul(dst[:, 2 * c:2 * c + 2], tmp[:, P * c:P * c + P], headone, start=True, stop=True)
                done(ins, ("K",))

                def turn(lv):
                    for g in range(4):
                        if lv == 1:
                            pe.wait_ge(x1, 4 * it + g + 1)
                        else:
                            copied(("Z", lv, g))
                        dst = bank(("T", lv, g))
                        for c in range(NCK):
                            ins = pe.transpose(dst[:, P * c:P * c + P], X[g][:, c, :], ident[:, :])
                        done(ins, ("T", lv, g))

                turn(1)
                for lv in range(2, NLEV + 1):
                    for g in range(4):
                        copied(("T", lv - 1, g))
                        dst = bank(("W", lv, g))
                        for c in range(NCK):
                            ins = pe.matmul(dst[:, P * c:P * c + P], SC[g][:, c, 0:P], XT[g][:, c, :], start=True, stop=True)
                        done(ins, ("W", lv, g))
                    for g in range(4):
                        copied(("W", lv, g))
                        dst = bank(("Z", lv, g))
                        for c in range(NCK):
                            ins = pe.matmul(dst[:, P * c:P * c + P], W1[g][:, c, :], X[g][:, c, :], start=True, stop=True)
                        done(ins, ("Z", lv, g))
                    if lv < NLEV:
                        turn(lv)
                for g in range(4):
                    dst = bank(("U", g))
                    h = g % 2
                    for c in range(NCK):
                        ins = pe.matmul(dst[:, HD * c:HD * c + HD], SC[g][:, c, 256:384], VS[:, c, HD * h:HD * h + HD],
                                        start=True, stop=True)
                    done(ins, ("U", g))
                for z in range(2):
                    copied(("N", z, 0))
                    dst = bank(("V", z))
                    for h in range(2):
                        copied(("Z", NLEV, 2 * z + h))
                        for c in range(NCK):
                            ins = pe.matmul(dst[HD * h:HD * h + HD, P * c:P * c + P], nat[z][0][:, c, HD * h:HD * h + HD],
                                            X[2 * z + h][:, c, :], start=True, stop=True)
                    done(ins, ("V", z))
                for g in range(4):
                    copied(("U", g))
                for z in range(2):
                    copied(("V", z))
                    copied(("N", z, 1))
                    copied(("N", z, 2))
                for n in range(NCK):
                    ck = (n, NCK - 1 - n)
                    for h in range(2):
                        half = slice(HD * h, HD * h + HD)
                        if n:
                            copied(("S", n - 1, h))
                        dst = bank(("A", n, h))
                        for z in range(2):
                            out = dst[:, HD * z:HD * z + HD]
                            ins = pe.matmul(out, X[2 * z + h][:, ck[z], :], U0[2 * z + h][:, ck[z], :], start=True, stop=(n == 0))
                            if n:
                                ins = pe.matmul(out, WT[z][half, ck[z], :], S[z][half, n % 2, :], start=False, stop=True)
                        done(ins, ("A", n, h))
                    if n < NCK - 1:
                        for h in range(2):
                            half = slice(HD * h, HD * h + HD)
                            copied(("A", n, h))
                            dst = bank(("S", n, h))
                            for z in range(2):
                                out = dst[half, HD * z:HD * z + HD]
                                pe.matmul(out, nat[z][1][:, ck[z], half], VS[:, ck[z], half], start=True, stop=False)
                                if n:
                                    pe.matmul(out, ident[half, half], S[z][half, n % 2, :], start=False, stop=False)
                                ins = pe.matmul(out, nat[z][2][:, ck[z], half], SA[:, h, z, :], start=False, stop=True)
                            done(ins, ("S", n, h))
                    for h in range(2):
                        half = slice(HD * h, HD * h + HD)
                        copied(("A", n, h))
                        dst = bank(("Y", n, h))
                        for z in range(2):
                            g = 2 * z + h
                            out = dst[:, HD * z:HD * z + HD]
                            if n:
                                pe.matmul(out, QR[z][half, ck[z], P:2 * P], S[z][half, n % 2, :], start=True, stop=False)
                            pe.matmul(out, SC[g][:, ck[z], 384:512], VS[:, ck[z], half], start=(n == 0), stop=False)
                            ins = pe.matmul(out, SC[g][:, ck[z], 128:256], SA[:, h, z, :], start=False, stop=True)
                        done(ins, ("Y", n, h))

        @block.scalar
        def _(act):
            act.activation(PT[:, DW, :], PT[:, DW, :], ACT.Tanh).then_inc(lora_act, 1)
            for p in range(NPAIR):
                act.activation(KK[:, p, :], PT[:, K0 + p, :], ACT.Identity,
                               scale=vec[:, rows["k_k"][0] + p:rows["k_k"][0] + p + 1]).then_inc(kraw, 1)
            for t in range(NT):
                key = ("v", t)
                act.wait_ge(Q.fill_sem(key), Q.count(0, key))
                act.activation(VN[:, t, :], Q.tile(key)[:, :], ACT.Copy).then_inc(Q.free_sem(key), 1)
            for p in range(NPAIR):
                key = ("k", p)
                act.wait_ge(Q.fill_sem(key), Q.count(0, key))
                if p >= 2:
                    act.wait_ge(kkok, p - 1)
                act.activation(sg[:, p % 2, :], Q.tile(key)[:, :], ACT.Sqrt).then_inc(Q.free_sem(key), 1)
            act.wait_ge(kkok, NPAIR)

            with act.Fori(0, NPAIR) as it:
                def take(dst, key, src=None):
                    act.wait_ge(B.fill_sem(key), B.count(it, key))
                    act.activation(dst, B.tile(key)[:, :] if src is None else src, ACT.Copy).then_inc(B.free_sem(key), 1)

                for z in range(2):
                    for what, dst, row in (("w", sg, "w0"), ("a", aa, "a0")):
                        key = ("L", what, z)
                        act.wait_ge(B.fill_sem(key), B.count(it, key))
                        act.activation(dst[:, z, :], B.tile(key)[:, :], ACT.Sigmoid,
                                       bias=vec[:, ds(rows[row][0] + 4 * z + it, 1)]).then_inc(B.free_sem(key), 1)
                for z in range(2):
                    act.wait_ge(dd, 3 * (2 * it + z) + 3)
                    act.activation(E3[:, :], D1[:, :], ACT.Exp, scale=KAPPA).then_inc(ed, 1)
                    act.activation(D2[:, :], D2[:, :], ACT.Exp, scale=-KAPPA).then_inc(ed, 1)
                    act.activation(D1[:, :], D1[:, :], ACT.Exp, scale=-KAPPA).then_inc(ed, 1)
                    act.activation(G[:, z, z:z + 3], mid[:, z, NCK + z:NCK + z + 3], ACT.Exp, scale=-KAPPA).then_inc(gd, 1)
                    for a in range(3):
                        key = ("N", z, a)
                        act.wait_ge(B.fill_sem(key), B.count(it, key))
                        act.activation(nat[z][a][:, :, :].rearrange("p c t -> p (c t)"), B.tile(key)[:, :], ACT.Copy,
                                       scale=-1.0 if a == 2 else 1.0).then_inc(B.free_sem(key), 1)
                take(coef[:, :, ds(2 * it, 2)], ("K",), B.tile(("K",))[:, 0:8].rearrange("p (t h) -> p t h", h=2))
                for lv in range(1, NLEV):
                    for g in range(4):
                        take(XT[g][:, :, :].rearrange("p c t -> p (c t)"), ("T", lv, g))
                for g in range(4):
                    take(U0[g], ("U", g), B.tile(("U", g))[:, 0:256].rearrange("p (c v) -> p c v", v=HD))
                for z in range(2):
                    take(WT[z][:, :, :].rearrange("p c t -> p (c t)"), ("V", z))
                for n in range(NCK):
                    for h in range(2):
                        key = ("A", n, h)
                        take(SA[:, h, :, :].rearrange("p z v -> p (z v)"), key, B.tile(key)[:, 0:P])
                    if n < NCK - 1:
                        for h in range(2):
                            key = ("S", n, h)
                            half = slice(HD * h, HD * h + HD)
                            act.wait_ge(B.fill_sem(key), B.count(it, key))
                            act.activation(S[0][half, (n + 1) % 2, :], B.tile(key)[half, 0:HD], ACT.Identity, scale=G[half, 0, n:n + 1])
                            act.activation(S[1][half, (n + 1) % 2, :], B.tile(key)[half, HD:P], ACT.Identity,
                                           scale=G[half, 1, NCK - 1 - n:NCK - n]).then_inc(B.free_sem(key), 1)

        @block.vector
        def _(dve):
            ch = Chain(dve, kch)
            for p in range(NPAIR):
                key = ("k", p)
                root = sg[:, p % 2, :]
                dve.wait_ge(Q.free_sem(key), Q.after(0, key))
                ch(dve.tensor_scalar(root, root, 1e-12, None, ALU.max))
                ch(dve.reciprocal(root, root))
                dve.tensor_tensor(KK[:, p, :], KK[:, p, :], root, ALU.mult).then_inc(kkok, 1)
            dve.wait_ge(kkok, NPAIR)
            dve.wait_ge(rst, 2)
            dve.wait_ge(c_in, 16)
            dve.wait_ge(ymem, 1)

            with dve.Fori(0, NPAIR) as it:
                ch = Chain(dve, pch, it, PREP)
                q4 = lambda ap: ap.rearrange("p (c t) -> p c t", t=P)
                kk = flat2(KK[:, ds(it, 1), :])
                rr = flat2(PT[:, ds(R0 + it, 1), :])
                kp = flat2(PT[:, ds(K0 + it, 1), :])
                for z in range(2):
                    s = sg[:, z, :]
                    dve.wait_ge(B.free_sem(("L", "w", z)), B.after(it, ("L", "w", z)))
                    dve.wait_ge(B.free_sem(("L", "a", z)), B.after(it, ("L", "a", z)))
                    ch(dve.tensor_tensor_scan(Ps[:, :], reset[:, :], s, 0.0, ALU.mult, ALU.add))
                    m = q4(Ps[:, :])[:, :, HD - 1:HD]
                    mb = m.to_broadcast([P, NCK, P])
                    M, Rm = mid[:, z, 0:NCK], mid[:, z, NCK:2 * NCK]
                    ch(dve.tensor_copy(M, m.rearrange("p c a -> p (c a)")))
                    ch(dve.tensor_tensor(Rm, q4(Ps[:, :])[:, :, P - 1:P].rearrange("p c a -> p (c a)"), M, ALU.subtract))
                    if z == 0:
                        ch(dve.tensor_tensor(Rm[:, 0:3], Rm[:, 0:3], M[:, 1:4], ALU.add))
                    else:
                        ch(dve.tensor_tensor(M[:, 1:4], M[:, 1:4], Rm[:, 0:3], ALU.add))
                        ch(dve.tensor_copy(Rm[:, 1:4], M[:, 1:4]))
                    if z == 0:
                        ch(dve.tensor_tensor(q4(D1[:, :]), q4(Ps[:, :]), mb, ALU.subtract))
                        dve.tensor_tensor(D2[:, :], D1[:, :], s, ALU.subtract).then_inc(dd, 3)
                    else:
                        ch(dve.tensor_tensor(q4(D2[:, :]), mb, q4(Ps[:, :]), ALU.subtract))
                        dve.tensor_tensor(D1[:, :], D2[:, :], s, ALU.add).then_inc(dd, 3)
                    a = aa[:, z, :]
                    ch(dve.tensor_scalar(Ps[:, :], a, 1.0, vec[:, ds(rows["k_a"][0] + it, 1)], ALU.subtract, ALU.mult))
                    dst = kds if z == 0 else Ps
                    ch(dve.scalar_tensor_tensor(out=dst[:, :], in0=Ps[:, :], scalar=1.0, in1=kp, op0=ALU.add, op1=ALU.mult))
                    ch(dve.tensor_tensor(a, a, kk, ALU.mult))
                    dve.wait_ge(ed, 3 * (2 * it + z) + 3)
                    q = q4(D2[:, :])
                    dve.tensor_tensor(QR[z][:, :, 0:P], q4(kk), q, ALU.mult).then_inc(prod, 1)
                    dve.tensor_tensor(QR[z][:, :, P:2 * P], q4(rr), q4(D1[:, :]), ALU.mult).then_inc(prod, 1)
                    dve.tensor_tensor(KD[z][:, :], dst[:, :], E3[:, :], ALU.mult).then_inc(prod, 1)
                    dve.tensor_tensor(AD[z][:, :], a, E3[:, :], ALU.mult).then_inc(prod, 1)
                    dve.wait_ge(prod, 4 * (2 * it + z) + 4)
                ch(dve.tensor_tensor(kds[:, :], kds[:, :], Ps[:, :], ALU.add))
                dve.scalar_tensor_tensor(out=tmp[:, :], in0=rr, scalar=vec[:, ds(rows["r_k"][0] + it, 1)], in1=kds[:, :],
                                         op0=ALU.mult, op1=ALU.mult).then_inc(csum, 1)
                assert ch.n <= PREP, ch.n
                for z in range(2):
                    for c in range(NCK):
                        for h in range(2):
                            key = ("X", z, c, h)
                            dve.wait_ge(B.fill_sem(key), B.count(it, key))
                            dve.tensor_tensor(SC[2 * z + h][:, c, :], B.tile(key)[:, :], scmask[z], ALU.mult)\
                               .then_inc(B.free_sem(key), 1)
                for lv in range(2, NLEV + 1):
                    for g in range(4):
                        key = ("W", lv, g)
                        dve.wait_ge(B.fill_sem(key), B.count(it, key))
                        dve.tensor_tensor(W1[g][:, :, :], q4(B.tile(key)[:, :]),
                                          lvmask[lv - 1].unsqueeze(1).to_broadcast([P, NCK, P]), ALU.mult)\
                           .then_inc(B.free_sem(key), 1)
                    for g in range(4):
                        key = ("Z", lv, g)
                        dve.wait_ge(B.fill_sem(key), B.count(it, key))
                        dve.tensor_tensor(X[g][:, :, :], X[g][:, :, :], q4(B.tile(key)[:, :]), ALU.add)\
                           .then_inc(B.free_sem(key), 1)
                for n in range(NCK):
                    for h in range(2):
                        key = ("Y", n, h)
                        if n:
                            dve.wait_ge(B.free_sem(("Y", n - 1, h)), B.after(it, ("Y", n - 1, h)))
                        dve.wait_ge(B.fill_sem(key), B.count(it, key))
                        for z in range(2):
                            dst = flat2(Y[:, (n, NCK - 1 - n)[z]:(n, NCK - 1 - n)[z] + 1, ds(P * it + HD * h, HD)])
                            ins = dve.tensor_tensor(dst, dst, B.tile(key)[:, HD * z:HD * z + HD], ALU.add)
                        ins.then_inc(B.free_sem(key), 1)
                assert ch.n == PREP, ch.n


def mixed_output(nc, psum, ext, keep):
    rows, nrows = vec_rows()
    with ExitStack() as ctx:
        sb = lambda name, shape, dt=F32: ctx.enter_context(nc.sbuf_tensor("mix_" + name, shape, dt))
        sem = phase_semaphores(nc, ctx, "mix")
        x, ident, vec, att, Y, VN, coef = (keep[k] for k in ("x", "ident", "vec", "att", "rk", "VN", "coef"))
        dg = keep["PTb"][:, 14, :]
        g2 = sb("g2", [P, C])
        lnw = sb("ln_w", [P, C])
        lnb = sb("ln_b", [P, C])
        cat_hi = sb("cat_hi", [P, KD, T], F32R)
        cat_lo = sb("cat_lo", [P, KD, T], F32R)
        sq = sb("squares", [P, NT, C])
        bonus = sb("bonus", [P, NT, C])
        st = sb("gn_sum", [P, NT, NH])
        vr = sb("gn_var", [P, NT, NH])
        ss = sb("att_sumsq", [P, NT])
        NS = 4
        raw = sb("wo_raw", [P, NS, D])
        w_hi = sb("wo_hi", [P, NS, D], F32R)
        w_lo = sb("wo_lo", [P, NS, D], F32R)
        g2_in = sem("g2_in")
        ln_in = sem("ln_in")
        raw_in = [sem(f"wo_in{s}") for s in range(NS)]
        hi_w = [sem(f"wo_hi_done{s}") for s in range(NS)]
        lo_w = [sem(f"wo_lo_done{s}") for s in range(NS)]
        used = [sem(f"wo_used{s}") for s in range(NS)]
        gate = sem("gate_done")
        asum = sem("att_sums_done")
        aroot = sem("att_roots_done")
        an = sem("att_norm_done")
        avar = sem("att_var_done")
        chn = sem("gn_chain")
        cent = sem("centred")
        sqd = sem("squared")
        vrd = sem("var_done")
        root = sem("gn_root")
        bon = sem("bonus_done")
        rkd = sem("rk_done")
        hi_c = sem("cat_hi_done")
        Gk = Banks(sem, "gate", psum, [("g", t) for t in range(NT)] + [("c", k) for k in range(KD)]
                   + [("o", t, n) for t in range(NT) for n in range(2)])
        wo = ext["w_o"].rearrange("(k p) n -> p k n", p=P)

        block = ctx.enter_context(nc.Block())

        @block.sync
        def _(sp):
            sp.dma_start(g2[:, :], ext["g2"]).then_inc(g2_in, 16)
            for dst, name in ((lnw, "ln_w"), (lnb, "ln_b")):
                sp.dma_start(dst[:, :], ext[name].partition_broadcast(P)).then_inc(ln_in, 16)
            for k in range(KD):
                if k >= NS:
                    sp.wait_ge(lo_w[k % NS], k // NS)
                sp.dma_start(raw[:, k % NS, :], wo[:, k, :]).then_inc(raw_in[k % NS], 16)

        @block.gpsimd
        def _(pool):
            for b in range(8):
                pool.sem_inc(Gk.freed[b], 1)
            for t in range(NT):
                h3 = lambda ap: ap.rearrange("p (h v) -> p h v", h=NH)
                pool.tensor_tensor(h3(bonus[:, t, :]), h3(VN[:, t, :]),
                                   coef[:, t, :].unsqueeze(2).to_broadcast([P, NH, HD]), ALU.mult).then_inc(bon, 1)

        @block.tensor
        def _(pe):
            pe.wait_ge(gate, 1)
            pe.wait_ge(g2_in, 16)
            for t in range(NT):
                key = ("g", t)
                pe.wait_ge(Gk.free_sem(key), Gk.before(0, key))
                pe.matmul(Gk.tile(key)[:, :], dg[:, P * t:P * t + P], g2[:, :], start=True, stop=True)\
                  .then_inc(Gk.fill_sem(key), 1)
            for k in range(KD):
                key = ("c", k)
                pe.wait_ge(Gk.free_sem(key), Gk.before(0, key))
                for t in range(NT):
                    if k < 4:
                        if k == 0:
                            pe.wait_ge(an, t + 1)
                        dst = Gk.tile(key).rearrange("p (r j c) -> p j r c", j=NT, c=QC)[:, t, :, :]
                        ins = pe.transpose(dst, att[:, t, P * k:P * k + P], ident[:, :])
                    else:
                        if k == 4:
                            pe.wait_ge(rkd, t + 1)
                        ins = pe.transpose(Gk.tile(key)[:, P * t:P * t + P], Y[:, t, P * (k - 4):P * (k - 4) + P], ident[:, :])
                ins.then_inc(Gk.fill_sem(key), 1)
            for k in range(KD):
                s = k % NS
                pe.wait_ge(Gk.free_sem(("c", k)), Gk.after(0, ("c", k)))
                pe.wait_ge(lo_w[s], k // NS + 1)
                for t in range(NT):
                    for n in range(2):
                        key = ("o", t, n)
                        if k == 0:
                            pe.wait_ge(Gk.free_sem(key), Gk.before(0, key))
                        out = Gk.tile(key)[:, :]
                        col = slice(512 * n, 512 * n + 512)
                        tok = slice(P * t, P * t + P)
                        pe.matmul(out, cat_hi[:, k, tok], w_hi[:, s, col], start=(k == 0), stop=False)
                        pe.matmul(out, cat_lo[:, k, tok], w_hi[:, s, col], start=False, stop=False)
                        ins = pe.matmul(out, cat_hi[:, k, tok], w_lo[:, s, col], start=False, stop=(k == KD - 1))
                        if k == KD - 1:
                            ins.then_inc(Gk.fill_sem(key), 1)
                if k < KD - 1:
                    ins.then_inc(used[s], 1)

        @block.scalar
        def _(act):
            act.activation(dg, dg, ACT.Sigmoid).then_inc(gate, 1)
            for t in range(NT):
                act.activation(sq[:, t, :], att[:, t, :], ACT.Square, accum_out=ss[:, t:t + 1]).then_inc(asum, 1)
            act.wait_ge(avar, 1)
            act.activation(ss[:, :], ss[:, :], ACT.Sqrt).then_inc(aroot, 1)

            def split_w(k):
                s = k % NS
                act.wait_ge(raw_in[s], 16 * (k // NS) + 16)
                if k >= NS:
                    act.wait_ge(used[s], k // NS)
                act.activation(w_hi[:, s, :], raw[:, s, :], ACT.Copy).then_inc(hi_w[s], 1)

            for k in range(NS):
                split_w(k)
            for t in range(NT):
                act.wait_ge(cent, t + 1)
                act.activation(sq[:, t, :], Y[:, t, :], ACT.Square).then_inc(sqd, 1)
            for t in range(NT):
                act.wait_ge(vrd, t + 1)
                act.activation(vr[:, t, :], vr[:, t, :], ACT.Sqrt).then_inc(root, 1)
            for k in range(KD):
                key = ("c", k)
                act.wait_ge(Gk.fill_sem(key), Gk.count(0, key))
                scale = vec[:, rows["attn_norm_w"][0] + k:rows["attn_norm_w"][0] + k + 1] if k < 4 else 1.0
                act.activation(cat_hi[:, k, :], Gk.tile(key)[:, :], ACT.Identity, scale=scale).then_inc(hi_c, 1)
            for k in range(NS, KD):
                split_w(k)

        @block.vector
        def _(dve):
            ch = Chain(dve, chn)
            h3 = lambda ap: ap.rearrange("p (h v) -> p h v", h=NH)
            wide = lambda ap: ap.unsqueeze(2).to_broadcast([P, NH, HD])
            dve.wait_ge(asum, NT)
            dve.tensor_scalar(ss[:, :], ss[:, :], 1.0 / C, RMS_EPS, ALU.mult, ALU.add).then_inc(avar, 1)
            for t in range(NT):
                ch(dve.tensor_reduce(st[:, t, :], h3(Y[:, t, :]), AX.X, ALU.add))
                ch(dve.tensor_scalar(st[:, t, :], st[:, t, :], 1.0 / HD, None, ALU.mult))
                dve.tensor_tensor(h3(Y[:, t, :]), h3(Y[:, t, :]), wide(st[:, t, :]), ALU.subtract).then_inc(cent, 1)
            dve.wait_ge(aroot, 1)
            ch(dve.reciprocal(ss[:, :], ss[:, :]))
            for t in range(NT):
                dve.tensor_scalar(att[:, t, :], att[:, t, :], ss[:, t:t + 1], None, ALU.mult).then_inc(an, 1)
            for t in range(NT):
                dve.wait_ge(sqd, t + 1)
                ch(dve.tensor_reduce(vr[:, t, :], h3(sq[:, t, :]), AX.X, ALU.add))
                dve.tensor_scalar(vr[:, t, :], vr[:, t, :], 1.0 / HD, GN_EPS, ALU.mult, ALU.add).then_inc(vrd, 1)

            def split_w(k):
                s = k % NS
                dve.wait_ge(hi_w[s], k // NS + 1)
                dve.tensor_tensor(w_lo[:, s, :], raw[:, s, :], w_hi[:, s, :].bitcast(F32), ALU.subtract).then_inc(lo_w[s], 1)

            for k in range(NS):
                split_w(k)
            dve.wait_ge(ln_in, 32)
            for t in range(NT):
                y = Y[:, t, :]
                dve.wait_ge(root, t + 1)
                ch(dve.reciprocal(vr[:, t, :], vr[:, t, :]))
                ch(dve.tensor_tensor(h3(y), h3(y), wide(vr[:, t, :]), ALU.mult))
                ch(dve.tensor_tensor(y, y, lnw[:, :], ALU.mult))
                ch(dve.tensor_tensor(y, y, lnb[:, :], ALU.add))
                dve.wait_ge(bon, t + 1)
                ch(dve.tensor_tensor(y, y, bonus[:, t, :], ALU.add))
                key = ("g", t)
                dve.wait_ge(Gk.fill_sem(key), Gk.count(0, key))
                dve.tensor_tensor(y, y, Gk.tile(key)[:, :], ALU.mult).then_inc(Gk.free_sem(key), 1)
                dve.wait_ge(Gk.free_sem(key), Gk.after(0, key))
                dve.sem_inc(rkd, 1)
            for k in range(KD):
                key = ("c", k)
                dve.wait_ge(hi_c, k + 1)
                scale = vec[:, rows["attn_norm_w"][0] + k:rows["attn_norm_w"][0] + k + 1] if k < 4 else 1.0
                dve.scalar_tensor_tensor(out=cat_lo[:, k, :], in0=Gk.tile(key)[:, :], scalar=scale,
                                         in1=cat_hi[:, k, :].bitcast(F32), op0=ALU.mult, op1=ALU.subtract)\
                   .then_inc(Gk.free_sem(key), 1)
            for k in range(NS, KD):
                split_w(k)
            for t in range(NT):
                for n in range(2):
                    key = ("o", t, n)
                    dst = x[:, t, 512 * n:512 * n + 512]
                    dve.wait_ge(Gk.fill_sem(key), Gk.count(0, key))
                    dve.tensor_tensor(dst, dst, Gk.tile(key)[:, :], ALU.add).then_inc(Gk.free_sem(key), 1)


NOV = 15
FAR = 4096


def router(nc, psum, ext, keep, hn_dram):
    rows, nrows = vec_rows()
    with ExitStack() as ctx:
        sb = lambda name, shape, dt=F32: ctx.enter_context(nc.sbuf_tensor("route_" + name, shape, dt))
        sem = phase_semaphores(nc, ctx, "route")
        x, ident = keep["x"], keep["ident"]
        gates, posm, meta, over, biasb = (keep[k] for k in ("gates", "posm", "meta", "over", "biasb"))
        iota = keep["iota"]
        w2 = sb("norm2_bcast", [P, D])
        hn = sb("hn", [P, NT, D])
        hT = sb("hn_turned", [P, KD, T])
        rw = sb("router_w", [P, KD, E])
        rb = sb("router_b", [P, E])
        ss = sb("h_sumsq", [P, NT])
        lg = sb("logits", [P, NT, E])
        top = sb("top_values", [P, NT, 8])
        tix = sb("top_index", [P, NT, 8], U32)
        tif = sb("top_index_f", [P, NT, TOPK])
        neg = sb("neg_top", [P, NT])
        esum = sb("gate_sums", [P, NT])
        eq = sb("chosen", [P, NT, TOPK, E])
        msk = sb("mask", [P, NT, E])
        mskb = sb("mask_bf16", [P, NT, E], BF16)
        rank = sb("rank", [P, NT, E])
        rc = sb("router_consts", [P, TOPK * E + NT * E + NOV])
        rank512 = rc[:, 0:TOPK * E].rearrange("p (k e) -> p k e", k=TOPK)
        tbase = rc[:, TOPK * E:TOPK * E + NT * E].rearrange("p (t e) -> p t e", t=NT)
        oiota = rc[:, TOPK * E + NT * E:TOPK * E + NT * E + NOV]
        tri = sb("earlier_ones", [P, 2 * P], BF16)
        cnt = sb("counts", [P, E])
        nov = sb("overflows", [P, E])
        inc = sb("overflow_sums", [P, E])
        le = sb("overflow_le", [P, NOV, E])
        ov = sb("overflow_f", [P, 2, NOV])
        ovn = sb("overflow_n", [P, NOV])
        ones = sb("ones_row", [P, E])
        braw = sb("bias_raw", [96, 3 * F])
        c_in = sem("router_consts_in")
        b_in = sem("bias_in")
        hsum = sem("h_sums_done")
        hvar = sem("h_var_done")
        hroot = sem("h_root_done")
        chn = sem("router_chain")
        hnd = sem("hn_done")
        hno = sem("hn_out")
        topd = sem("top_done")
        gex = sem("gate_exp_done")
        mdone = sem("mask_done")
        bz = sem("bias_zeroed")
        bh = sem("bias_parts_cast")
        br = sem("bias_rests")
        B = Banks(sem, "route", psum, [("t", k) for k in range(KD)] + [("l", t) for t in range(NT)] + [("p",)])

        block = ctx.enter_context(nc.Block())

        @block.sync
        def _(sp):
            sp.dma_start(w2[:, :], ext["norm2_row"].partition_broadcast(P)).then_inc(c_in, 16)
            sp.dma_start(rw[:, :, :], ext["router_w"].rearrange("(k p) e -> p k e", p=P)).then_inc(c_in, 16)
            sp.dma_start(rb[:, :], ext["router_b"].partition_broadcast(P)).then_inc(c_in, 16)
            sp.dma_start(rc[:, :], ext["c_router"]).then_inc(c_in, 16)
            sp.dma_start(tri[:, :], ext["c_tri"].bitcast(BF16)).then_inc(c_in, 16)
            sp.dma_start(iota[:, :], ext["c_iota"].partition_broadcast(P)).then_inc(c_in, 16)
            for g in range(3):
                sp.dma_start(braw[E * g:E * g + E, 0:2 * F], ext["expert_b_up"]).then_inc(b_in, 16)
                sp.dma_start(braw[E * g:E * g + E, 2 * F:3 * F], ext["expert_b_down"]).then_inc(b_in, 16)
            sp.dma_start(keep["selb"][:, :, :], ext["c_selb"].bitcast(BF16).rearrange("p (e s) -> p e s", e=E)).then_inc(b_in, 16)
            sp.dma_start(keep["prow"][:, :], ext["c_prow"].bitcast(BF16)).then_inc(b_in, 16)
            hd = hn_dram.rearrange("(t p) d -> p t d", p=P)
            for t in range(NT):
                sp.wait_ge(hnd, t + 1)
                sp.dma_start(hd[:, t, :], hn[:, t, :]).then_inc(hno, 16)
            sp.wait_ge(hno, 16 * NT)
            sp.wait_ge(b_in, 16 * 8)

        @block.gpsimd
        def _(pool):
            for b in range(8):
                pool.sem_inc(B.freed[b], 1)
            pool.memset(biasb[:, :], 0.0).then_inc(bz, 1)
            pool.memset(ones[:, :], 1.0).then_inc(bz, 1)

        @block.scalar
        def _(act):
            for t in range(NT):
                act.activation(hn[:, t, :], x[:, t, :], ACT.Square, accum_out=ss[:, t:t + 1]).then_inc(hsum, 1)
            act.wait_ge(hvar, 1)
            act.activation(ss[:, :], ss[:, :], ACT.Sqrt).then_inc(hroot, 1)
            act.wait_ge(b_in, 16 * 8)
            act.wait_ge(bz, 2)
            for g in range(3):
                act.activation(biasb[E * g:E * g + E, :], braw[E * g:E * g + E, :], ACT.Copy).then_inc(bh, 1)
            for k in range(KD):
                key = ("t", k)
                act.wait_ge(B.fill_sem(key), B.count(0, key))
                act.activation(hT[:, k, :], B.tile(key)[:, :], ACT.Copy).then_inc(B.free_sem(key), 1)
            act.wait_ge(br, 2)
            for g in range(1, 3):
                act.activation(biasb[E * g:E * g + E, :], braw[E * g:E * g + E, :], ACT.Copy).then_inc(bh, 1)
            for t in range(NT):
                act.wait_ge(topd, t + 1)
                act.activation(gates[:, t, :], top[:, t, 0:TOPK], ACT.Exp, bias=neg[:, t:t + 1],
                               accum_out=esum[:, t:t + 1]).then_inc(gex, 1)
            act.wait_ge(br, 3)
            act.activation(biasb[2 * E:3 * E, :], braw[2 * E:3 * E, :], ACT.Copy).then_inc(bh, 1)

        @block.tensor
        def _(pe):
            for t in range(NT):
                pe.wait_ge(hnd, t + 1)
                for k in range(KD):
                    key = ("t", k)
                    if t == 0:
                        pe.wait_ge(B.free_sem(key), B.before(0, key))
                    ins = pe.transpose(B.tile(key)[:, P * t:P * t + P], hn[:, t, P * k:P * k + P], ident[:, :])
                    if t == NT - 1:
                        ins.then_inc(B.fill_sem(key), 1)
            pe.wait_ge(c_in, 16 * 6)
            for k in range(KD):
                pe.wait_ge(B.free_sem(("t", k)), B.after(0, ("t", k)))
            for t in range(NT):
                key = ("l", t)
                for k in range(KD):
                    ins = pe.matmul(B.tile(key)[:, 0:E], hT[:, k, P * t:P * t + P], rw[:, k, :], start=(k == 0), stop=(k == KD - 1))
                ins.then_inc(B.fill_sem(key), 1)
            pe.wait_ge(mdone, 1)
            dst = B.tile(("p",))
            for t in range(NT + 1):
                out = dst[:, E * t:E * t + E]
                parts = [(P, u) for u in range(t)] + ([(0, t)] if t < NT else [])
                for i, (c, u) in enumerate(parts):
                    ins = pe.matmul(out, tri[:, c:c + P], mskb[:, u, :], start=(i == 0), stop=(i == len(parts) - 1))
            ins.then_inc(B.fill_sem(("p",)), 1)

        @block.vector
        def _(dve):
            ch = Chain(dve, chn)
            dve.wait_ge(hsum, NT)
            dve.tensor_scalar(ss[:, :], ss[:, :], 1.0 / D, RMS_EPS, ALU.mult, ALU.add).then_inc(hvar, 1)
            dve.wait_ge(hroot, 1)
            ch(dve.reciprocal(ss[:, :], ss[:, :]))
            dve.wait_ge(c_in, 16 * 6)
            for t in range(NT):
                ch(dve.tensor_scalar(hn[:, t, :], x[:, t, :], ss[:, t:t + 1], None, ALU.mult))
                dve.tensor_tensor(hn[:, t, :], hn[:, t, :], w2[:, :], ALU.mult).then_inc(hnd, 1)
            for g in range(1, 3):
                dve.wait_ge(bh, 3)
                r = slice(E * g, E * g + E)
                dve.tensor_tensor(braw[r, :], braw[r, :], biasb[r, :], ALU.subtract).then_inc(br, 1)
            for t in range(NT):
                key = ("l", t)
                dve.wait_ge(B.fill_sem(key), B.count(0, key))
                dve.tensor_tensor(lg[:, t, :], B.tile(key)[:, 0:E], rb[:, :], ALU.add).then_inc(B.free_sem(key), 1)
                dve.wait_ge(B.free_sem(key), B.after(0, key))
                ch(dve.max(top[:, t, :], lg[:, t, :]))
                ch(dve.max_index(tix[:, t, :], top[:, t, :], lg[:, t, :]))
                dve.tensor_scalar(neg[:, t:t + 1], top[:, t, 0:1], -1.0, None, ALU.mult).then_inc(topd, 1)
            ch(dve.tensor_copy(tif[:, :, :], tix[:, :, 0:TOPK]))
            ch(dve.tensor_tensor(eq[:, :, :, :].rearrange("p t k e -> p (t k) e"),
                                 iota[:, 0:E].unsqueeze(1).to_broadcast([P, NT * TOPK, E]),
                                 tif[:, :, :].rearrange("p t k -> p (t k)").unsqueeze(2).to_broadcast([P, NT * TOPK, E]),
                                 ALU.is_equal))
            ch(dve.tensor_reduce(msk[:, :, :], eq[:, :, :, :].rearrange("p t k e -> p t e k"), AX.X, ALU.add))
            dve.tensor_copy(mskb[:, :, :], msk[:, :, :]).then_inc(mdone, 1)
            for t in range(NT):
                ch(dve.tensor_tensor(eq[:, t, :, :], eq[:, t, :, :], rank512, ALU.mult))
            ch(dve.tensor_reduce(rank[:, :, :], eq[:, :, :, :].rearrange("p t k e -> p t e k"), AX.X, ALU.add))
            ch(dve.tensor_copy(meta[:, :, :, 0], tbase))
            ch(dve.tensor_tensor(meta[:, :, :, 1], rank[:, :, :], tbase, ALU.add))
            dve.wait_ge(gex, NT)
            ch(dve.reciprocal(esum[:, :], esum[:, :]))
            ch(dve.tensor_tensor(gates[:, :, :], gates[:, :, :], esum[:, :].unsqueeze(2).to_broadcast([P, NT, TOPK]), ALU.mult))
            key = ("p",)
            pos = B.tile(key)[:, 0:NT * E].rearrange("p (t e) -> p t e", t=NT)
            dve.wait_ge(B.fill_sem(key), B.count(0, key))
            dve.wait_ge(mdone, 1)
            ch(dve.tensor_scalar(posm[:, :, :], pos, 1.0, None, ALU.add))
            ch(dve.tensor_tensor(posm[:, :, :], posm[:, :, :], msk[:, :, :], ALU.mult))
            ch(dve.tensor_scalar(posm[:, :, :], posm[:, :, :], -1.0, None, ALU.add))
            ch(dve.tensor_copy(cnt[:, :], B.tile(key)[:, NT * E:NT * E + E]))
            ch(dve.tensor_scalar(nov[:, :], cnt[:, :], float(P), None, ALU.is_gt))
            for m in (2, 3):
                ch(dve.tensor_scalar(inc[:, :], cnt[:, :], float(P * m), None, ALU.is_gt))
                ch(dve.tensor_tensor(nov[:, :], nov[:, :], inc[:, :], ALU.add))
            dve.wait_ge(bz, 2)
            ch(dve.tensor_tensor_scan(inc[:, :], ones[:, :], nov[:, :], 0.0, ALU.mult, ALU.add))
            ch(dve.tensor_tensor(le[:, :, :], inc[:, :].unsqueeze(1).to_broadcast([P, NOV, E]),
                                 oiota.unsqueeze(2).to_broadcast([P, NOV, E]), ALU.is_le))
            ch(dve.tensor_reduce(ov[:, 0, :], le[:, :, :], AX.X, ALU.add))
            ch(dve.tensor_tensor(le[:, :, :], le[:, :, :], nov[:, :].unsqueeze(1).to_broadcast([P, NOV, E]), ALU.mult))
            ch(dve.tensor_reduce(ovn[:, :], le[:, :, :], AX.X, ALU.add))
            ch(dve.tensor_scalar(ov[:, 0, :], ov[:, 0, :], float(E - 1), None, ALU.min))
            ch(dve.tensor_tensor(ov[:, 1, :], oiota, ovn[:, :], ALU.subtract))
            ch(dve.tensor_scalar(ov[:, 1, :], ov[:, 1, :], float(P), float(P), ALU.mult, ALU.add))
            ch(dve.tensor_scalar(ov[:, 1, :], ov[:, 1, :], float(3 * P), None, ALU.min))
            ch(dve.tensor_copy(over[:, 0:2 * NOV], ov[:, :, :].rearrange("p a i -> p (a i)")))
            ch(dve.tensor_copy(over[:, 2 * NOV:2 * NOV + 1], inc[:, E - 1:E]))
            dve.wait_ge(bh, 5)
            r = slice(2 * E, 3 * E)
            dve.tensor_tensor(braw[r, :], braw[r, :], biasb[r, :], ALU.subtract).then_inc(br, 1)


def expert_keys(par):
    return [(par, k) for k in ("U00", "U01", "M", "U10", "U11", "A0", "X0", "D0", "D1", "A1", "X1")]


def experts(nc, psum, ext, keep, hn_dram, c_dram):
    RAW, RING = 6, 4
    SLOTS = 12
    PAIRS = E // 2
    with ExitStack() as ctx:
        sb = lambda name, shape, dt=F32: ctx.enter_context(nc.sbuf_tensor("moe_" + name, shape, dt))
        sem = phase_semaphores(nc, ctx, "moe")
        ident = keep["ident"]
        posm, meta, over, biasb, selb, prow, iota = (keep[k] for k in ("posm", "meta", "over", "biasb", "selb", "prow", "iota"))
        raw = sb("w_raw", [P, RAW, 2 * D])
        w_hi = sb("w_hi", [P, RING, 2 * D], F32R)
        w_lo = sb("w_lo", [P, RING, 2 * D], F32R)
        xg = sb("x_gathered", [P, D])
        x_hi = sb("x_hi", [P, KD, P], F32R)
        x_lo = sb("x_lo", [P, KD, P], F32R)
        a_hi = sb("a_hi", [P, KD, P], F32R)
        a_lo = sb("a_lo", [P, KD, P], F32R)
        gm = sb("gate_part", [P, 2, 512])
        lm = sb("linear_part", [P, 2, 512])
        sg = sb("sigmoid_part", [P, 2, 512])
        an = sb("act_natural", [P, D])
        y = sb("y", [P, D])
        sel = sb("slot_of_token", [P, NT, P], BF16)
        idx = sb("row_index", [P, 2, 2], I32)

        raw_in = [sem(f"w_in{i}") for i in range(RAW)]
        hi_w = [sem(f"w_hi_done{i}") for i in range(RING)]
        lo_w = [sem(f"w_lo_done{i}") for i in range(RING)]
        used = [sem(f"w_used{i}") for i in range(RING)]
        seld = sem("sel_done")
        gathered = sem("gathered")
        scattered = sem("scattered")
        begun = sem("gathers_scatters_begun")
        rows_out = sem("rows_out")
        hi_x = sem("x_hi_done")
        hi_a = sem("a_hi_done")
        sigd = sem("sigmoid_done")
        lmd = sem("linear_done")
        glud = sem("glu_done")
        actd = sem("act_done")
        cleared = sem("x_cleared")
        main = Banks(sem, "moe", psum, expert_keys(0) + expert_keys(1))
        pro = Banks(sem, "moepro", psum[5:8], [(0, k) for k in ("M", "X0", "X1")])
        more = Banks(sem, "moeov", psum, [(0, k) for k in ("M", "X0", "X1", "U00", "U01", "U10", "U11", "A0", "D0", "D1", "A1")])
        up, down = ext["expert_w_up"], ext["expert_w_down"]
        nslot = lambda n, j: 3 * n + j // RING

        def load(sp, n, e, j):
            g = (j - RAW) // RING
            sp.wait_ge(lo_w[(j - RAW) % RING], 3 * n + g + 3)
            r = (j % RAW)
            for k2 in range(2):
                dst = raw[:, r, D * k2:D * k2 + D]
                rows = slice(256 * (j % 4) + P * k2, 256 * (j % 4) + P * k2 + P)
                if j < 8:
                    src = up[ds(e, 1), rows, :].rearrange("a p (g h c) -> p (a g) h c", g=2, h=2)
                    sp.dma_start(dst.rearrange("p (g c) -> p g c", g=2), src[:, :, j // 4, :]).then_inc(raw_in[r], 16)
                else:
                    sp.dma_start(dst, down[ds(e, 1), rows, :].rearrange("a p c -> p (a c)")).then_inc(raw_in[r], 16)

        def split_hi(act, n, j):
            act.wait_ge(raw_in[j % RAW], 32 * (2 * n + j // RAW) + 32)
            act.wait_ge(used[j % RING], nslot(n, j) + 1)
            act.activation(w_hi[:, j % RING, :], raw[:, j % RAW, :], ACT.Copy).then_inc(hi_w[j % RING], 1)

        def split_lo(eng, n, j):
            eng.wait_ge(hi_w[j % RING], nslot(n, j) + 1)
            eng.tensor_tensor(w_lo[:, j % RING, :], raw[:, j % RAW, :], w_hi[:, j % RING, :].bitcast(F32), ALU.subtract)\
               .then_inc(lo_w[j % RING], 1)

        def slot_matmuls(pe, n, j, B, it, keys, s_hi, s_lo, k0):
            pe.wait_ge(lo_w[j % RING], nslot(n, j) + 3)
            for k2 in range(2):
                k = k0 + k2
                for i, key in enumerate(keys):
                    first = k == 0
                    if first:
                        pe.wait_ge(B.free_sem(key), B.before(it, key))
                    out = B.tile(key)[:, :]
                    w = slice(1024 * k2 + 512 * i, 1024 * k2 + 512 * i + 512)
                    pe.matmul(out, s_hi[:, k, :], w_hi[:, j % RING, w], start=first, stop=False)
                    pe.matmul(out, s_lo[:, k, :], w_hi[:, j % RING, w], start=False, stop=False)
                    ins = pe.matmul(out, s_hi[:, k, :], w_lo[:, j % RING, w], start=False, stop=False)
            ins.then_inc(used[j % RING], 1)

        def add_bias(pe, e, B, key, col):
            pe.matmul(B.tile(key)[:, :], selb[:, ds(e, 1), :].rearrange("p a s -> p (a s)"), biasb[:, col:col + 512],
                      start=False, stop=True).then_inc(B.fill_sem(key), 1)

        def pe_meta(pe, n, e, B, it, key):
            pe.wait_ge(seld, n + 1)
            pe.wait_ge(B.free_sem(key), B.before(it, key))
            for t in range(NT):
                pe.matmul(B.tile(key)[:, 0:2], sel[:, t, :], prow[:, :], start=(t == 0), stop=False)
                ins = pe.matmul(B.tile(key)[:, 0:2], sel[:, t, :],
                                meta[:, t, ds(e, 1), :].rearrange("p a b -> p (a b)"), start=False, stop=(t == NT - 1))
            ins.then_inc(B.fill_sem(key), 1)

        def pe_turn(pe, B, it, key, src, half):
            pe.wait_ge(B.free_sem(key), B.before(it, key))
            for q in range(4):
                k = 4 * half + q
                ins = pe.transpose(B.tile(key)[:, P * q:P * q + P], src[:, P * k:P * k + P], ident[:, :])
            ins.then_inc(B.fill_sem(key), 1)

        def take_hi(act, B, it, key, dst, half, done):
            act.wait_ge(B.fill_sem(key), B.count(it, key))
            act.activation(dst[:, 4 * half:4 * half + 4, :].rearrange("p k s -> p (k s)"), B.tile(key)[:, :], ACT.Copy)\
               .then_inc(done, 1)

        def take_lo(dve, B, it, key, hi, lo, half, done, count):
            dve.wait_ge(done, count)
            part = lambda ap: ap[:, 4 * half:4 * half + 4, :].rearrange("p k s -> p (k s)")
            dve.tensor_tensor(part(lo), B.tile(key)[:, :], part(hi).bitcast(F32), ALU.subtract).then_inc(B.free_sem(key), 1)

        def dve_sel(dve, n, e, off):
            for t in range(NT):
                ins = dve.tensor_scalar(sel[:, t, :], iota[:, ds(off, P)], posm[:, t, ds(e, 1)], None, ALU.is_equal)
            ins.then_inc(seld, 1)

        def dve_index(dve, n, B, it, key, par):
            dve.wait_ge(B.fill_sem(key), B.count(it, key))
            dve.wait_ge(rows_out, n + (2 if B is more else 1))
            dve.tensor_scalar(idx[:, par, :], B.tile(key)[:, 0:2], float(FAR), None, ALU.add).then_inc(B.free_sem(key), 1)

        def pool_gather(pool, n, B, it, key, par):
            pool.wait_ge(B.free_sem(key), B.after(it, key))
            pool.sem_inc(begun, 1)
            pool.indirect_dma_start(out=xg[:, :], out_offset=None, in_=hn_dram,
                                    in_offset=bass.IndirectOffsetOnAxis(ap=idx[:, par, 0:1], axis=0),
                                    bounds_check=T - 1, oob_is_err=False).then_inc(gathered, 16)

        def pool_scatter(pool, n, B, it, par, ipar):
            for k in ("D0", "D1"):
                pool.wait_ge(B.free_sem((par, k)), B.after(it, (par, k)))
            pool.sem_inc(begun, 1)
            pool.indirect_dma_start(out=c_dram, out_offset=bass.IndirectOffsetOnAxis(ap=idx[:, ipar, 1:2], axis=0),
                                    in_=y[:, :], in_offset=None,
                                    bounds_check=TOPK * T - 1, oob_is_err=False).then_inc(scattered, 16)
            pool.wait_ge(scattered, 16 * n + 16)
            pool.sem_inc(rows_out, 1)

        def dve_swiglu(dve, n, B, it, par, hf, part):
            g, l = (par, f"U{hf}0"), (par, f"U{hf}1")
            if part == 0:
                dve.wait_ge(B.fill_sem(g), B.count(it, g))
                dve.tensor_scalar(gm[:, hf, :], B.tile(g)[:, :], 7.0, None, ALU.min).then_inc(B.free_sem(g), 1)
                dve.wait_ge(B.fill_sem(l), B.count(it, l))
                dve.tensor_scalar(lm[:, hf, :], B.tile(l)[:, :], 7.0, -7.0, ALU.min, ALU.max).then_inc(B.free_sem(l), 1)
            else:
                dve.wait_ge(B.free_sem(l), B.after(it, l))
                dve.scalar_tensor_tensor(out=lm[:, hf, :], in0=lm[:, hf, :], scalar=1.0, in1=gm[:, hf, :],
                                         op0=ALU.add, op1=ALU.mult).then_inc(glud, 1)
                dve.wait_ge(glud, 2 * n + hf + 1)
                dve.wait_ge(sigd, 2 * n + hf + 1)
                dve.tensor_tensor(an[:, 512 * hf:512 * hf + 512], lm[:, hf, :], sg[:, hf, :], ALU.mult).then_inc(actd, 1)

        def act_sigmoid(act, n, B, it, par, hf):
            g = (par, f"U{hf}0")
            act.wait_ge(B.free_sem(g), B.after(it, g))
            act.activation(sg[:, hf, :], gm[:, hf, :], ACT.Sigmoid, scale=1.702).then_inc(sigd, 1)

        POOL_LO = (5, 9)

        def pe_block(pe, n, e, B, it, par, nxt):
            for hf in range(2):
                keys = [(par, f"U{hf}0"), (par, f"U{hf}1")]
                for j in range(4 * hf, 4 * hf + 4):
                    slot_matmuls(pe, n, j, B, it, keys, x_hi, x_lo, 2 * (j % 4))
                for i, key in enumerate(keys):
                    add_bias(pe, e, B, key, F * i + 512 * hf)
                if hf == 0 and nxt:
                    pe_meta(pe, n + 1, e + 1, B, it, (par, "M"))
            pe.wait_ge(actd, 2 * n + 1)
            pe_turn(pe, B, it, (par, "A0"), an, 0)
            if nxt:
                pe.wait_ge(gathered, 16 * n + 32)
                pe_turn(pe, B, it, (par, "X0"), xg, 0)
            keys = [(par, "D0"), (par, "D1")]
            pe.wait_ge(B.free_sem((par, "A0")), B.after(it, (par, "A0")))
            for j in (8, 9):
                slot_matmuls(pe, n, j, B, it, keys, a_hi, a_lo, 2 * (j - 8))
            pe.wait_ge(actd, 2 * n + 2)
            pe_turn(pe, B, it, (par, "A1"), an, 1)
            if nxt:
                pe_turn(pe, B, it, (par, "X1"), xg, 1)
            pe.wait_ge(B.free_sem((par, "A1")), B.after(it, (par, "A1")))
            for j in (10, 11):
                slot_matmuls(pe, n, j, B, it, keys, a_hi, a_lo, 2 * (j - 8))
            for i, key in enumerate(keys):
                add_bias(pe, e, B, key, 2 * F + 512 * i)
            if nxt:
                for k in ("X0", "X1"):
                    pe.wait_ge(B.free_sem((par, k)), B.after(it, (par, k)))

        def act_block(act, n, B, it, par, nxt):
            for j in (3, 4, 5, 6):
                split_hi(act, n, j)
            act_sigmoid(act, n, B, it, par, 0)
            for j in (7, 8, 9, 10):
                split_hi(act, n, j)
            take_hi(act, B, it, (par, "A0"), a_hi, 0, hi_a)
            if nxt:
                take_hi(act, B, it, (par, "X0"), x_hi, 0, hi_x)
            act_sigmoid(act, n, B, it, par, 1)
            split_hi(act, n, 11)
            if nxt:
                split_hi(act, n + 1, 0)
            take_hi(act, B, it, (par, "A1"), a_hi, 1, hi_a)
            if nxt:
                take_hi(act, B, it, (par, "X1"), x_hi, 1, hi_x)
                split_hi(act, n + 1, 1)
                split_hi(act, n + 1, 2)
            act.wait_ge(rows_out, n + 2)
            for i in range(2):
                key = (par, f"D{i}")
                act.wait_ge(B.fill_sem(key), B.count(it, key))
                act.activation(y[:, 512 * i:512 * i + 512], B.tile(key)[:, :], ACT.Copy).then_inc(B.free_sem(key), 1)

        def dve_block(dve, n, e, B, it, par, nxt):
            lo = lambda m, *js: [split_lo(dve, m, j) for j in js if j not in POOL_LO]
            lo(n, 3, 4)
            if nxt:
                dve_sel(dve, n + 1, e + 1, 0)
            lo(n, 5, 6)
            dve_swiglu(dve, n, B, it, par, 0, 0)
            lo(n, 7)
            dve_swiglu(dve, n, B, it, par, 0, 1)
            if nxt:
                dve_index(dve, n + 1, B, it, (par, "M"), 1 - par)
            lo(n, 8, 9, 10)
            take_lo(dve, B, it, (par, "A0"), a_hi, a_lo, 0, hi_a, 2 * n + 1)
            if nxt:
                take_lo(dve, B, it, (par, "X0"), x_hi, x_lo, 0, hi_x, 2 * n + 3)
            dve_swiglu(dve, n, B, it, par, 1, 0)
            lo(n, 11)
            dve_swiglu(dve, n, B, it, par, 1, 1)
            if nxt:
                lo(n + 1, 0)
            take_lo(dve, B, it, (par, "A1"), a_hi, a_lo, 1, hi_a, 2 * n + 2)
            if nxt:
                take_lo(dve, B, it, (par, "X1"), x_hi, x_lo, 1, hi_x, 2 * n + 4)
                lo(n + 1, 1, 2)

        def pool_block(pool, n, B, it, par, ipar, nxt):
            split_lo(pool, n, 5)
            if nxt:
                pool_gather(pool, n + 1, B, it, (par, "M"), 1 - par)
            split_lo(pool, n, 9)
            pool_scatter(pool, n, B, it, par, ipar)

        def lead_in(eng, what, n, e, off, B, it, par=0):
            if what == "pe":
                pe_meta(eng, n, e, B, it, (0, "M"))
                eng.wait_ge(gathered, 16 * n + 16)
                for i in range(2):
                    pe_turn(eng, B, it, (0, f"X{i}"), xg, i)
                for i in range(2):
                    eng.wait_ge(B.free_sem((0, f"X{i}")), B.after(it, (0, f"X{i}")))
            if what == "act":
                for i in range(2):
                    take_hi(eng, B, it, (0, f"X{i}"), x_hi, i, hi_x)
                for j in range(3):
                    split_hi(eng, n, j)
            if what == "dve":
                dve_sel(eng, n, e, off)
                dve_index(eng, n, B, it, (0, "M"), 0)
                for i in range(2):
                    take_lo(eng, B, it, (0, f"X{i}"), x_hi, x_lo, i, hi_x, 2 * n + i + 1)
                for j in range(3):
                    split_lo(eng, n, j)
            if what == "pool":
                pool_gather(eng, n, B, it, (0, "M"), 0)

        block = ctx.enter_context(nc.Block())

        def program(eng, what):
            step = {"pe": lambda n, e, B, it, par, ipar, nxt: pe_block(eng, n, e, B, it, par, nxt),
                    "act": lambda n, e, B, it, par, ipar, nxt: act_block(eng, n, B, it, par, nxt),
                    "dve": lambda n, e, B, it, par, ipar, nxt: dve_block(eng, n, e, B, it, par, nxt),
                    "pool": lambda n, e, B, it, par, ipar, nxt: pool_block(eng, n, B, it, par, ipar, nxt)}[what]
            lead_in(eng, what, 0, 0, 0, pro, 0)
            with eng.Fori(0, PAIRS - 1) as i:
                for par in range(2):
                    step(2 * i + par, 2 * i + par, main, i, par, par, True)
            for par in range(2):
                step(E - 2 + par, E - 2 + par, main, PAIRS - 1, par, par, par == 0)
            total = eng.value_load(over[0:1, 2 * NOV:2 * NOV + 1], min_val=0, max_val=NOV)
            with eng.Fori(0, NOV) as i:
                with eng.If(total > i):
                    e = eng.value_load(over[0:1, ds(i, 1)], min_val=0, max_val=E - 1)
                    off = eng.value_load(over[0:1, ds(i + NOV, 1)], min_val=0, max_val=3 * P)
                    lead_in(eng, what, E + i, e, off, more, i)
                    step(E + i, e, more, i, 0, 0, False)

        @block.sync
        def _(sp):
            with sp.Fori(0, E) as n:
                for j in range(SLOTS):
                    load(sp, n, n, j)
            total = sp.value_load(over[0:1, 2 * NOV:2 * NOV + 1], min_val=0, max_val=NOV)
            with sp.Fori(0, NOV) as i:
                with sp.If(total > i):
                    e = sp.value_load(over[0:1, ds(i, 1)], min_val=0, max_val=E - 1)
                    for j in range(SLOTS):
                        load(sp, E + i, e, j)

        @block.gpsimd
        def _(pool):
            for r in range(RING):
                pool.sem_inc(lo_w[r], 2)
                pool.sem_inc(used[r], 1)
            for B in (main, pro, more):
                for f in B.freed:
                    pool.sem_inc(f, 1)
            pool.sem_inc(rows_out, 2)
            pool.memset(xg[:, :], 0.0).then_inc(cleared, 1)
            pool.wait_ge(cleared, 1)
            program(pool, "pool")

        @block.tensor
        def _(pe):
            program(pe, "pe")

        @block.scalar
        def _(act):
            program(act, "act")

        @block.vector
        def _(dve):
            program(dve, "dve")


def final_norm(nc, psum, ext, keep, c_dram, out):
    with ExitStack() as ctx:
        sb = lambda name, shape, dt=F32: ctx.enter_context(nc.sbuf_tensor("final_" + name, shape, dt))
        sem = phase_semaphores(nc, ctx, "final")
        x, gates = keep["x"], keep["gates"]
        c = sb("contributions", [P, NT, TOPK, D])
        w = sb("final_w", [P, D])
        sq = sb("final_squares", [P, D])
        ss = sb("final_sums", [P, NT])
        c_in = [sem(f"contributions_in{t}") for t in range(NT)]
        w_in = sem("final_w_in")
        acc = sem("sum_chain")
        sumd = sem("final_sum_done")
        ssd = sem("final_squares_done")
        var = sem("final_var_done")
        root = sem("final_root_done")
        rch = sem("final_chain")
        outd = sem("rows_done")
        stored = sem("out_stored")
        block = ctx.enter_context(nc.Block())

        @block.sync
        def _(sp):
            cd = c_dram.rearrange("(k t p) d -> p t k d", k=TOPK, p=P)
            for t in range(NT):
                sp.dma_start(c[:, t, :, :], cd[:, t, :, :]).then_inc(c_in[t], 16)
            sp.dma_start(w[:, :], ext["final_norm_w"].partition_broadcast(P)).then_inc(w_in, 16)
            od = out.rearrange("(t p) d -> p t d", p=P)
            for t in range(NT):
                sp.wait_ge(outd, t + 1)
                sp.dma_start(od[:, t, :], x[:, t, :]).then_inc(stored, 16)
            sp.wait_ge(stored, 16 * NT)

        @block.scalar
        def _(act):
            for t in range(NT):
                act.wait_ge(sumd, t + 1)
                if t:
                    act.wait_ge(ssd, t)
                act.activation(sq[:, :], x[:, t, :], ACT.Square, accum_out=ss[:, t:t + 1]).then_inc(ssd, 1)
                act.wait_ge(var, t + 1)
                act.activation(ss[:, t:t + 1], ss[:, t:t + 1], ACT.Sqrt).then_inc(root, 1)

        @block.vector
        def _(dve):
            ch = Chain(dve, acc)

            def total(t):
                dve.wait_ge(c_in[t], 16)
                for k in range(TOPK):
                    ins = dve.scalar_tensor_tensor(out=x[:, t, :], in0=c[:, t, k, :], scalar=gates[:, t, k:k + 1],
                                                   in1=x[:, t, :], op0=ALU.mult, op1=ALU.add)
                    if k < TOPK - 1:
                        ch(ins)
                ins.then_inc(sumd, 1)

            def scale(t):
                dve.wait_ge(ssd, t + 1)
                dve.tensor_scalar(ss[:, t:t + 1], ss[:, t:t + 1], 1.0 / D, RMS_EPS, ALU.mult, ALU.add).then_inc(var, 1)
                dve.wait_ge(root, t + 1)
                ch(dve.reciprocal(ss[:, t:t + 1], ss[:, t:t + 1]))
                dve.wait_ge(w_in, 16)
                dve.scalar_tensor_tensor(out=x[:, t, :], in0=x[:, t, :], scalar=ss[:, t:t + 1], in1=w[:, :],
                                         op0=ALU.mult, op1=ALU.mult).then_inc(outd, 1)

            total(0)
            for t in range(NT):
                if t + 1 < NT:
                    total(t + 1)
                scale(t)


def rwkv_constants():
    s, t = np.arange(P)[:, None], np.arange(P)[None, :]
    out = []
    for before, upto in ((s < t, s <= t), (s > t, s >= t)):
        out += [-1.0 * before, -1.0 * upto, 1.0 * before, 1.0 * upto]
    for lv in range(1, NLEV + 1):
        out.append(1.0 * ((s >> lv == t >> lv) & (s >> (lv - 1) != t >> (lv - 1))))
    out.append(1.0 * (s // HD == t // HD))
    out.append(1.0 * (s // HD == np.arange(2)[None, :]))
    return np.concatenate(out, axis=1).astype(np.float32)


def attention_mask():
    qc = QC * np.arange(NT)[:, None, None] + np.arange(QC)[None, :, None]
    kc = QC * np.arange(NT)[:, None, None] - PADC + np.arange(KC)[None, None, :]
    start = np.clip(qc - WIN // 2, 0, GRID - WIN)
    m = np.where((kc >= start) & (kc < start + WIN), 0.0, -1e30).astype(np.float32)
    return np.broadcast_to(m.transpose(1, 0, 2)[None], (ROWS, QC, NT, KC)).reshape(P, NT * KC)


def router_constants():
    row = lambda v, n: np.repeat(np.asarray(v, np.float32), n)
    rc = np.concatenate([row(T * np.arange(TOPK), E), row(P * np.arange(NT) - FAR, E), np.arange(NOV, dtype=np.float32)])
    p = np.arange(P)
    tri = np.concatenate([1.0 * (p[:, None] < p[None, :]), np.ones((P, P))], axis=1)
    selb = np.zeros((P, E, P))
    for part in range(3):
        selb[E * part + np.arange(E), np.arange(E), :] = 1.0
    b16 = lambda v: (v.astype(np.float32).view(np.uint32) >> 16).astype(np.uint16)
    return {"c_router": np.tile(rc[None], (P, 1)), "c_tri": b16(tri), "c_selb": b16(selb.reshape(P, E * P)),
            "c_prow": b16(np.tile(p[:, None], (1, 2))), "c_iota": np.arange(T, dtype=np.float32)}


def build(nc, ext, out):
    nrows = vec_rows()[1]
    with ExitStack() as ctx:
        sb = lambda name, shape, dt=F32, c=ctx: c.enter_context(nc.sbuf_tensor(name, shape, dt))
        psum = [ctx.enter_context(nc.psum_tensor(f"bank{i}", [P, 512], F32)) for i in range(8)]
        vpad = nc.dram_tensor("v_padded", [ROWS * PGRID, C], F32).ap()
        keep = {"x": sb("x", [P, NT, D]), "ident": sb("ident", [P, P]), "vec": sb("vec", [P, nrows])}
        with ExitStack() as mixer:
            keep["PTb"] = sb("proj_rwkv", [P, NTILE - N_ATT_TILES, T], c=mixer)
            keep["att"] = sb("att", [P, NT, C], c=mixer)
            keep["rk"] = sb("rk", [P, NT, C], c=mixer)
            keep["VN"] = sb("v_nat_rwkv", [P, NT, C], c=mixer)
            keep["coef"] = sb("bonus_coef", [P, NT, NH], c=mixer)
            with ExitStack() as first:
                keep["PTa"] = sb("proj_att", [P, N_ATT_TILES, T], c=first)
                in_projection(nc, psum, ext, keep)
                attention(nc, psum, ext, {**keep}, vpad)
            rwkv(nc, psum, ext, keep)
            mixed_output(nc, psum, ext, keep)
        hn_dram = nc.dram_tensor("hn_rows", [T, D], F32).ap()
        c_dram = nc.dram_tensor("contribution_rows", [TOPK * T, D], F32).ap()
        for name, shape, dt in (("gates", [P, NT, TOPK], F32), ("posm", [P, NT, E], F32), ("meta", [P, NT, E, 2], BF16),
                                ("over", [P, 2 * NOV + 1], I32), ("biasb", [P, 3 * F], BF16), ("iota", [P, T], F32),
                                ("selb", [P, E, P], BF16), ("prow", [P, 2], BF16)):
            keep[name] = sb(name, shape, dt)
        router(nc, psum, ext, keep, hn_dram)
        experts(nc, psum, ext, keep, hn_dram, c_dram)
        final_norm(nc, psum, ext, keep, c_dram, out)


def lay_out(a):
    lines = lambda v: np.ascontiguousarray(v).reshape(-1, P)
    ext = {n: a[n][0] for n in ("x", "w_in", "w_o", "router_w", "router_b", "expert_w_up", "expert_b_up",
                                "expert_w_down", "expert_b_down")}
    ext.update({n: lines(a[n]) for n in ("norm1_w", "norm2_w", "attn_norm_w")})
    ext.update({n: lines(a["rwkv_" + n]) for n in ("mu_prev", "mu_next", "w0", "a0", "k_k", "k_a", "r_k")})
    ext.update({n: a["rwkv_" + n].reshape(P, C) for n in ("w2", "a2", "g2")})
    ext.update({n: a["rwkv_" + n].reshape(C) for n in ("ln_w", "ln_b")})
    ext["norm2_row"] = a["norm2_w"].reshape(D)
    ext["final_norm_w"] = a["final_norm_w"]
    wide = np.pad(a["attn_rpb"][0], ((0, 0), (0, 0), (QC, QC)))
    ext["rpb"] = np.stack([wide[:, :, QC + WIN // 2 - 1 - c:][:, :, :KC] for c in range(QC)])
    ext["c_ident"] = np.eye(P, dtype=np.float32)
    ext["c_att_mask"] = attention_mask()
    ext["c_rwkv"] = rwkv_constants()
    ext.update(router_constants())
    return {n: np.ascontiguousarray(v) for n, v in ext.items()}


def kernel(**inputs):
    import concourse.bacc as bacc
    from concourse.bass_utils import run_bass_kernel_spmd

    nc = bacc.Bacc("TRN2", target_bir_lowering=False, num_devices=1)
    arrays, ext = {}, {}
    for name, a in lay_out({k: np.asarray(v) for k, v in inputs.items()}).items():
        arrays[f"in_{name}"] = a
        ext[name] = nc.dram_tensor(f"in_{name}", a.shape, mybir.dt.from_np(a.dtype), kind="ExternalInput").ap()
    out = nc.dram_tensor("out", (T, D), F32, kind="ExternalOutput").ap()
    build(nc, ext, out)
    r = run_bass_kernel_spmd(nc, [arrays], core_ids=[0])
    return r.results[0]["out"].reshape(1, T, D)
```

```python
from contextlib import ExitStack

import numpy as np

import concourse.bass as bass
from concourse import mybir

ALU = mybir.AluOpType
ACT = mybir.ActivationFunctionType
AX = mybir.AxisListType
F32 = mybir.dt.float32
F32R = mybir.dt.float32r
BF16 = mybir.dt.bfloat16
I32 = mybir.dt.int32
U32 = mybir.dt.uint32

P = 128
D = 1024
T = 512
NT = T // P
KD = D // P
HD = 64
NH = 8
C = NH * HD
NPAIR = NH // 2
GRID = 64
ROWS = T // GRID
WIN = 16
LORA_TILES = 3
NTILE = 6 * NPAIR + LORA_TILES
TQ, TK, TV, TR, TRK, TRV, TDW, TDA, TDG = 0, 4, 8, 12, 16, 20, 24, 25, 26
N_ATT_TILES = 12
E = 32
F = 1024
TOPK = 4
RMS_EPS = 1e-5
GN_EPS = 64e-5
KAPPA = float(np.exp(-0.5))
ds = bass.ds


class Banks:

    def __init__(self, sem, name, psum, keys, banks=None):
        n = len(psum)
        self.psum = psum
        self.per = [0] * n
        self.at = {}
        for i, k in enumerate(keys):
            b = banks[i] if banks else i % n
            self.at[k] = (b, self.per[b])
            self.per[b] += 1
        assert len(self.at) == len(keys)
        self.filled = [sem(f"{name}_filled{b}") for b in range(n)]
        self.freed = [sem(f"{name}_freed{b}") for b in range(n)]

    def tile(self, key):
        return self.psum[self.at[key][0]]

    def fill_sem(self, key):
        return self.filled[self.at[key][0]]

    def free_sem(self, key):
        return self.freed[self.at[key][0]]

    def count(self, it, key):
        b, o = self.at[key]
        return it * self.per[b] + (o + 1)

    def before(self, it, key):
        return self.count(it, key)

    def after(self, it, key):
        b, o = self.at[key]
        return it * self.per[b] + (o + 2)


def phase_semaphores(nc, ctx, phase):
    mine = []

    def finish():
        nc.clear_and_free_semaphores(mine)
        nc.all_engine_barrier(sem_only=True)

    ctx.callback(finish)

    def sem(name):
        mine.append(nc.alloc_semaphore(f"{phase}_{name}"))
        return mine[-1]

    return sem


def vec_rows():
    at, out = 0, {}
    for name, n in (("norm1_w", KD), ("norm2_w", KD), ("attn_norm_w", 4), ("mu_prev", 15), ("mu_next", 15),
                    ("w0", 8), ("a0", 8), ("k_k", 4), ("k_a", 4), ("r_k", 4)):
        out[name] = (at, n)
        at += n
    return out, at


def flat2(ap):
    return ap.rearrange("p a b -> p (a b)")


def in_projection(nc, psum, ext, keep):
    rows, nrows = vec_rows()
    with ExitStack() as ctx:
        sb = lambda name, shape, dt=F32: ctx.enter_context(nc.sbuf_tensor("proj_" + name, shape, dt))
        sem = phase_semaphores(nc, ctx, "proj")
        x, PTa, PTb, ident, vec = (keep[k] for k in ("x", "PTa", "PTb", "ident", "vec"))
        xn = sb("xn", [P, NT, D])
        x_hi = sb("x_hi", [P, KD, T], F32R)
        x_lo = sb("x_lo", [P, KD, T], F32R)
        ss = sb("ss", [P, NT])
        rs = sb("rs", [P, NT])
        vrow = sb("vrow", [nrows, P])
        keepw = sb("shift_keep", [P, NTILE])
        prevw = sb("shift_prev", [P, NTILE])
        nextw = sb("shift_next", [P, NTILE])
        NS = 4
        CW = 3 * P
        raw = sb("w_raw", [P, NS, 2 * CW])
        w_hi = sb("w_hi", [P, NS, 2 * CW], F32R)
        w_lo = sb("w_lo", [P, NS, 2 * CW], F32R)
        NCH = NTILE // 3
        OUTS = ((0, 2, PTa, 0), (2, 4, PTb, N_ATT_TILES))
        x_in = [sem(f"x_in{t}") for t in range(NT)]
        c_in = sem("consts_in")
        v_in = sem("vectors_in")
        sumsq = sem("sumsq_done")
        ms_done = sem("meansq_done")
        root = sem("root_done")
        rstd = sem("rstd_done")
        xn_done = sem("xn_done")
        turned = sem("x_turned")
        hi_x = sem("x_hi_done")
        lo_x = sem("x_lo_done")
        vt = sem("vectors_turned")
        vec_ok = sem("vec_done")
        shw = sem("shift_weights_done")
        raw_in = [sem(f"w_raw_in{s}") for s in range(NS)]
        hi_w = [sem(f"w_hi_done{s}") for s in range(NS)]
        lo_w = [sem(f"w_lo_done{s}") for s in range(NS)]
        used = [sem(f"w_used{s}") for s in range(NS)]
        kept = sem("own_part_done")
        prevd = sem("prev_part_done")
        nextd = sem("next_part_done")
        B = Banks(sem, "inproj", psum, [(h, j) for h in range(2) for j in range(3)])
        w_dram = ext["w_in"].rearrange("(k p) n -> p k n", p=P)

        block = ctx.enter_context(nc.Block())

        @block.sync
        def _(sp):
            for name, (r, n) in rows.items():
                sp.dma_start(vrow[r:r + n, :], ext[name]).then_inc(v_in, 16)
            sp.dma_start(ident[:, :], ext["c_ident"]).then_inc(c_in, 16)

            def load_chunk(c):
                for s in range(NS):
                    sp.wait_ge(lo_w[s], c + 1)
                    sp.dma_start(raw[:, s, :].rearrange("p (k n) -> p k n", k=2),
                                 w_dram[:, 2 * s:2 * s + 2, ds(CW * c, CW)]).then_inc(raw_in[s], 16)

            with sp.Fori(0, NCH) as c:
                load_chunk(c)

        @block.scalar
        def _(act):
            xd = ext["x"].rearrange("(t p) d -> p t d", p=P)
            for t in range(NT):
                act.dma_start(x[:, t, :], xd[:, t, :]).then_inc(x_in[t], 16)
            for t in range(NT):
                act.wait_ge(x_in[t], 16)
                act.activation(xn[:, t, :], x[:, t, :], ACT.Square, accum_out=ss[:, t:t + 1]).then_inc(sumsq, 1)
                act.wait_ge(ms_done, t + 1)
                act.activation(rs[:, t:t + 1], rs[:, t:t + 1], ACT.Sqrt).then_inc(root, 1)

            def split_w(c, s, it=None, h=None):
                act.wait_ge(raw_in[s], 16 * c + 16)
                if it is not None:
                    if s < NS - 1:
                        act.wait_ge(used[s], 2 * it + h + 1)
                    else:
                        act.wait_ge(B.fill_sem((h, 2)), B.count(it, (h, 2)))
                act.activation(w_hi[:, s, :], raw[:, s, :], ACT.Copy).then_inc(hi_w[s], 1)

            def own_part(it, h, j, PT, first):
                g = 6 * it + 3 * h + j
                key = (h, j)
                act.wait_ge(B.fill_sem(key), B.count(it, key))
                act.activation(flat2(PT[:, ds(g - first, 1), :]), B.tile(key)[:, :], ACT.Identity,
                               scale=keepw[:, ds(g, 1)]).then_inc(kept, 1)

            for s in range(NS):
                split_w(0, s)
            act.wait_ge(vec_ok, 1)
            for k in range(KD):
                act.wait_ge(turned, k + 1)
                act.activation(x_hi[:, k, :], psum[k][:, :], ACT.Identity,
                               scale=vec[:, rows["norm1_w"][0] + k:rows["norm1_w"][0] + k + 1]).then_inc(hi_x, 1)
            act.wait_ge(shw, 5)
            for i0, i1, PT, first in OUTS:
                with act.Fori(i0, i1) as it:
                    for h in range(2):
                        for s in range(NS):
                            split_w(2 * it + h + 1, s, it, h)
                        for j in range(3):
                            own_part(it, h, j, PT, first)
            for j in range(3):
                own_part(NCH // 2, 0, j, PT, first)

        @block.gpsimd
        def _(pool):
            for s in range(NS):
                pool.sem_inc(lo_w[s], 1)
            for b in range(len(psum)):
                pool.sem_inc(B.freed[b], 1)

        @block.vector
        def _(dve):
            for t in range(NT):
                dve.wait_ge(sumsq, t + 1)
                dve.tensor_scalar(rs[:, t:t + 1], ss[:, t:t + 1], 1.0 / D, RMS_EPS, ALU.mult, ALU.add).then_inc(ms_done, 1)
                dve.wait_ge(root, t + 1)
                dve.reciprocal(rs[:, t:t + 1], rs[:, t:t + 1]).then_inc(rstd, 1)
                dve.wait_ge(rstd, t + 1)
                dve.tensor_scalar(xn[:, t, :], x[:, t, :], rs[:, t:t + 1], None, ALU.mult).then_inc(xn_done, 1)
            dve.wait_ge(vt, 1)
            dve.tensor_copy(vec[:, :], psum[0][:, 0:nrows]).then_inc(vec_ok, 1)
            dve.wait_ge(vec_ok, 1)
            dve.memset(prevw[:, 0:N_ATT_TILES], 0.0)
            dve.memset(nextw[:, 0:N_ATT_TILES], 0.0)
            m0, m1 = rows["mu_prev"][0], rows["mu_next"][0]
            dve.tensor_copy(prevw[:, N_ATT_TILES:NTILE], vec[:, m0:m0 + 15]).then_inc(shw, 1)
            dve.tensor_copy(nextw[:, N_ATT_TILES:NTILE], vec[:, m1:m1 + 15]).then_inc(shw, 1)
            dve.wait_ge(shw, 2)
            dve.memset(keepw[:, 0:4], HD ** -0.5)
            dve.memset(keepw[:, 4:N_ATT_TILES], 1.0)
            dve.tensor_scalar(keepw[:, N_ATT_TILES:NTILE], prevw[:, N_ATT_TILES:NTILE], -1.0, 1.0,
                              ALU.mult, ALU.add).then_inc(shw, 1)
            dve.wait_ge(shw, 3)
            dve.tensor_tensor(keepw[:, N_ATT_TILES:NTILE], keepw[:, N_ATT_TILES:NTILE],
                              nextw[:, N_ATT_TILES:NTILE], ALU.subtract).then_inc(shw, 2)

            def split_w(c, s):
                dve.wait_ge(hi_w[s], c + 1)
                dve.tensor_tensor(w_lo[:, s, :], raw[:, s, :], w_hi[:, s, :].bitcast(F32), ALU.subtract).then_inc(lo_w[s], 1)

            def other_parts(it, h, j, PT, first):
                g = 6 * it + 3 * h + j
                key = (h, j)
                b = B.tile(key)
                dst = flat2(PT[:, ds(g - first, 1), :])
                dve.wait_ge(kept, g + 1)
                dve.scalar_tensor_tensor(out=dst[:, 1:T], in0=b[:, 0:T - 1], scalar=prevw[:, ds(g, 1)], in1=dst[:, 1:T],
                                         op0=ALU.mult, op1=ALU.add).then_inc(prevd, 1)
                dve.wait_ge(prevd, g + 1)
                dve.scalar_tensor_tensor(out=dst[:, 0:T - 1], in0=b[:, 1:T], scalar=nextw[:, ds(g, 1)],
                                         in1=dst[:, 0:T - 1], op0=ALU.mult, op1=ALU.add).then_inc(B.free_sem(key), 1)

            for s in range(NS):
                split_w(0, s)
            for k in range(KD):
                dve.wait_ge(hi_x, k + 1)
                ins = dve.scalar_tensor_tensor(out=x_lo[:, k, :], in0=psum[k][:, :],
                                               scalar=vec[:, rows["norm1_w"][0] + k:rows["norm1_w"][0] + k + 1],
                                               in1=x_hi[:, k, :].bitcast(F32), op0=ALU.mult, op1=ALU.subtract)
                ins.then_inc(lo_x, 1)
            for i0, i1, PT, first in OUTS:
                with dve.Fori(i0, i1) as it:
                    for h in range(2):
                        for s in range(NS):
                            split_w(2 * it + h + 1, s)
                        for j in range(3):
                            other_parts(it, h, j, PT, first)
            for j in range(3):
                other_parts(NCH // 2, 0, j, PT, first)

        @block.tensor
        def _(pe):
            pe.wait_ge(c_in, 16)
            pe.wait_ge(v_in, 16 * len(rows))
            pe.transpose(psum[0][:, 0:nrows], vrow[:, :], ident[0:nrows, 0:nrows]).then_inc(vt, 1)
            pe.wait_ge(vec_ok, 1)
            for t in range(NT):
                pe.wait_ge(xn_done, t + 1)
                for k in range(KD):
                    ins = pe.transpose(psum[k][:, P * t:P * t + P], xn[:, t, P * k:P * k + P], ident[:, :])
                    if t == NT - 1:
                        ins.then_inc(turned, 1)

            def chunk(it, h):
                c = 2 * it + h
                for s in range(NS):
                    pe.wait_ge(lo_w[s], c + 2)
                    for k2 in range(2):
                        k = 2 * s + k2
                        for j in range(3):
                            key = (h, j)
                            if k == 0:
                                pe.wait_ge(B.free_sem(key), B.before(it, key))
                            out = B.tile(key)[:, :]
                            w = slice(k2 * CW + j * P, k2 * CW + j * P + P)
                            pe.matmul(out, w_hi[:, s, w], x_hi[:, k, :], start=(k == 0), stop=False)
                            pe.matmul(out, w_hi[:, s, w], x_lo[:, k, :], start=False, stop=False)
                            ins = pe.matmul(out, w_lo[:, s, w], x_hi[:, k, :], start=False, stop=(k == KD - 1))
                            if k == KD - 1:
                                ins.then_inc(B.fill_sem(key), 1)
                    if s < NS - 1:
                        ins.then_inc(used[s], 1)

            pe.wait_ge(lo_x, KD)
            with pe.Fori(0, NCH // 2) as it:
                for h in range(2):
                    chunk(it, h)
            chunk(NCH // 2, 0)


PADC = 8
PGRID = GRID + 2 * PADC
QC = 16
KC = QC + WIN
RPBH = 15 * 31
RPB_PAD = 16


def attention(nc, psum, ext, keep, vpad):
    with ExitStack() as ctx:
        sb = lambda name, shape, dt=F32: ctx.enter_context(nc.sbuf_tensor("att_" + name, shape, dt))
        sem = phase_semaphores(nc, ctx, "att")
        PT, ident, att = keep["PTa"], keep["ident"], keep["att"]
        v_nat = sb("v_nat", [P, NT, C])
        zero = sb("zero", [P, C])
        kpad = sb("k_padded", [P, NPAIR, ROWS, PGRID])
        bias = sb("bias_table", [P, NH * ROWS, KC])
        mask = sb("mask_table", [P, NT, KC])
        tab = sb("bias_and_mask", [P, NH * ROWS, KC])
        vw = sb("v_windows", [P, NT, 2, C])
        qw = sb("q_window", [P, NPAIR, ROWS, QC])
        kw = sb("k_window", [P, NPAIR, ROWS, KC])
        sc = sb("scores", [P, 2, 2, ROWS * KC])
        pT = sb("probs_turned", [P, 2, 4, P])
        nmax = sb("neg_max", [P, NPAIR, 2])
        sums = sb("exp_sums", [P, NPAIR, 2])
        rec = sb("recip_sums", [P, NPAIR, 2])
        zeroed = sem("zeroed")
        bias_in = sem("bias_in")
        mask_in = sem("mask_in")
        v_out = sem("v_padded_out")
        pads_out = sem("pads_out")
        vw_in = sem("v_windows_in")
        kp_ok = sem("k_padded_done")
        win = sem("windows_done")
        tabd = sem("table_done")
        scd = sem("scores_biased")
        maxd = sem("max_done")
        expd = sem("exp_done")
        rcd = sem("recip_done")
        V = Banks(sem, "vturn", psum[:4], [(t,) for t in range(NT)])
        order = []
        for i in range(NPAIR + 2):
            order += [("S", i)] * (i < NPAIR) + [("T", i - 1)] * (1 <= i <= NPAIR) + [("O", i - 2)] * (i >= 2)
        A = Banks(sem, "att", psum, order)
        vp = vpad.rearrange("(r c) n -> r c n", c=PGRID)

        def heads(u):
            return 4 * (u // 2) + u % 2, 4 * (u // 2) + u % 2 + 2

        block = ctx.enter_context(nc.Block())

        @block.sync
        def _(sp):
            sp.dma_start(mask[:, :, :], ext["c_att_mask"].rearrange("p (t k) -> p t k", t=NT)).then_inc(mask_in, 16)
            for r in range(ROWS):
                sp.dma_start(bias[QC * r:QC * r + QC, :, :].rearrange("c (h k) x -> c h k x", h=NH),
                             ext["rpb"][:, :, ROWS - 1 - r:2 * ROWS - 1 - r, :]).then_inc(bias_in, 16)
            sp.wait_ge(zeroed, 1)
            sp.dma_start(vp[:, 0:PADC, :], zero[0:GRID, :]).then_inc(pads_out, 16)
            sp.dma_start(vp[:, PADC + GRID:PGRID, :], zero[0:GRID, :]).then_inc(pads_out, 16)
            for t in range(NT):
                sp.wait_ge(V.free_sem((t,)), V.after(0, (t,)))
                sp.dma_start(vp[2 * t:2 * t + 2, PADC:PADC + GRID, :], v_nat[:, t, :]).then_inc(v_out, 16)
            sp.wait_ge(v_out, 16 * NT)
            sp.wait_ge(pads_out, 32)
            for jt in range(NT):
                for hf in range(2):
                    sp.dma_start(vw[:, jt, hf, :], vp[4 * hf:4 * hf + 4, QC * jt:QC * jt + KC, :]).then_inc(vw_in, 16)

        @block.gpsimd
        def _(pool):
            for b in range(4):
                pool.sem_inc(V.freed[b], 1)
            for b in range(8):
                pool.sem_inc(A.freed[b], 1)
            pool.memset(zero[:, :], 0.0).then_inc(zeroed, 1)
            pool.memset(kpad[:, :, :, 0:PADC], 0.0)
            pool.memset(kpad[:, :, :, PADC + GRID:PGRID], 0.0)
            for p in range(NPAIR):
                pool.tensor_copy(kpad[:, p, :, PADC:PADC + GRID],
                                 PT[:, TK + p, :].rearrange("p (r c) -> p r c", c=GRID)).then_inc(kp_ok, 1)
            pool.wait_ge(kp_ok, NPAIR)
            pool.wait_ge(mask_in, 16)
            pool.wait_ge(bias_in, 16 * ROWS)
            with pool.Fori(0, NT) as jt:
                for p in range(NPAIR):
                    for u in (p // 2 * 2, p // 2 * 2 + 1):
                        pool.wait_ge(A.free_sem(("S", u)), A.before(jt, ("S", u)))
                    pool.tensor_copy(qw[:, p, :, :], PT[:, TQ + p, :].rearrange("p (r c) -> p r c", c=GRID)
                                     [:, :, ds(QC * jt, QC)])
                    pool.tensor_copy(kw[:, p, :, :], kpad[:, p, :, ds(QC * jt, KC)]).then_inc(win, 1)
                    rows = slice(2 * ROWS * p, 2 * ROWS * p + 2 * ROWS)
                    pool.tensor_tensor(tab[:, rows, :], bias[:, rows, :],
                                       mask[:, ds(jt, 1), :].to_broadcast([P, 2 * ROWS, KC]), ALU.add).then_inc(tabd, 1)

        @block.tensor
        def _(pe):
            for t in range(NT):
                for p in range(NPAIR):
                    ins = pe.transpose(V.tile((t,))[:, P * p:P * p + P], PT[:, TV + p, P * t:P * t + P], ident[:, :])
                ins.then_inc(V.fill_sem((t,)), 1)
            for t in range(NT):
                pe.wait_ge(V.free_sem((t,)), V.after(0, (t,)))

            def scores(jt, u):
                key = ("S", u)
                pe.wait_ge(win, 4 * jt + u // 2 * 2 + 2)
                pe.wait_ge(A.free_sem(key), A.before(jt, key))
                half = slice(HD * (u % 2), HD * (u % 2) + HD)
                for n in range(2):
                    pair = u // 2 * 2 + n
                    ins = pe.matmul(A.tile(key)[:, 256 * n:256 * n + 256],
                                    qw[half, pair, :, :].rearrange("p r c -> p (r c)"),
                                    kw[half, pair, :, :].rearrange("p r c -> p (r c)"), start=True, stop=True)
                ins.then_inc(A.fill_sem(key), 1)

            def turn(jt, p):
                key = ("T", p)
                pe.wait_ge(expd, 8 * jt + 2 * p + 2)
                pe.wait_ge(A.free_sem(key), A.before(jt, key))
                for h in range(2):
                    for hf in range(2):
                        q = 2 * h + hf
                        ins = pe.transpose(A.tile(key)[:, P * q:P * q + P], sc[:, p % 2, h, P * hf:P * hf + P], ident[:, :])
                ins.then_inc(A.fill_sem(key), 1)

            def values(jt, p):
                key = ("O", p)
                pe.wait_ge(A.free_sem(("T", p)), A.after(jt, ("T", p)))
                pe.wait_ge(A.free_sem(key), A.before(jt, key))
                for h in range(2):
                    for hf in range(2):
                        v = vw[:, ds(jt, 1), hf, HD * heads(p)[h]:HD * heads(p)[h] + HD].rearrange("p a b -> p (a b)")
                        ins = pe.matmul(A.tile(key)[:, HD * h:HD * h + HD], pT[:, p % 2, 2 * h + hf, :], v,
                                        start=(hf == 0), stop=(hf == 1))
                ins.then_inc(A.fill_sem(key), 1)

            pe.wait_ge(vw_in, 16 * 2 * NT)
            with pe.Fori(0, NT) as jt:
                for i in range(NPAIR + 2):
                    if i < NPAIR:
                        scores(jt, i)
                    if 1 <= i <= NPAIR:
                        turn(jt, i - 1)
                    if i >= 2:
                        values(jt, i - 2)

        @block.scalar
        def _(act):
            for t in range(NT):
                act.wait_ge(V.fill_sem((t,)), 1)
                act.activation(v_nat[:, t, :], V.tile((t,))[:, :], ACT.Copy).then_inc(V.free_sem((t,)), 1)

            def exps(jt, p):
                act.wait_ge(maxd, 4 * jt + p + 1)
                for h in range(2):
                    act.activation(sc[:, p % 2, h, :], sc[:, p % 2, h, :], ACT.Exp, bias=nmax[:, p, h:h + 1],
                                   accum_out=sums[:, p, h:h + 1]).then_inc(expd, 1)

            def probs(jt, p):
                key = ("T", p)
                act.wait_ge(A.fill_sem(key), A.count(jt, key))
                act.activation(pT[:, p % 2, :, :].rearrange("p a b -> p (a b)"), A.tile(key)[:, :], ACT.Copy)\
                   .then_inc(A.free_sem(key), 1)

            with act.Fori(0, NT) as jt:
                for i in range(NPAIR + 1):
                    if i < NPAIR:
                        exps(jt, i)
                    if i >= 1:
                        probs(jt, i - 1)

        @block.vector
        def _(dve):
            def biased(jt, p):
                key = ("S", p)
                dve.wait_ge(A.fill_sem(key), A.count(jt, key))
                dve.wait_ge(tabd, 4 * jt + p // 2 * 2 + 2)
                both = tab[:, :, :].rearrange("p (h r) k -> p h (r k)", h=NH)[:, heads(p)[0]:heads(p)[1] + 1:2, :]
                dve.tensor_tensor(sc[:, p % 2, :, :], A.tile(key).rearrange("p (h k) -> p h k", h=2), both,
                                  ALU.add).then_inc(A.free_sem(key), 1)
                dve.wait_ge(A.free_sem(key), A.after(jt, key))
                dve.tensor_reduce(nmax[:, p, :], sc[:, p % 2, :, :], AX.X, ALU.max, negate=True).then_inc(maxd, 1)

            def out(jt, p):
                key = ("O", p)
                dve.wait_ge(expd, 8 * jt + 2 * p + 2)
                dve.reciprocal(rec[:, p, :], sums[:, p, :]).then_inc(rcd, 1)
                dve.wait_ge(rcd, 4 * jt + p + 1)
                dve.wait_ge(A.fill_sem(key), A.count(jt, key))
                dst = att[:, ds(jt, 1), :].rearrange("p a (h d) -> p (a h) d", h=NH)[:, heads(p)[0]:heads(p)[1] + 1:2, :]
                dve.tensor_tensor(dst, A.tile(key)[:, 0:P].rearrange("p (h d) -> p h d", h=2),
                                  rec[:, p, :].unsqueeze(2).to_broadcast([P, 2, HD]), ALU.mult)\
                   .then_inc(A.free_sem(key), 1)

            with dve.Fori(0, NT) as jt:
                for i in range(NPAIR + 2):
                    if i < NPAIR:
                        biased(jt, i)
                    if i >= 2:
                        out(jt, i - 2)


class Chain:

    def __init__(self, eng, sem, it=0, per=0):
        self.eng, self.sem, self.base, self.n = eng, sem, it * per, 0

    def __call__(self, ins):
        self.n += 1
        ins.then_inc(self.sem, 1)
        self.eng.wait_ge(self.sem, self.base + self.n)


NLEV = 7
NCK = NT


def rwkv_keys():
    keys = [("X", z, c, h) for z in range(2) for c in range(NCK) for h in range(2)]
    keys += [("N", z, a) for z in range(2) for a in range(3)]
    keys += [("K",)]
    keys += [("T", 1, g) for g in range(4)]
    keys += [("L", what, z) for z in range(2) for what in "wa"]
    for lv in range(2, NLEV + 1):
        for s in "WZT" if lv < NLEV else "WZ":
            keys += [(s, lv, g) for g in range(4)]
    keys += [("U", g) for g in range(4)] + [("V", z) for z in range(2)]
    for n in range(NCK):
        keys += [("A", n, h) for h in range(2)]
        keys += [("S", n, h) for h in range(2)] if n < NCK - 1 else []
        keys += [("Y", n, h) for h in range(2)]
    return keys


def rwkv(nc, psum, ext, keep):
    rows, nrows = vec_rows()
    with ExitStack() as ctx:
        sb = lambda name, shape, dt=F32: ctx.enter_context(nc.sbuf_tensor("rwkv_" + name, shape, dt))
        sem = phase_semaphores(nc, ctx, "rwkv")
        PT, ident, vec, Y = keep["PTb"], keep["ident"], keep["vec"], keep["rk"]
        R0, K0, V0, DW, DA, DG = 0, 4, 8, 12, 13, 14
        VN, coef = keep["VN"], keep["coef"]
        KK = sb("kk", [P, NPAIR, T])
        w2 = sb("w2", [P, C])
        a2 = sb("a2", [P, C])
        consts = sb("rw_consts", [P, 2 * 512 + NLEV * P + P + 2])
        scmask = [consts[:, 512 * z:512 * z + 512] for z in range(2)]
        lvmask = [consts[:, 1024 + P * i:1024 + P * i + P] for i in range(NLEV)]
        headsum = consts[:, 1024 + NLEV * P:1024 + NLEV * P + P]
        headone = consts[:, 1024 + NLEV * P + P:1024 + NLEV * P + P + 2]
        reset = sb("scan_reset", [P, T])
        w2s = sb("w2_part", [P, P])
        a2s = sb("a2_part", [P, P])
        VS = sb("v_part", [P, NT, P])
        sg = sb("decay_sig", [P, 2, T])
        aa = sb("a_gate", [P, 2, T])
        Ps = sb("decay_sums", [P, T])
        D1 = sb("d_incl", [P, T])
        D2 = sb("d_excl", [P, T])
        E3 = sb("e_neg", [P, T])
        kds = sb("k_dirs", [P, T])
        tmp = sb("rw_tmp", [P, T])
        mid = sb("mids", [P, 2, 2 * NCK])
        G = sb("chunk_decay", [P, 2, NCK])
        Gn = sb("chunk_decay_next", [P, 2, NCK])
        RQ = [sb(f"rq{z}", [P, NCK, P]) for z in range(2)]
        QR = [sb(f"qr{z}", [P, NCK, 2 * P]) for z in range(2)]
        KD = [sb(f"kd{z}", [P, T]) for z in range(2)]
        AD = [sb(f"ad{z}", [P, T]) for z in range(2)]
        nat = [[sb(f"nat{z}{a}", [P, NCK, P]) for a in range(3)] for z in range(2)]
        SC = [sb(f"sc{g}", [P, NCK, 512]) for g in range(4)]
        X = [sb(f"x{g}", [P, NCK, P]) for g in range(4)]
        XT = [sb(f"xt{g}", [P, NCK, P]) for g in range(4)]
        W1 = [sb(f"w1{g}", [P, NCK, P]) for g in range(4)]
        WT = XT[0:2]
        U0 = [W1[g][:, :, 0:HD] for g in range(4)]
        SA = sb("sa", [P, 2, 2, HD])
        S = [sb(f"state{z}", [P, 2, HD]) for z in range(2)]
        PREP = 18

        c_in = sem("rw_consts_in")
        w_in = sem("lora_in")
        lora_act = sem("lora_activated")
        rst = sem("reset_done")
        kraw = sem("kk_scaled")
        ksq = sem("kk_squared")
        kroot = sem("kk_root")
        kch = sem("kk_chain")
        kkok = sem("kk_done")
        parts = sem("parts_done")
        sgd = sem("sigmoids_done")
        pch = sem("prep_chain")
        dd = sem("exponents_done")
        ed = sem("exps_done")
        prod = sem("products_done")
        csum = sem("coef_input_done")
        x1 = sem("x1_done")
        x1c = sem("x1_masked")
        gd = sem("decays_done")
        gcd = sem("decays_copied")
        rqd = sem("rq_copied")
        vsd = sem("v_part_copied")
        ymem = sem("y_cleared")
        keysC = [("v", t) for t in range(NT)] + [("k", p) for p in range(NPAIR)]
        Q = Banks(sem, "rwpre", psum, keysC + [("L", what, z) for z in range(2) for what in "wa"])
        B = Banks(sem, "rw", psum, rwkv_keys())

        block = ctx.enter_context(nc.Block())

        @block.sync
        def _(sp):
            sp.dma_start(consts[:, :], ext["c_rwkv"]).then_inc(c_in, 16)
            sp.dma_start(w2[:, :], ext["w2"]).then_inc(w_in, 16)
            sp.dma_start(a2[:, :], ext["a2"]).then_inc(w_in, 16)

        @block.gpsimd
        def _(pool):
            for b in range(8):
                pool.sem_inc(Q.freed[b], 1)
                pool.sem_inc(B.freed[b], 1)
            pool.memset(Y[:, :, :], 0.0).then_inc(ymem, 1)
            pool.memset(reset[:, :], 1.0).then_inc(rst, 1)
            pool.wait_ge(rst, 1)
            pool.memset(reset[:, :].rearrange("p (c t) -> p c t", t=P)[:, :, 0:1], 0.0).then_inc(rst, 1)
            for p in range(NPAIR):
                pool.wait_ge(kraw, p + 1)
                pool.tensor_tensor(tmp[:, :] if p % 2 else D1[:, :], KK[:, p, :], KK[:, p, :], ALU.mult).then_inc(ksq, 1)
                if p + 2 < NPAIR:
                    pool.wait_ge(Q.fill_sem(("k", p)), Q.count(0, ("k", p)))
            pool.wait_ge(w_in, 32)
            pool.wait_ge(c_in, 16)
            for t in range(NT):
                pool.wait_ge(Q.free_sem(("v", t)), Q.after(0, ("v", t)))
            def lora_parts(m):
                pool.tensor_copy(w2s[:, :], w2[:, ds(P * m, P)]).then_inc(parts, 1)
                pool.tensor_copy(a2s[:, :], a2[:, ds(P * m, P)]).then_inc(parts, 1)

            def trip(it, nxt):
                for h in range(2):
                    key = ("Y", NCK - 1, h)
                    pool.wait_ge(B.free_sem(key), B.after(it, key) - B.per[B.at[key][0]])
                pool.wait_ge(prod, 8 * it + 8)
                pool.tensor_copy(VS[:, :, :], VN[:, :, ds(P * it, P)]).then_inc(vsd, 1)
                if nxt:
                    lora_parts(it + 1)
                for g in range(4):
                    z, h = divmod(g, 2)
                    for c in range(NCK):
                        key = ("X", z, c, h)
                        pool.wait_ge(B.free_sem(key), B.after(it, key))
                    pool.tensor_tensor(X[g][:, :, :], SC[g][:, :, 0:P],
                                       lvmask[0].unsqueeze(1).to_broadcast([P, NCK, P]), ALU.mult).then_inc(x1c, 1)
                    pool.wait_ge(x1c, 4 * it + g + 1)
                    pool.tensor_tensor(X[g][:, :, :], X[g][:, :, :],
                                       ident[:, :].unsqueeze(1).to_broadcast([P, NCK, P]), ALU.add).then_inc(x1, 1)

            lora_parts(0)
            with pool.Fori(0, NPAIR - 1) as it:
                trip(it, True)
            trip(NPAIR - 1, False)

        @block.tensor
        def _(pe):
            for t in range(NT):
                for p in range(NPAIR):
                    ins = pe.transpose(Q.tile(("v", t))[:, P * p:P * p + P], PT[:, V0 + p, P * t:P * t + P], ident[:, :])
                ins.then_inc(Q.fill_sem(("v", t)), 1)
            pe.wait_ge(c_in, 16)
            for p in range(NPAIR):
                pe.wait_ge(ksq, p + 1)
                pe.matmul(Q.tile(("k", p))[:, :], headsum, (tmp if p % 2 else D1)[:, :], start=True, stop=True)\
                  .then_inc(Q.fill_sem(("k", p)), 1)
            for k in keysC:
                pe.wait_ge(Q.free_sem(k), Q.after(0, k))
            pe.wait_ge(lora_act, 1)

            def lora(Bk, i, m):
                pe.wait_ge(parts, 2 * m + 2)
                for z in range(2):
                    zz = slice(HD * z, HD * z + HD)
                    for what, w, src in (("w", w2s, DW), ("a", a2s, DA)):
                        key = ("L", what, z)
                        pe.wait_ge(Bk.free_sem(key), Bk.before(i, key))
                        pe.matmul(Bk.tile(key)[:, :], w[zz, :], PT[zz, src, :], start=True, stop=True).then_inc(Bk.fill_sem(key), 1)

            def trip(it, nxt):
                def bank(key):
                    pe.wait_ge(B.free_sem(key), B.before(it, key))
                    return B.tile(key)

                def copied(key):
                    pe.wait_ge(B.free_sem(key), B.after(it, key))

                def done(ins, key):
                    ins.then_inc(B.fill_sem(key), 1)

                for z in range(2):
                    pe.wait_ge(prod, 4 * (2 * it + z) + 4)
                    for c in range(NCK):
                        for h in range(2):
                            half = slice(HD * h, HD * h + HD)
                            dst = bank(("X", z, c, h))
                            pe.matmul(dst[:, 0:256], AD[z][half, P * c:P * c + P], QR[z][half, c, :], start=True, stop=True)
                            done(pe.matmul(dst[:, 256:512], KD[z][half, P * c:P * c + P], QR[z][half, c, :],
                                           start=True, stop=True), ("X", z, c, h))
                for z in range(2):
                    for a in range(3):
                        dst = bank(("N", z, a))
                        for c in range(NCK):
                            src = (QR[z][:, c, 0:P], KD[z][:, P * c:P * c + P], AD[z][:, P * c:P * c + P])[a]
                            ins = pe.transpose(dst[:, P * c:P * c + P], src, ident[:, :])
                        done(ins, ("N", z, a))
                pe.wait_ge(csum, it + 1)
                dst = bank(("K",))
                for c in range(NCK):
                    ins = pe.matmul(dst[:, 2 * c:2 * c + 2], tmp[:, P * c:P * c + P], headone, start=True, stop=True)
                done(ins, ("K",))

                def turn(lv):
                    for g in range(4):
                        if lv == 1:
                            pe.wait_ge(x1, 4 * it + g + 1)
                        else:
                            copied(("Z", lv, g))
                        dst = bank(("T", lv, g))
                        for c in range(NCK):
                            ins = pe.transpose(dst[:, P * c:P * c + P], X[g][:, c, :], ident[:, :])
                        done(ins, ("T", lv, g))

                turn(1)
                if nxt:
                    lora(B, it, it + 1)
                else:
                    for z in range(2):
                        for what in "wa":
                            key = ("L", what, z)
                            bank(key)
                            pe.sem_inc(B.fill_sem(key), 1)
                            pe.sem_inc(B.free_sem(key), 1)
                for lv in range(2, NLEV + 1):
                    for g in range(4):
                        copied(("T", lv - 1, g))
                        dst = bank(("W", lv, g))
                        for c in range(NCK):
                            ins = pe.matmul(dst[:, P * c:P * c + P], SC[g][:, c, 0:P], XT[g][:, c, :], start=True, stop=True)
                        done(ins, ("W", lv, g))
                    for g in range(4):
                        copied(("W", lv, g))
                        dst = bank(("Z", lv, g))
                        for c in range(NCK):
                            ins = pe.matmul(dst[:, P * c:P * c + P], W1[g][:, c, :], X[g][:, c, :], start=True, stop=True)
                        done(ins, ("Z", lv, g))
                    if lv < NLEV:
                        turn(lv)
                pe.wait_ge(vsd, it + 1)
                for g in range(4):
                    dst = bank(("U", g))
                    h = g % 2
                    for c in range(NCK):
                        ins = pe.matmul(dst[:, HD * c:HD * c + HD], SC[g][:, c, 256:384], VS[:, c, HD * h:HD * h + HD],
                                        start=True, stop=True)
                    done(ins, ("U", g))
                for z in range(2):
                    copied(("N", z, 0))
                    dst = bank(("V", z))
                    for h in range(2):
                        copied(("Z", NLEV, 2 * z + h))
                        for c in range(NCK):
                            ins = pe.matmul(dst[HD * h:HD * h + HD, P * c:P * c + P], nat[z][0][:, c, HD * h:HD * h + HD],
                                            X[2 * z + h][:, c, :], start=True, stop=True)
                    done(ins, ("V", z))
                for g in range(4):
                    copied(("U", g))
                for z in range(2):
                    copied(("V", z))
                    copied(("N", z, 1))
                    copied(("N", z, 2))
                pe.wait_ge(rqd, 2 * it + 2)
                half = [slice(HD * h, HD * h + HD) for h in range(2)]
                ck = lambda z, n: (n, NCK - 1 - n)[z]

                def begin_sa(n):
                    for h in range(2):
                        dst = bank(("A", n, h))
                        for z in range(2):
                            ins = pe.matmul(dst[:, HD * z:HD * z + HD], X[2 * z + h][:, ck(z, n), :],
                                            U0[2 * z + h][:, ck(z, n), :], start=(z == 0 or n == 0), stop=(n == 0))
                        if n == 0:
                            done(ins, ("A", n, h))

                begin_sa(0)
                for n in range(NCK):
                    if n:
                        for h in range(2):
                            copied(("S", n - 1, h))
                            for z in range(2):
                                ins = pe.matmul(B.tile(("A", n, h))[:, HD * z:HD * z + HD], WT[z][half[h], ck(z, n), :],
                                                S[z][half[h], n % 2, :], start=False, stop=(z == 1))
                            done(ins, ("A", n, h))
                    if n < NCK - 1:
                        for h in range(2):
                            dst = bank(("S", n, h))
                            for z in range(2):
                                out = dst[half[h], HD * z:HD * z + HD]
                                pe.matmul(out, nat[z][1][:, ck(z, n), half[h]], VS[:, ck(z, n), half[h]], start=(z == 0), stop=False)
                                if n:
                                    pe.matmul(out, ident[half[h], half[h]], S[z][half[h], n % 2, :], start=False, stop=False)
                    for h in range(2):
                        dst = bank(("Y", n, h))
                        for z in range(2):
                            out = dst[:, HD * z:HD * z + HD]
                            pe.matmul(out, SC[2 * z + h][:, ck(z, n), 384:512], VS[:, ck(z, n), half[h]], start=(z == 0), stop=False)
                            if n:
                                pe.matmul(out, RQ[z][half[h], ck(z, n), :], S[z][half[h], n % 2, :], start=False, stop=False)
                    if n < NCK - 1:
                        for h in range(2):
                            copied(("A", n, h))
                            for z in range(2):
                                ins = pe.matmul(B.tile(("S", n, h))[half[h], HD * z:HD * z + HD], nat[z][2][:, ck(z, n), half[h]],
                                                SA[:, h, z, :], start=False, stop=(z == 1))
                            done(ins, ("S", n, h))
                    for h in range(2):
                        copied(("A", n, h))
                        for z in range(2):
                            ins = pe.matmul(B.tile(("Y", n, h))[:, HD * z:HD * z + HD], SC[2 * z + h][:, ck(z, n), 128:256],
                                            SA[:, h, z, :], start=False, stop=(z == 1))
                        done(ins, ("Y", n, h))
                    if n < NCK - 1:
                        begin_sa(n + 1)

            lora(Q, 0, 0)
            with pe.Fori(0, NPAIR - 1) as it:
                trip(it, True)
            trip(NPAIR - 1, False)

        @block.scalar
        def _(act):
            act.activation(PT[:, DW, :], PT[:, DW, :], ACT.Tanh).then_inc(lora_act, 1)
            for p in range(NPAIR):
                act.activation(KK[:, p, :], PT[:, K0 + p, :], ACT.Identity,
                               scale=vec[:, rows["k_k"][0] + p:rows["k_k"][0] + p + 1]).then_inc(kraw, 1)
            for t in range(NT):
                key = ("v", t)
                act.wait_ge(Q.fill_sem(key), Q.count(0, key))
                act.activation(VN[:, t, :], Q.tile(key)[:, :], ACT.Copy).then_inc(Q.free_sem(key), 1)
            for p in range(NPAIR):
                key = ("k", p)
                act.wait_ge(Q.fill_sem(key), Q.count(0, key))
                if p >= 2:
                    act.wait_ge(kkok, p - 1)
                act.activation(sg[:, p % 2, :], Q.tile(key)[:, :], ACT.Sqrt).then_inc(Q.free_sem(key), 1)
            act.wait_ge(kkok, NPAIR)

            def sigmoids(Bk, i, m):
                for z in range(2):
                    for what, dst, row in (("w", sg, "w0"), ("a", aa, "a0")):
                        key = ("L", what, z)
                        act.wait_ge(Bk.fill_sem(key), Bk.count(i, key))
                        act.activation(dst[:, z, :], Bk.tile(key)[:, :], ACT.Sigmoid,
                                       bias=vec[:, ds(rows[row][0] + 4 * z + m, 1)]).then_inc(Bk.free_sem(key), 1)

            def exps(m, z):
                act.wait_ge(dd, 3 * (2 * m + z) + 3)
                act.activation(E3[:, :], D1[:, :], ACT.Exp, scale=KAPPA).then_inc(ed, 1)
                act.activation(D2[:, :], D2[:, :], ACT.Exp, scale=-KAPPA).then_inc(ed, 1)
                act.activation(D1[:, :], D1[:, :], ACT.Exp, scale=-KAPPA).then_inc(ed, 1)
                act.activation(Gn[:, z, z:z + 3], mid[:, z, NCK + z:NCK + z + 3], ACT.Exp, scale=-KAPPA).then_inc(gd, 1)

            def trip(it, nxt):
                def take(dst, key, src=None):
                    act.wait_ge(B.fill_sem(key), B.count(it, key))
                    act.activation(dst, B.tile(key)[:, :] if src is None else src, ACT.Copy).then_inc(B.free_sem(key), 1)

                for h in range(2):
                    key = ("Y", NCK - 1, h)
                    act.wait_ge(B.free_sem(key), B.after(it, key) - B.per[B.at[key][0]])
                act.wait_ge(prod, 8 * it + 8)
                for z in range(2):
                    act.activation(RQ[z][:, :, :], QR[z][:, :, P:2 * P], ACT.Copy).then_inc(rqd, 1)
                for z in range(2):
                    for a in range(3):
                        key = ("N", z, a)
                        act.wait_ge(B.fill_sem(key), B.count(it, key))
                        act.activation(nat[z][a][:, :, :].rearrange("p c t -> p (c t)"), B.tile(key)[:, :], ACT.Copy,
                                       scale=-1.0 if a == 2 else 1.0).then_inc(B.free_sem(key), 1)
                take(coef[:, :, ds(2 * it, 2)], ("K",), B.tile(("K",))[:, 0:8].rearrange("p (t h) -> p t h", h=2))
                for lv in range(1, NLEV):
                    for g in range(4):
                        take(XT[g][:, :, :].rearrange("p c t -> p (c t)"), ("T", lv, g))
                    if lv == 1:
                        act.wait_ge(gd, 2 * it + 2)
                        for z in range(2):
                            act.activation(G[:, z, z:z + 3], Gn[:, z, z:z + 3], ACT.Copy).then_inc(gcd, 1)
                    if nxt and lv == 1:
                        sigmoids(B, it, it + 1)
                    if nxt and lv in (2, 4):
                        exps(it + 1, lv // 2 - 1)
                for g in range(4):
                    take(U0[g], ("U", g), B.tile(("U", g))[:, 0:256].rearrange("p (c v) -> p c v", v=HD))
                for z in range(2):
                    take(WT[z][:, :, :].rearrange("p c t -> p (c t)"), ("V", z))
                act.wait_ge(gcd, 2 * it + 2)
                for n in range(NCK):
                    take(SA[:, 0, :, :].rearrange("p z v -> p (z v)"), ("A", n, 0), B.tile(("A", n, 0))[:, 0:P])
                    if n < NCK - 1:
                        key = ("S", n, 0)
                        act.wait_ge(B.fill_sem(key), B.count(it, key))
                        for z in range(2):
                            g = (n, NCK - 1 - n)[z]
                            ins = act.activation(S[z][0:HD, (n + 1) % 2, :], B.tile(key)[0:HD, HD * z:HD * z + HD],
                                                 ACT.Identity, scale=G[0:HD, z, g:g + 1])
                        ins.then_inc(B.free_sem(key), 1)

            sigmoids(Q, 0, 0)
            for z in range(2):
                exps(0, z)
            with act.Fori(0, NPAIR - 1) as it:
                trip(it, True)
            trip(NPAIR - 1, False)

        @block.vector
        def _(dve):
            ch = Chain(dve, kch)
            for p in range(NPAIR):
                key = ("k", p)
                root = sg[:, p % 2, :]
                dve.wait_ge(Q.free_sem(key), Q.after(0, key))
                ch(dve.tensor_scalar(root, root, 1e-12, None, ALU.max))
                ch(dve.reciprocal(root, root))
                dve.tensor_tensor(KK[:, p, :], KK[:, p, :], root, ALU.mult).then_inc(kkok, 1)
            dve.wait_ge(kkok, NPAIR)
            dve.wait_ge(rst, 2)
            dve.wait_ge(c_in, 16)
            dve.wait_ge(ymem, 1)

            q4 = lambda ap: ap.rearrange("p (c t) -> p c t", t=P)

            def prepare(step, ch, Bk, i, m):
                kk = flat2(KK[:, ds(m, 1), :])
                rr = flat2(PT[:, ds(R0 + m, 1), :])
                kp = flat2(PT[:, ds(K0 + m, 1), :])
                z, part = divmod(step, 4)
                s, a = sg[:, z % 2, :], aa[:, z % 2, :]
                mb = q4(Ps[:, :])[:, :, HD - 1:HD].to_broadcast([P, NCK, P])
                dst = kds if z == 0 else Ps
                if step == 8:
                    ch(dve.tensor_tensor(kds[:, :], kds[:, :], Ps[:, :], ALU.add))
                    dve.scalar_tensor_tensor(out=tmp[:, :], in0=rr, scalar=vec[:, ds(rows["r_k"][0] + m, 1)], in1=kds[:, :],
                                             op0=ALU.mult, op1=ALU.mult).then_inc(csum, 1)
                    assert ch.n == PREP, ch.n
                elif part == 0:
                    for what in "wa":
                        key = ("L", what, z)
                        dve.wait_ge(Bk.free_sem(key), Bk.after(i, key))
                    ch(dve.tensor_tensor_scan(Ps[:, :], reset[:, :], s, 0.0, ALU.mult, ALU.add))
                    M, Rm = mid[:, z, 0:NCK], mid[:, z, NCK:2 * NCK]
                    ch(dve.tensor_copy(M, q4(Ps[:, :])[:, :, HD - 1:HD].rearrange("p c a -> p (c a)")))
                    ch(dve.tensor_tensor(Rm, q4(Ps[:, :])[:, :, P - 1:P].rearrange("p c a -> p (c a)"), M, ALU.subtract))
                    if z == 0:
                        ch(dve.tensor_tensor(Rm[:, 0:3], Rm[:, 0:3], M[:, 1:4], ALU.add))
                    else:
                        ch(dve.tensor_tensor(M[:, 1:4], M[:, 1:4], Rm[:, 0:3], ALU.add))
                        ch(dve.tensor_copy(Rm[:, 1:4], M[:, 1:4]))
                elif part == 1:
                    if z == 0:
                        ch(dve.tensor_tensor(q4(D1[:, :]), q4(Ps[:, :]), mb, ALU.subtract))
                        dve.tensor_tensor(D2[:, :], D1[:, :], s, ALU.subtract).then_inc(dd, 3)
                    else:
                        ch(dve.tensor_tensor(q4(D2[:, :]), mb, q4(Ps[:, :]), ALU.subtract))
                        dve.tensor_tensor(D1[:, :], D2[:, :], s, ALU.add).then_inc(dd, 3)
                elif part == 2:
                    ch(dve.tensor_scalar(Ps[:, :], a, 1.0, vec[:, ds(rows["k_a"][0] + m, 1)], ALU.subtract, ALU.mult))
                    ch(dve.scalar_tensor_tensor(out=dst[:, :], in0=Ps[:, :], scalar=1.0, in1=kp, op0=ALU.add, op1=ALU.mult))
                    ch(dve.tensor_tensor(a, a, kk, ALU.mult))
                else:
                    dve.wait_ge(ed, 3 * (2 * m + z) + 3)
                    if Bk is B:
                        dve.wait_ge(rqd, 2 * m)
                    q = q4(D2[:, :])
                    dve.tensor_tensor(QR[z][:, :, 0:P], q4(kk), q, ALU.mult).then_inc(prod, 1)
                    dve.tensor_tensor(QR[z][:, :, P:2 * P], q4(rr), q4(D1[:, :]), ALU.mult).then_inc(prod, 1)
                    dve.tensor_tensor(KD[z][:, :], dst[:, :], E3[:, :], ALU.mult).then_inc(prod, 1)
                    dve.tensor_tensor(AD[z][:, :], a, E3[:, :], ALU.mult).then_inc(prod, 1)
                    dve.wait_ge(prod, 4 * (2 * m + z) + 4)

            def trip(it, nxt):
                ch = Chain(dve, pch, it + 1, PREP)
                prep = lambda step: prepare(step, ch, B, it, it + 1) if nxt and step < 9 else None
                for z in range(2):
                    for c in range(NCK):
                        for h in range(2):
                            key = ("X", z, c, h)
                            dve.wait_ge(B.fill_sem(key), B.count(it, key))
                            dve.tensor_tensor(SC[2 * z + h][:, c, :], B.tile(key)[:, :], scmask[z], ALU.mult)\
                               .then_inc(B.free_sem(key), 1)
                for lv in range(2, NLEV + 1):
                    for g in range(4):
                        key = ("W", lv, g)
                        dve.wait_ge(B.fill_sem(key), B.count(it, key))
                        dve.tensor_tensor(W1[g][:, :, :], q4(B.tile(key)[:, :]),
                                          lvmask[lv - 1].unsqueeze(1).to_broadcast([P, NCK, P]), ALU.mult)\
                           .then_inc(B.free_sem(key), 1)
                    prep(2 * (lv - 2))
                    for g in range(4):
                        key = ("Z", lv, g)
                        dve.wait_ge(B.fill_sem(key), B.count(it, key))
                        dve.tensor_tensor(X[g][:, :, :], X[g][:, :, :], q4(B.tile(key)[:, :]), ALU.add)\
                           .then_inc(B.free_sem(key), 1)
                    prep(2 * (lv - 2) + 1)
                dve.wait_ge(gcd, 2 * it + 2)
                for n in range(NCK):
                    key = ("A", n, 1)
                    dve.wait_ge(B.fill_sem(key), B.count(it, key))
                    dve.tensor_copy(SA[:, 1, :, :].rearrange("p z v -> p (z v)"), B.tile(key)[:, 0:P])\
                       .then_inc(B.free_sem(key), 1)
                    if n < NCK - 1:
                        key = ("S", n, 1)
                        dve.wait_ge(B.fill_sem(key), B.count(it, key))
                        for z in range(2):
                            g = (n, NCK - 1 - n)[z]
                            ins = dve.tensor_scalar(S[z][HD:P, (n + 1) % 2, :], B.tile(key)[HD:P, HD * z:HD * z + HD],
                                                    G[HD:P, z, g:g + 1], None, ALU.mult)
                        ins.then_inc(B.free_sem(key), 1)
                    for h in range(2):
                        key = ("Y", n, h)
                        if n:
                            dve.wait_ge(B.free_sem(("Y", n - 1, h)), B.after(it, ("Y", n - 1, h)))
                        dve.wait_ge(B.fill_sem(key), B.count(it, key))
                        for z in range(2):
                            dst = flat2(Y[:, (n, NCK - 1 - n)[z]:(n, NCK - 1 - n)[z] + 1, ds(P * it + HD * h, HD)])
                            ins = dve.tensor_tensor(dst, dst, B.tile(key)[:, HD * z:HD * z + HD], ALU.add)
                        ins.then_inc(B.free_sem(key), 1)

            ch0 = Chain(dve, pch)
            for step in range(9):
                prepare(step, ch0, Q, 0, 0)
            with dve.Fori(0, NPAIR - 1) as it:
                trip(it, True)
            trip(NPAIR - 1, False)


def mixed_output(nc, psum, ext, keep):
    rows, nrows = vec_rows()
    with ExitStack() as ctx:
        sb = lambda name, shape, dt=F32: ctx.enter_context(nc.sbuf_tensor("mix_" + name, shape, dt))
        sem = phase_semaphores(nc, ctx, "mix")
        x, ident, vec, att, Y, VN, coef = (keep[k] for k in ("x", "ident", "vec", "att", "rk", "VN", "coef"))
        dg = keep["PTb"][:, 14, :]
        g2 = sb("g2", [P, C])
        lnw = sb("ln_w", [P, C])
        lnb = sb("ln_b", [P, C])
        cat_hi = sb("cat_hi", [P, KD, T], F32R)
        cat_lo = sb("cat_lo", [P, KD, T], F32R)
        sq = sb("squares", [P, NT, C])
        bonus = sb("bonus", [P, NT, C])
        st = sb("gn_sum", [P, NT, NH])
        vr = sb("gn_var", [P, NT, NH])
        ss = sb("att_sumsq", [P, NT])
        NS = 4
        raw = sb("wo_raw", [P, NS, D])
        w_hi = sb("wo_hi", [P, NS, D], F32R)
        w_lo = sb("wo_lo", [P, NS, D], F32R)
        g2_in = sem("g2_in")
        ln_in = sem("ln_in")
        raw_in = [sem(f"wo_in{s}") for s in range(NS)]
        hi_w = [sem(f"wo_hi_done{s}") for s in range(NS)]
        lo_w = [sem(f"wo_lo_done{s}") for s in range(NS)]
        used = [sem(f"wo_used{s}") for s in range(NS)]
        gate = sem("gate_done")
        asum = sem("att_sums_done")
        aroot = sem("att_roots_done")
        an = sem("att_norm_done")
        avar = sem("att_var_done")
        chn = sem("gn_chain")
        cent = sem("centred")
        sqd = sem("squared")
        vrd = sem("var_done")
        root = sem("gn_root")
        bon = sem("bonus_done")
        rkd = sem("rk_done")
        hi_c = sem("cat_hi_done")
        Gk = Banks(sem, "gate", psum, [("g", t) for t in range(NT)] + [("c", k) for k in range(KD)]
                   + [("o", t, n) for t in range(NT) for n in range(2)])
        wo = ext["w_o"].rearrange("(k p) n -> p k n", p=P)

        block = ctx.enter_context(nc.Block())

        @block.sync
        def _(sp):
            sp.dma_start(g2[:, :], ext["g2"]).then_inc(g2_in, 16)
            for dst, name in ((lnw, "ln_w"), (lnb, "ln_b")):
                sp.dma_start(dst[:, :], ext[name].partition_broadcast(P)).then_inc(ln_in, 16)
            for k in range(KD):
                if k >= NS:
                    sp.wait_ge(lo_w[k % NS], k // NS)
                sp.dma_start(raw[:, k % NS, :], wo[:, k, :]).then_inc(raw_in[k % NS], 16)

        @block.gpsimd
        def _(pool):
            for b in range(8):
                pool.sem_inc(Gk.freed[b], 1)
            for t in range(NT):
                h3 = lambda ap: ap.rearrange("p (h v) -> p h v", h=NH)
                pool.tensor_tensor(h3(bonus[:, t, :]), h3(VN[:, t, :]),
                                   coef[:, t, :].unsqueeze(2).to_broadcast([P, NH, HD]), ALU.mult).then_inc(bon, 1)

        @block.tensor
        def _(pe):
            pe.wait_ge(gate, 1)
            pe.wait_ge(g2_in, 16)
            for t in range(NT):
                key = ("g", t)
                pe.wait_ge(Gk.free_sem(key), Gk.before(0, key))
                pe.matmul(Gk.tile(key)[:, :], dg[:, P * t:P * t + P], g2[:, :], start=True, stop=True)\
                  .then_inc(Gk.fill_sem(key), 1)
            for k in range(KD):
                key = ("c", k)
                pe.wait_ge(Gk.free_sem(key), Gk.before(0, key))
                for t in range(NT):
                    if k < 4:
                        if k == 0:
                            pe.wait_ge(an, t + 1)
                        dst = Gk.tile(key).rearrange("p (r j c) -> p j r c", j=NT, c=QC)[:, t, :, :]
                        ins = pe.transpose(dst, att[:, t, P * k:P * k + P], ident[:, :])
                    else:
                        if k == 4:
                            pe.wait_ge(rkd, t + 1)
                        ins = pe.transpose(Gk.tile(key)[:, P * t:P * t + P], Y[:, t, P * (k - 4):P * (k - 4) + P], ident[:, :])
                ins.then_inc(Gk.fill_sem(key), 1)
            for k in range(KD):
                s = k % NS
                pe.wait_ge(Gk.free_sem(("c", k)), Gk.after(0, ("c", k)))
                pe.wait_ge(lo_w[s], k // NS + 1)
                for t in range(NT):
                    for n in range(2):
                        key = ("o", t, n)
                        if k == 0:
                            pe.wait_ge(Gk.free_sem(key), Gk.before(0, key))
                        out = Gk.tile(key)[:, :]
                        col = slice(512 * n, 512 * n + 512)
                        tok = slice(P * t, P * t + P)
                        pe.matmul(out, cat_hi[:, k, tok], w_hi[:, s, col], start=(k == 0), stop=False)
                        pe.matmul(out, cat_lo[:, k, tok], w_hi[:, s, col], start=False, stop=False)
                        ins = pe.matmul(out, cat_hi[:, k, tok], w_lo[:, s, col], start=False, stop=(k == KD - 1))
                        if k == KD - 1:
                            ins.then_inc(Gk.fill_sem(key), 1)
                if k < KD - 1:
                    ins.then_inc(used[s], 1)

        @block.scalar
        def _(act):
            act.activation(dg, dg, ACT.Sigmoid).then_inc(gate, 1)
            for t in range(NT):
                act.activation(sq[:, t, :], att[:, t, :], ACT.Square, accum_out=ss[:, t:t + 1]).then_inc(asum, 1)
            act.wait_ge(avar, 1)
            act.activation(ss[:, :], ss[:, :], ACT.Sqrt).then_inc(aroot, 1)

            def split_w(k):
                s = k % NS
                act.wait_ge(raw_in[s], 16 * (k // NS) + 16)
                if k >= NS:
                    act.wait_ge(used[s], k // NS)
                act.activation(w_hi[:, s, :], raw[:, s, :], ACT.Copy).then_inc(hi_w[s], 1)

            for k in range(NS):
                split_w(k)
            for t in range(NT):
                act.wait_ge(cent, t + 1)
                act.activation(sq[:, t, :], Y[:, t, :], ACT.Square).then_inc(sqd, 1)
            for t in range(NT):
                act.wait_ge(vrd, t + 1)
                act.activation(vr[:, t, :], vr[:, t, :], ACT.Sqrt).then_inc(root, 1)
            for k in range(KD):
                key = ("c", k)
                act.wait_ge(Gk.fill_sem(key), Gk.count(0, key))
                scale = vec[:, rows["attn_norm_w"][0] + k:rows["attn_norm_w"][0] + k + 1] if k < 4 else 1.0
                act.activation(cat_hi[:, k, :], Gk.tile(key)[:, :], ACT.Identity, scale=scale).then_inc(hi_c, 1)
            for k in range(NS, KD):
                split_w(k)

        @block.vector
        def _(dve):
            ch = Chain(dve, chn)
            h3 = lambda ap: ap.rearrange("p (h v) -> p h v", h=NH)
            wide = lambda ap: ap.unsqueeze(2).to_broadcast([P, NH, HD])
            dve.wait_ge(asum, NT)
            dve.tensor_scalar(ss[:, :], ss[:, :], 1.0 / C, RMS_EPS, ALU.mult, ALU.add).then_inc(avar, 1)
            for t in range(NT):
                ch(dve.tensor_reduce(st[:, t, :], h3(Y[:, t, :]), AX.X, ALU.add))
                ch(dve.tensor_scalar(st[:, t, :], st[:, t, :], 1.0 / HD, None, ALU.mult))
                dve.tensor_tensor(h3(Y[:, t, :]), h3(Y[:, t, :]), wide(st[:, t, :]), ALU.subtract).then_inc(cent, 1)
            dve.wait_ge(aroot, 1)
            ch(dve.reciprocal(ss[:, :], ss[:, :]))
            for t in range(NT):
                dve.tensor_scalar(att[:, t, :], att[:, t, :], ss[:, t:t + 1], None, ALU.mult).then_inc(an, 1)
            for t in range(NT):
                dve.wait_ge(sqd, t + 1)
                ch(dve.tensor_reduce(vr[:, t, :], h3(sq[:, t, :]), AX.X, ALU.add))
                dve.tensor_scalar(vr[:, t, :], vr[:, t, :], 1.0 / HD, GN_EPS, ALU.mult, ALU.add).then_inc(vrd, 1)

            def split_w(k):
                s = k % NS
                dve.wait_ge(hi_w[s], k // NS + 1)
                dve.tensor_tensor(w_lo[:, s, :], raw[:, s, :], w_hi[:, s, :].bitcast(F32), ALU.subtract).then_inc(lo_w[s], 1)

            for k in range(NS):
                split_w(k)
            dve.wait_ge(ln_in, 32)
            for t in range(NT):
                y = Y[:, t, :]
                dve.wait_ge(root, t + 1)
                ch(dve.reciprocal(vr[:, t, :], vr[:, t, :]))
                ch(dve.tensor_tensor(h3(y), h3(y), wide(vr[:, t, :]), ALU.mult))
                ch(dve.tensor_tensor(y, y, lnw[:, :], ALU.mult))
                ch(dve.tensor_tensor(y, y, lnb[:, :], ALU.add))
                dve.wait_ge(bon, t + 1)
                ch(dve.tensor_tensor(y, y, bonus[:, t, :], ALU.add))
                key = ("g", t)
                dve.wait_ge(Gk.fill_sem(key), Gk.count(0, key))
                dve.tensor_tensor(y, y, Gk.tile(key)[:, :], ALU.mult).then_inc(Gk.free_sem(key), 1)
                dve.wait_ge(Gk.free_sem(key), Gk.after(0, key))
                dve.sem_inc(rkd, 1)
            for k in range(KD):
                key = ("c", k)
                dve.wait_ge(hi_c, k + 1)
                scale = vec[:, rows["attn_norm_w"][0] + k:rows["attn_norm_w"][0] + k + 1] if k < 4 else 1.0
                dve.scalar_tensor_tensor(out=cat_lo[:, k, :], in0=Gk.tile(key)[:, :], scalar=scale,
                                         in1=cat_hi[:, k, :].bitcast(F32), op0=ALU.mult, op1=ALU.subtract)\
                   .then_inc(Gk.free_sem(key), 1)
            for k in range(NS, KD):
                split_w(k)
            for t in range(NT):
                for n in range(2):
                    key = ("o", t, n)
                    dst = x[:, t, 512 * n:512 * n + 512]
                    dve.wait_ge(Gk.fill_sem(key), Gk.count(0, key))
                    dve.tensor_tensor(dst, dst, Gk.tile(key)[:, :], ALU.add).then_inc(Gk.free_sem(key), 1)


NOV = 15
FAR = 4096


def router(nc, psum, ext, keep, hn_dram):
    rows, nrows = vec_rows()
    with ExitStack() as ctx:
        sb = lambda name, shape, dt=F32: ctx.enter_context(nc.sbuf_tensor("route_" + name, shape, dt))
        sem = phase_semaphores(nc, ctx, "route")
        x, ident = keep["x"], keep["ident"]
        gates, posm, meta, over, biasb = (keep[k] for k in ("gates", "posm", "meta", "over", "biasb"))
        iota = keep["iota"]
        w2 = sb("norm2_bcast", [P, D])
        hn = sb("hn", [P, NT, D])
        hT = sb("hn_turned", [P, KD, T])
        rw = sb("router_w", [P, KD, E])
        rb = sb("router_b", [P, E])
        ss = sb("h_sumsq", [P, NT])
        lg = sb("logits", [P, NT, E])
        top = sb("top_values", [P, NT, 8])
        tix = sb("top_index", [P, NT, 8], U32)
        tif = sb("top_index_f", [P, NT, TOPK])
        neg = sb("neg_top", [P, NT])
        esum = sb("gate_sums", [P, NT])
        eq = sb("chosen", [P, NT, TOPK, E])
        msk = sb("mask", [P, NT, E])
        mskb = sb("mask_bf16", [P, NT, E], BF16)
        rank = sb("rank", [P, NT, E])
        rc = sb("router_consts", [P, TOPK * E + NT * E + NOV])
        rank512 = rc[:, 0:TOPK * E].rearrange("p (k e) -> p k e", k=TOPK)
        tbase = rc[:, TOPK * E:TOPK * E + NT * E].rearrange("p (t e) -> p t e", t=NT)
        oiota = rc[:, TOPK * E + NT * E:TOPK * E + NT * E + NOV]
        tri = sb("earlier_ones", [P, 2 * P], BF16)
        cnt = sb("counts", [P, E])
        nov = sb("overflows", [P, E])
        inc = sb("overflow_sums", [P, E])
        le = sb("overflow_le", [P, NOV, E])
        ov = sb("overflow_f", [P, 2, NOV])
        ovn = sb("overflow_n", [P, NOV])
        ones = sb("ones_row", [P, E])
        braw = sb("bias_raw", [96, 3 * F])
        c_in = sem("router_consts_in")
        b_in = sem("bias_in")
        hsum = sem("h_sums_done")
        hvar = sem("h_var_done")
        hroot = sem("h_root_done")
        chn = sem("router_chain")
        hnd = sem("hn_done")
        hno = sem("hn_out")
        topd = sem("top_done")
        gex = sem("gate_exp_done")
        mdone = sem("mask_done")
        bz = sem("bias_zeroed")
        bh = sem("bias_parts_cast")
        br = sem("bias_rests")
        B = Banks(sem, "route", psum, [("t", k) for k in range(KD)] + [("l", t) for t in range(NT)] + [("p",)])

        block = ctx.enter_context(nc.Block())

        @block.sync
        def _(sp):
            sp.dma_start(w2[:, :], ext["norm2_row"].partition_broadcast(P)).then_inc(c_in, 16)
            sp.dma_start(rw[:, :, :], ext["router_w"].rearrange("(k p) e -> p k e", p=P)).then_inc(c_in, 16)
            sp.dma_start(rb[:, :], ext["router_b"].partition_broadcast(P)).then_inc(c_in, 16)
            sp.dma_start(rc[:, :], ext["c_router"]).then_inc(c_in, 16)
            sp.dma_start(tri[:, :], ext["c_tri"].bitcast(BF16)).then_inc(c_in, 16)
            sp.dma_start(iota[:, :], ext["c_iota"].partition_broadcast(P)).then_inc(c_in, 16)
            for g in range(3):
                sp.dma_start(braw[E * g:E * g + E, 0:2 * F], ext["expert_b_up"]).then_inc(b_in, 16)
                sp.dma_start(braw[E * g:E * g + E, 2 * F:3 * F], ext["expert_b_down"]).then_inc(b_in, 16)
            sp.dma_start(keep["selb"][:, :, :], ext["c_selb"].bitcast(BF16).rearrange("p (e s) -> p e s", e=E)).then_inc(b_in, 16)
            sp.dma_start(keep["prow"][:, :], ext["c_prow"].bitcast(BF16)).then_inc(b_in, 16)
            hd = hn_dram.rearrange("(t p) d -> p t d", p=P)
            for t in range(NT):
                sp.wait_ge(hnd, t + 1)
                sp.dma_start(hd[:, t, :], hn[:, t, :]).then_inc(hno, 16)
            sp.wait_ge(hno, 16 * NT)
            sp.wait_ge(b_in, 16 * 8)

        @block.gpsimd
        def _(pool):
            for b in range(8):
                pool.sem_inc(B.freed[b], 1)
            pool.memset(biasb[:, :], 0.0).then_inc(bz, 1)
            pool.memset(ones[:, :], 1.0).then_inc(bz, 1)

        @block.scalar
        def _(act):
            for t in range(NT):
                act.activation(hn[:, t, :], x[:, t, :], ACT.Square, accum_out=ss[:, t:t + 1]).then_inc(hsum, 1)
            act.wait_ge(hvar, 1)
            act.activation(ss[:, :], ss[:, :], ACT.Sqrt).then_inc(hroot, 1)
            act.wait_ge(b_in, 16 * 8)
            act.wait_ge(bz, 2)
            for g in range(3):
                act.activation(biasb[E * g:E * g + E, :], braw[E * g:E * g + E, :], ACT.Copy).then_inc(bh, 1)
            for k in range(KD):
                key = ("t", k)
                act.wait_ge(B.fill_sem(key), B.count(0, key))
                act.activation(hT[:, k, :], B.tile(key)[:, :], ACT.Copy).then_inc(B.free_sem(key), 1)
            act.wait_ge(br, 2)
            for g in range(1, 3):
                act.activation(biasb[E * g:E * g + E, :], braw[E * g:E * g + E, :], ACT.Copy).then_inc(bh, 1)
            for t in range(NT):
                act.wait_ge(topd, t + 1)
                act.activation(gates[:, t, :], top[:, t, 0:TOPK], ACT.Exp, bias=neg[:, t:t + 1],
                               accum_out=esum[:, t:t + 1]).then_inc(gex, 1)
            act.wait_ge(br, 3)
            act.activation(biasb[2 * E:3 * E, :], braw[2 * E:3 * E, :], ACT.Copy).then_inc(bh, 1)

        @block.tensor
        def _(pe):
            for t in range(NT):
                pe.wait_ge(hnd, t + 1)
                for k in range(KD):
                    key = ("t", k)
                    if t == 0:
                        pe.wait_ge(B.free_sem(key), B.before(0, key))
                    ins = pe.transpose(B.tile(key)[:, P * t:P * t + P], hn[:, t, P * k:P * k + P], ident[:, :])
                    if t == NT - 1:
                        ins.then_inc(B.fill_sem(key), 1)
            pe.wait_ge(c_in, 16 * 6)
            for k in range(KD):
                pe.wait_ge(B.free_sem(("t", k)), B.after(0, ("t", k)))
            for t in range(NT):
                key = ("l", t)
                for k in range(KD):
                    ins = pe.matmul(B.tile(key)[:, 0:E], hT[:, k, P * t:P * t + P], rw[:, k, :], start=(k == 0), stop=(k == KD - 1))
                ins.then_inc(B.fill_sem(key), 1)
            pe.wait_ge(mdone, 1)
            dst = B.tile(("p",))
            for t in range(NT + 1):
                out = dst[:, E * t:E * t + E]
                parts = [(P, u) for u in range(t)] + ([(0, t)] if t < NT else [])
                for i, (c, u) in enumerate(parts):
                    ins = pe.matmul(out, tri[:, c:c + P], mskb[:, u, :], start=(i == 0), stop=(i == len(parts) - 1))
            ins.then_inc(B.fill_sem(("p",)), 1)

        @block.vector
        def _(dve):
            ch = Chain(dve, chn)
            dve.wait_ge(hsum, NT)
            dve.tensor_scalar(ss[:, :], ss[:, :], 1.0 / D, RMS_EPS, ALU.mult, ALU.add).then_inc(hvar, 1)
            dve.wait_ge(hroot, 1)
            ch(dve.reciprocal(ss[:, :], ss[:, :]))
            dve.wait_ge(c_in, 16 * 6)
            for t in range(NT):
                ch(dve.tensor_scalar(hn[:, t, :], x[:, t, :], ss[:, t:t + 1], None, ALU.mult))
                dve.tensor_tensor(hn[:, t, :], hn[:, t, :], w2[:, :], ALU.mult).then_inc(hnd, 1)
            for g in range(1, 3):
                dve.wait_ge(bh, 3)
                r = slice(E * g, E * g + E)
                dve.tensor_tensor(braw[r, :], braw[r, :], biasb[r, :], ALU.subtract).then_inc(br, 1)
            for t in range(NT):
                key = ("l", t)
                dve.wait_ge(B.fill_sem(key), B.count(0, key))
                dve.tensor_tensor(lg[:, t, :], B.tile(key)[:, 0:E], rb[:, :], ALU.add).then_inc(B.free_sem(key), 1)
                dve.wait_ge(B.free_sem(key), B.after(0, key))
                ch(dve.max(top[:, t, :], lg[:, t, :]))
                ch(dve.max_index(tix[:, t, :], top[:, t, :], lg[:, t, :]))
                dve.tensor_scalar(neg[:, t:t + 1], top[:, t, 0:1], -1.0, None, ALU.mult).then_inc(topd, 1)
            ch(dve.tensor_copy(tif[:, :, :], tix[:, :, 0:TOPK]))
            ch(dve.tensor_tensor(eq[:, :, :, :].rearrange("p t k e -> p (t k) e"),
                                 iota[:, 0:E].unsqueeze(1).to_broadcast([P, NT * TOPK, E]),
                                 tif[:, :, :].rearrange("p t k -> p (t k)").unsqueeze(2).to_broadcast([P, NT * TOPK, E]),
                                 ALU.is_equal))
            ch(dve.tensor_reduce(msk[:, :, :], eq[:, :, :, :].rearrange("p t k e -> p t e k"), AX.X, ALU.add))
            dve.tensor_copy(mskb[:, :, :], msk[:, :, :]).then_inc(mdone, 1)
            for t in range(NT):
                ch(dve.tensor_tensor(eq[:, t, :, :], eq[:, t, :, :], rank512, ALU.mult))
            ch(dve.tensor_reduce(rank[:, :, :], eq[:, :, :, :].rearrange("p t k e -> p t e k"), AX.X, ALU.add))
            ch(dve.tensor_copy(meta[:, :, :, 0], tbase))
            ch(dve.tensor_tensor(meta[:, :, :, 1], rank[:, :, :], tbase, ALU.add))
            dve.wait_ge(gex, NT)
            ch(dve.reciprocal(esum[:, :], esum[:, :]))
            ch(dve.tensor_tensor(gates[:, :, :], gates[:, :, :], esum[:, :].unsqueeze(2).to_broadcast([P, NT, TOPK]), ALU.mult))
            key = ("p",)
            pos = B.tile(key)[:, 0:NT * E].rearrange("p (t e) -> p t e", t=NT)
            dve.wait_ge(B.fill_sem(key), B.count(0, key))
            dve.wait_ge(mdone, 1)
            ch(dve.tensor_scalar(posm[:, :, :], pos, 1.0, None, ALU.add))
            ch(dve.tensor_tensor(posm[:, :, :], posm[:, :, :], msk[:, :, :], ALU.mult))
            ch(dve.tensor_scalar(posm[:, :, :], posm[:, :, :], -1.0, None, ALU.add))
            ch(dve.tensor_copy(cnt[:, :], B.tile(key)[:, NT * E:NT * E + E]))
            ch(dve.tensor_scalar(nov[:, :], cnt[:, :], float(P), None, ALU.is_gt))
            for m in (2, 3):
                ch(dve.tensor_scalar(inc[:, :], cnt[:, :], float(P * m), None, ALU.is_gt))
                ch(dve.tensor_tensor(nov[:, :], nov[:, :], inc[:, :], ALU.add))
            dve.wait_ge(bz, 2)
            ch(dve.tensor_tensor_scan(inc[:, :], ones[:, :], nov[:, :], 0.0, ALU.mult, ALU.add))
            ch(dve.tensor_tensor(le[:, :, :], inc[:, :].unsqueeze(1).to_broadcast([P, NOV, E]),
                                 oiota.unsqueeze(2).to_broadcast([P, NOV, E]), ALU.is_le))
            ch(dve.tensor_reduce(ov[:, 0, :], le[:, :, :], AX.X, ALU.add))
            ch(dve.tensor_tensor(le[:, :, :], le[:, :, :], nov[:, :].unsqueeze(1).to_broadcast([P, NOV, E]), ALU.mult))
            ch(dve.tensor_reduce(ovn[:, :], le[:, :, :], AX.X, ALU.add))
            ch(dve.tensor_scalar(ov[:, 0, :], ov[:, 0, :], float(E - 1), None, ALU.min))
            ch(dve.tensor_tensor(ov[:, 1, :], oiota, ovn[:, :], ALU.subtract))
            ch(dve.tensor_scalar(ov[:, 1, :], ov[:, 1, :], float(P), float(P), ALU.mult, ALU.add))
            ch(dve.tensor_scalar(ov[:, 1, :], ov[:, 1, :], float(3 * P), None, ALU.min))
            ch(dve.tensor_copy(over[:, 0:2 * NOV], ov[:, :, :].rearrange("p a i -> p (a i)")))
            ch(dve.tensor_copy(over[:, 2 * NOV:2 * NOV + 1], inc[:, E - 1:E]))
            dve.wait_ge(bh, 5)
            r = slice(2 * E, 3 * E)
            dve.tensor_tensor(braw[r, :], braw[r, :], biasb[r, :], ALU.subtract).then_inc(br, 1)


EXPERT_BANKS = {"U10": 2, "U11": 3, "A0": 6, "X0": 7, "X1": 7, "D0": 4, "D1": 5, "U00": 0, "U01": 1, "A1": 6, "M": 7}


def expert_banks(sem, name, psum, keys):
    return Banks(sem, name, psum, keys, [EXPERT_BANKS[k[1]] for k in keys])


def experts(nc, psum, ext, keep, hn_dram, c_dram):
    RAW, RING = 6, 4
    PAIRS = E // 2
    with ExitStack() as ctx:
        sb = lambda name, shape, dt=F32: ctx.enter_context(nc.sbuf_tensor("moe_" + name, shape, dt))
        sem = phase_semaphores(nc, ctx, "moe")
        ident = keep["ident"]
        posm, meta, over, biasb, selb, prow, iota = (keep[k] for k in ("posm", "meta", "over", "biasb", "selb", "prow", "iota"))
        raw = sb("w_raw", [P, RAW, 2 * D])
        w_hi = sb("w_hi", [P, RING, 2 * D], F32R)
        w_lo = sb("w_lo", [P, RING, 2 * D], F32R)
        xg = sb("x_gathered", [P, D])
        x_hi = sb("x_hi", [P, KD, P], F32R)
        x_lo = sb("x_lo", [P, KD, P], F32R)
        a_hi = sb("a_hi", [P, KD, P], F32R)
        a_lo = sb("a_lo", [P, KD, P], F32R)
        gm = sb("gate_part", [P, 2, 512])
        lm = sb("linear_part", [P, 2, 512])
        sg = sb("sigmoid_part", [P, 2, 512])
        an = sb("act_natural", [P, D])
        y = sb("y", [P, D])
        sel = sb("slot_of_token", [P, NT, P], BF16)
        from_row = sb("gather_rows", [P, 1], I32)
        to_next = sb("scatter_rows_next", [P, 1], I32)
        to_row = sb("scatter_rows", [P, 2], I32)

        raw_in = [sem(f"w_in{i}") for i in range(RAW)]
        hi_w = [sem(f"w_hi_done{i}") for i in range(RING)]
        lo_w = [sem(f"w_lo_done{i}") for i in range(RING)]
        used = [sem(f"w_used{i}") for i in range(RING)]
        seld = sem("sel_done")
        gathered = sem("gathered")
        idxd = sem("row_numbers_done")
        scattered = sem("scattered")
        begun = sem("gathers_scatters_begun")
        rows_out = sem("rows_out")
        tod = sem("scatter_rows_done")
        hi_x = sem("x_hi_done")
        hi_a = sem("a_hi_done")
        sigd = sem("sigmoid_done")
        lmd = sem("linear_done")
        glud = sem("glu_done")
        actd = sem("act_done")
        cleared = sem("x_cleared")
        main = expert_banks(sem, "moe", psum, [(par, k) for par in range(2) for k in
                            ("U10", "U11", "A0", "X0", "X1", "D0", "D1", "U00", "U01", "A1", "M")])
        pro = expert_banks(sem, "moepro", psum, [(0, k) for k in ("M", "X0", "X1", "U00", "U01")] + [(1, "M")])
        more = expert_banks(sem, "moeov", psum,
                            [(0, k) for k in ("M", "X0", "X1", "U00", "U01", "U10", "U11", "A0", "D0", "D1", "A1")])
        up, down = ext["expert_w_up"], ext["expert_w_down"]
        nslot = lambda n, j: 3 * n + j // RING

        def load(sp, n, j, part, e, kp):
            sp.wait_ge(lo_w[(j - RAW) % RING], 3 * n + (j - RAW) // RING + 3)
            r = j % RAW
            for k2 in range(2):
                dst = raw[:, r, D * k2:D * k2 + D]
                rows = slice(256 * kp + P * k2, 256 * kp + P * k2 + P)
                if part < 2:
                    src = up[ds(e, 1), rows, :].rearrange("a p (g h c) -> p (a g) h c", g=2, h=2)
                    sp.dma_start(dst.rearrange("p (g c) -> p g c", g=2), src[:, :, part, :]).then_inc(raw_in[r], 16)
                else:
                    sp.dma_start(dst, down[ds(e, 1), rows, :].rearrange("a p c -> p (a c)")).then_inc(raw_in[r], 16)

        def load_lead_in(sp, n, e):
            for kp in range(4):
                load(sp, n, kp, 0, e, kp)

        def load_block(sp, n, e, nxt):
            what = [(1, e, kp) for kp in range(4)] + [(2, e, kp) for kp in (0, 1)]
            if nxt:
                what += [(0, e + 1, kp) for kp in range(4)]
            what += [(2, e, kp) for kp in (2, 3)]
            for j, (part, ee, kp) in enumerate(what):
                load(sp, n, 4 + j, part, ee, kp)

        def split_hi(act, n, j):
            act.wait_ge(raw_in[j % RAW], 32 * (2 * n + j // RAW) + 32)
            act.wait_ge(used[j % RING], nslot(n, j) + 1)
            act.activation(w_hi[:, j % RING, :], raw[:, j % RAW, :], ACT.Copy).then_inc(hi_w[j % RING], 1)

        def split_lo(eng, n, j):
            eng.wait_ge(hi_w[j % RING], nslot(n, j) + 1)
            eng.tensor_tensor(w_lo[:, j % RING, :], raw[:, j % RAW, :], w_hi[:, j % RING, :].bitcast(F32), ALU.subtract)\
               .then_inc(lo_w[j % RING], 1)

        def slot_matmuls(pe, n, j, B, it, keys, s_hi, s_lo, k0):
            pe.wait_ge(lo_w[j % RING], nslot(n, j) + 3)
            for k2 in range(2):
                k = k0 + k2
                for i, key in enumerate(keys):
                    first = k == 0
                    if first:
                        pe.wait_ge(B.free_sem(key), B.before(it, key))
                    out = B.tile(key)[:, :]
                    w = slice(1024 * k2 + 512 * i, 1024 * k2 + 512 * i + 512)
                    pe.matmul(out, s_hi[:, k, :], w_hi[:, j % RING, w], start=first, stop=False)
                    pe.matmul(out, s_lo[:, k, :], w_hi[:, j % RING, w], start=False, stop=False)
                    ins = pe.matmul(out, s_hi[:, k, :], w_lo[:, j % RING, w], start=False, stop=False)
            ins.then_inc(used[j % RING], 1)

        def add_bias(pe, e, B, key, col):
            pe.matmul(B.tile(key)[:, :], selb[:, ds(e, 1), :].rearrange("p a s -> p (a s)"), biasb[:, col:col + 512],
                      start=False, stop=True).then_inc(B.fill_sem(key), 1)

        def pe_meta(pe, n, e, B, it, key):
            pe.wait_ge(seld, n + 1)
            pe.wait_ge(B.free_sem(key), B.before(it, key))
            for t in range(NT):
                pe.matmul(B.tile(key)[:, 0:2], sel[:, t, :], prow[:, :], start=(t == 0), stop=False)
                ins = pe.matmul(B.tile(key)[:, 0:2], sel[:, t, :],
                                meta[:, t, ds(e, 1), :].rearrange("p a b -> p (a b)"), start=False, stop=(t == NT - 1))
            ins.then_inc(B.fill_sem(key), 1)

        def pe_turn(pe, B, it, key, src, half):
            pe.wait_ge(B.free_sem(key), B.before(it, key))
            for q in range(4):
                k = 4 * half + q
                ins = pe.transpose(B.tile(key)[:, P * q:P * q + P], src[:, P * k:P * k + P], ident[:, :])
            ins.then_inc(B.fill_sem(key), 1)

        def take_hi(act, B, it, key, dst, half, done):
            act.wait_ge(B.fill_sem(key), B.count(it, key))
            act.activation(dst[:, 4 * half:4 * half + 4, :].rearrange("p k s -> p (k s)"), B.tile(key)[:, :], ACT.Copy)\
               .then_inc(done, 1)

        def take_lo(dve, B, it, key, hi, lo, half, done, count):
            dve.wait_ge(done, count)
            part = lambda ap: ap[:, 4 * half:4 * half + 4, :].rearrange("p k s -> p (k s)")
            dve.tensor_tensor(part(lo), B.tile(key)[:, :], part(hi).bitcast(F32), ALU.subtract).then_inc(B.free_sem(key), 1)

        def dve_sel(dve, n, e, off):
            for t in range(NT):
                ins = dve.tensor_scalar(sel[:, t, :], iota[:, ds(off, P)], posm[:, t, ds(e, 1)], None, ALU.is_equal)
            ins.then_inc(seld, 1)

        def dve_rows(dve, B, it, key):
            dve.wait_ge(B.fill_sem(key), B.count(it, key))
            dve.tensor_scalar(to_next[:, :], B.tile(key)[:, 1:2], float(FAR), None, ALU.add).then_inc(idxd, 1)
            dve.tensor_scalar(from_row[:, :], B.tile(key)[:, 0:1], float(FAR), None, ALU.add).then_inc(B.free_sem(key), 1)

        def dve_to_row(dve, n, par, before):
            dve.wait_ge(idxd, n + 1)
            if before is not None:
                dve.wait_ge(rows_out, before + 1)
            dve.tensor_copy(to_row[:, par:par + 1], to_next[:, :]).then_inc(tod, 1)

        def pool_gather(pool, B, it, key):
            pool.wait_ge(B.free_sem(key), B.after(it, key))
            pool.sem_inc(begun, 1)
            pool.indirect_dma_start(out=xg[:, :], out_offset=None, in_=hn_dram,
                                    in_offset=bass.IndirectOffsetOnAxis(ap=from_row[:, 0:1], axis=0),
                                    bounds_check=T - 1, oob_is_err=False).then_inc(gathered, 16)

        def pool_scatter(pool, n, B, it, par):
            pool.wait_ge(tod, n + 1)
            for k in ("D0", "D1"):
                pool.wait_ge(B.free_sem((par, k)), B.after(it, (par, k)))
            pool.sem_inc(begun, 1)
            pool.indirect_dma_start(out=c_dram, out_offset=bass.IndirectOffsetOnAxis(ap=to_row[:, par:par + 1], axis=0),
                                    in_=y[:, :], in_offset=None,
                                    bounds_check=TOPK * T - 1, oob_is_err=False).then_inc(scattered, 16)
            pool.wait_ge(scattered, 16 * n + 16)
            pool.sem_inc(rows_out, 1)

        def dve_swiglu(dve, n, B, it, par, hf, part):
            g, l = (par, f"U{hf}0"), (par, f"U{hf}1")
            if part == 0:
                dve.wait_ge(B.fill_sem(g), B.count(it, g))
                dve.tensor_scalar(gm[:, hf, :], B.tile(g)[:, :], 7.0, None, ALU.min).then_inc(B.free_sem(g), 1)
                dve.wait_ge(B.fill_sem(l), B.count(it, l))
                dve.tensor_scalar(lm[:, hf, :], B.tile(l)[:, :], 7.0, -7.0, ALU.min, ALU.max).then_inc(B.free_sem(l), 1)
            else:
                dve.wait_ge(B.free_sem(l), B.after(it, l))
                dve.scalar_tensor_tensor(out=lm[:, hf, :], in0=lm[:, hf, :], scalar=1.0, in1=gm[:, hf, :],
                                         op0=ALU.add, op1=ALU.mult).then_inc(glud, 1)
                dve.wait_ge(glud, 2 * n + hf + 1)
                dve.wait_ge(sigd, 2 * n + hf + 1)
                dve.tensor_tensor(an[:, 512 * hf:512 * hf + 512], lm[:, hf, :], sg[:, hf, :], ALU.mult).then_inc(actd, 1)

        def act_sigmoid(act, n, B, it, par, hf):
            g = (par, f"U{hf}0")
            act.wait_ge(B.free_sem(g), B.after(it, g))
            act.activation(sg[:, hf, :], gm[:, hf, :], ACT.Sigmoid, scale=1.702).then_inc(sigd, 1)

        POOL_LO = (10, 14)

        def pe_block(pe, n, e, B, it, par, nxt, nxt2):
            keys = [(par, "U10"), (par, "U11")]
            for j in range(4, 8):
                slot_matmuls(pe, n, j, B, it, keys, x_hi, x_lo, 2 * (j - 4))
                if j == 5:
                    pe.wait_ge(actd, 2 * n + 1)
                    pe_turn(pe, B, it, (par, "A0"), an, 0)
            for i, key in enumerate(keys):
                add_bias(pe, e, B, key, F * i + 512)
            if nxt:
                pe.wait_ge(gathered, 16 * n + 32)
                pe_turn(pe, B, it, (par, "X0"), xg, 0)
            keys = [(par, "D0"), (par, "D1")]
            pe.wait_ge(B.free_sem((par, "A0")), B.after(it, (par, "A0")))
            slot_matmuls(pe, n, 8, B, it, keys, a_hi, a_lo, 0)
            if nxt:
                pe_turn(pe, B, it, (par, "X1"), xg, 1)
            slot_matmuls(pe, n, 9, B, it, keys, a_hi, a_lo, 2)
            if nxt:
                pe.wait_ge(B.free_sem((par, "X1")), B.after(it, (par, "X1")))
                first = [(par, "U00"), (par, "U01")]
                for j in range(10, 14):
                    slot_matmuls(pe, n, j, B, it, first, x_hi, x_lo, 2 * (j - 10))
                    if j == 11:
                        pe.wait_ge(actd, 2 * n + 2)
                        pe_turn(pe, B, it, (par, "A1"), an, 1)
                for i, key in enumerate(first):
                    add_bias(pe, e + 1, B, key, F * i)
                if nxt2:
                    pe_meta(pe, n + 2, e + 2, B, it, (par, "M"))
            else:
                pe.wait_ge(actd, 2 * n + 2)
                pe_turn(pe, B, it, (par, "A1"), an, 1)
            pe.wait_ge(B.free_sem((par, "A1")), B.after(it, (par, "A1")))
            last = 14 if nxt else 10
            for j in (last, last + 1):
                slot_matmuls(pe, n, j, B, it, keys, a_hi, a_lo, 4 + 2 * (j - last))
            for i, key in enumerate(keys):
                add_bias(pe, e, B, key, 2 * F + 512 * i)

        def act_block(act, n, B, it, par, nxt):
            split_hi(act, n, 7)
            split_hi(act, n, 8)
            take_hi(act, B, it, (par, "A0"), a_hi, 0, hi_a)
            split_hi(act, n, 9)
            split_hi(act, n, 10)
            if nxt:
                take_hi(act, B, it, (par, "X0"), x_hi, 0, hi_x)
            split_hi(act, n, 11)
            if nxt:
                take_hi(act, B, it, (par, "X1"), x_hi, 1, hi_x)
                split_hi(act, n, 12)
            act_sigmoid(act, n, B, it, par, 1)
            if nxt:
                split_hi(act, n, 13)
                split_hi(act, n, 14)
            take_hi(act, B, it, (par, "A1"), a_hi, 1, hi_a)
            if nxt:
                for j in (15, 16, 17):
                    split_hi(act, n, j)
                act_sigmoid(act, n + 1, B, it, par, 0)
                split_hi(act, n, 18)
            act.wait_ge(rows_out, n + 1)
            for i in range(2):
                key = (par, f"D{i}")
                act.wait_ge(B.fill_sem(key), B.count(it, key))
                act.activation(y[:, 512 * i:512 * i + 512], B.tile(key)[:, :], ACT.Copy).then_inc(B.free_sem(key), 1)

        def dve_block(dve, n, e, B, it, par, nxt, nxt2):
            lo = lambda *js: [split_lo(dve, n, j) for j in js if j not in POOL_LO]
            lo(7, 8)
            take_lo(dve, B, it, (par, "A0"), a_hi, a_lo, 0, hi_a, 2 * n + 1)
            lo(9, 10)
            if nxt:
                take_lo(dve, B, it, (par, "X0"), x_hi, x_lo, 0, hi_x, 2 * n + 3)
            dve_swiglu(dve, n, B, it, par, 1, 0)
            lo(11)
            if nxt:
                take_lo(dve, B, it, (par, "X1"), x_hi, x_lo, 1, hi_x, 2 * n + 4)
                lo(12)
            dve_swiglu(dve, n, B, it, par, 1, 1)
            if nxt:
                dve_to_row(dve, n + 1, 1 - par, n)
                lo(13)
                if nxt2:
                    dve_sel(dve, n + 2, e + 2, 0)
            take_lo(dve, B, it, (par, "A1"), a_hi, a_lo, 1, hi_a, 2 * n + 2)
            if nxt:
                lo(15, 16)
                dve_swiglu(dve, n + 1, B, it, par, 0, 0)
                if nxt2:
                    dve_rows(dve, B, it, (par, "M"))
                lo(17)
                dve_swiglu(dve, n + 1, B, it, par, 0, 1)
                lo(18)

        def pool_block(pool, n, B, it, par, nxt, nxt2):
            split_lo(pool, n, 10)
            if nxt:
                split_lo(pool, n, 14)
            if nxt2:
                pool_gather(pool, B, it, (par, "M"))
            pool_scatter(pool, n, B, it, par)

        def lead_in(eng, what, n, e, off, B, it):
            first = B is pro
            if what == "pe":
                pe_meta(eng, n, e, B, it, (0, "M"))
                eng.wait_ge(gathered, 16 * n + 16)
                for i in range(2):
                    pe_turn(eng, B, it, (0, f"X{i}"), xg, i)
                eng.wait_ge(B.free_sem((0, "X1")), B.after(it, (0, "X1")))
                if first:
                    pe_meta(eng, 1, 1, B, it, (1, "M"))
                keys = [(0, "U00"), (0, "U01")]
                for j in range(4):
                    slot_matmuls(eng, n, j, B, it, keys, x_hi, x_lo, 2 * j)
                for i, key in enumerate(keys):
                    add_bias(eng, e, B, key, F * i)
            if what == "act":
                for i in range(2):
                    take_hi(eng, B, it, (0, f"X{i}"), x_hi, i, hi_x)
                for j in range(7):
                    split_hi(eng, n, j)
                act_sigmoid(eng, n, B, it, 0, 0)
            if what == "dve":
                dve_sel(eng, n, e, off)
                dve_rows(eng, B, it, (0, "M"))
                dve_to_row(eng, n, 0, None if first else n)
                for i in range(2):
                    take_lo(eng, B, it, (0, f"X{i}"), x_hi, x_lo, i, hi_x, 2 * n + i + 1)
                if first:
                    dve_sel(eng, 1, 1, 0)
                    dve_rows(eng, B, it, (1, "M"))
                for j in range(6):
                    split_lo(eng, n, j)
                dve_swiglu(eng, n, B, it, 0, 0, 0)
                dve_swiglu(eng, n, B, it, 0, 0, 1)
                split_lo(eng, n, 6)
            if what == "pool":
                pool_gather(eng, B, it, (0, "M"))
                if first:
                    pool_gather(eng, B, it, (1, "M"))

        block = ctx.enter_context(nc.Block())

        def program(eng, what):
            def body(n, e, B, it, par, nxt, nxt2):
                if what == "pe":
                    pe_block(eng, n, e, B, it, par, nxt, nxt2)
                if what == "act":
                    act_block(eng, n, B, it, par, nxt)
                if what == "dve":
                    dve_block(eng, n, e, B, it, par, nxt, nxt2)
                if what == "pool":
                    pool_block(eng, n, B, it, par, nxt, nxt2)

            lead_in(eng, what, 0, 0, 0, pro, 0)
            with eng.Fori(0, PAIRS - 1) as i:
                for par in range(2):
                    body(2 * i + par, 2 * i + par, main, i, par, True, True)
            for par in range(2):
                body(E - 2 + par, E - 2 + par, main, PAIRS - 1, par, par == 0, False)
            total = eng.value_load(over[0:1, 2 * NOV:2 * NOV + 1], min_val=0, max_val=NOV)
            with eng.Fori(0, NOV) as i:
                with eng.If(total > i):
                    e = eng.value_load(over[0:1, ds(i, 1)], min_val=0, max_val=E - 1)
                    off = eng.value_load(over[0:1, ds(i + NOV, 1)], min_val=0, max_val=3 * P)
                    lead_in(eng, what, E + i, e, off, more, i)
                    body(E + i, e, more, i, 0, False, False)

        @block.sync
        def _(sp):
            load_lead_in(sp, 0, 0)
            with sp.Fori(0, E - 1) as n:
                load_block(sp, n, n, True)
            load_block(sp, E - 1, E - 1, False)
            total = sp.value_load(over[0:1, 2 * NOV:2 * NOV + 1], min_val=0, max_val=NOV)
            with sp.Fori(0, NOV) as i:
                with sp.If(total > i):
                    e = sp.value_load(over[0:1, ds(i, 1)], min_val=0, max_val=E - 1)
                    load_lead_in(sp, E + i, e)
                    load_block(sp, E + i, e, False)

        @block.gpsimd
        def _(pool):
            for r in range(RING):
                pool.sem_inc(lo_w[r], 2)
                pool.sem_inc(used[r], 1)
            for B in (main, pro, more):
                for f in B.freed:
                    pool.sem_inc(f, 1)
            pool.sem_inc(rows_out, 1)
            pool.memset(xg[:, :], 0.0).then_inc(cleared, 1)
            pool.wait_ge(cleared, 1)
            program(pool, "pool")

        @block.tensor
        def _(pe):
            program(pe, "pe")

        @block.scalar
        def _(act):
            program(act, "act")

        @block.vector
        def _(dve):
            program(dve, "dve")


def final_norm(nc, psum, ext, keep, c_dram, out):
    with ExitStack() as ctx:
        sb = lambda name, shape, dt=F32: ctx.enter_context(nc.sbuf_tensor("final_" + name, shape, dt))
        sem = phase_semaphores(nc, ctx, "final")
        x, gates = keep["x"], keep["gates"]
        c = sb("contributions", [P, NT, TOPK, D])
        w = sb("final_w", [P, D])
        sq = sb("final_squares", [P, D])
        ss = sb("final_sums", [P, NT])
        c_in = [sem(f"contributions_in{t}") for t in range(NT)]
        w_in = sem("final_w_in")
        acc = sem("sum_chain")
        sumd = sem("final_sum_done")
        ssd = sem("final_squares_done")
        var = sem("final_var_done")
        root = sem("final_root_done")
        rch = sem("final_chain")
        outd = sem("rows_done")
        stored = sem("out_stored")
        block = ctx.enter_context(nc.Block())

        @block.sync
        def _(sp):
            cd = c_dram.rearrange("(k t p) d -> p t k d", k=TOPK, p=P)
            for t in range(NT):
                sp.dma_start(c[:, t, :, :], cd[:, t, :, :]).then_inc(c_in[t], 16)
            sp.dma_start(w[:, :], ext["final_norm_w"].partition_broadcast(P)).then_inc(w_in, 16)
            od = out.rearrange("(t p) d -> p t d", p=P)
            for t in range(NT):
                sp.wait_ge(outd, t + 1)
                sp.dma_start(od[:, t, :], x[:, t, :]).then_inc(stored, 16)
            sp.wait_ge(stored, 16 * NT)

        @block.scalar
        def _(act):
            for t in range(NT):
                act.wait_ge(sumd, t + 1)
                if t:
                    act.wait_ge(ssd, t)
                act.activation(sq[:, :], x[:, t, :], ACT.Square, accum_out=ss[:, t:t + 1]).then_inc(ssd, 1)
                act.wait_ge(var, t + 1)
                act.activation(ss[:, t:t + 1], ss[:, t:t + 1], ACT.Sqrt).then_inc(root, 1)

        @block.vector
        def _(dve):
            ch = Chain(dve, acc)

            def total(t):
                dve.wait_ge(c_in[t], 16)
                for k in range(TOPK):
                    ins = dve.scalar_tensor_tensor(out=x[:, t, :], in0=c[:, t, k, :], scalar=gates[:, t, k:k + 1],
                                                   in1=x[:, t, :], op0=ALU.mult, op1=ALU.add)
                    if k < TOPK - 1:
                        ch(ins)
                ins.then_inc(sumd, 1)

            def scale(t):
                dve.wait_ge(ssd, t + 1)
                dve.tensor_scalar(ss[:, t:t + 1], ss[:, t:t + 1], 1.0 / D, RMS_EPS, ALU.mult, ALU.add).then_inc(var, 1)
                dve.wait_ge(root, t + 1)
                ch(dve.reciprocal(ss[:, t:t + 1], ss[:, t:t + 1]))
                dve.wait_ge(w_in, 16)
                dve.scalar_tensor_tensor(out=x[:, t, :], in0=x[:, t, :], scalar=ss[:, t:t + 1], in1=w[:, :],
                                         op0=ALU.mult, op1=ALU.mult).then_inc(outd, 1)

            total(0)
            for t in range(NT):
                if t + 1 < NT:
                    total(t + 1)
                scale(t)


def rwkv_constants():
    s, t = np.arange(P)[:, None], np.arange(P)[None, :]
    out = []
    for before, upto in ((s < t, s <= t), (s > t, s >= t)):
        out += [-1.0 * before, -1.0 * upto, 1.0 * before, 1.0 * upto]
    for lv in range(1, NLEV + 1):
        out.append(1.0 * ((s >> lv == t >> lv) & (s >> (lv - 1) != t >> (lv - 1))))
    out.append(1.0 * (s // HD == t // HD))
    out.append(1.0 * (s // HD == np.arange(2)[None, :]))
    return np.concatenate(out, axis=1).astype(np.float32)


def attention_mask():
    qc = QC * np.arange(NT)[:, None, None] + np.arange(QC)[None, :, None]
    kc = QC * np.arange(NT)[:, None, None] - PADC + np.arange(KC)[None, None, :]
    start = np.clip(qc - WIN // 2, 0, GRID - WIN)
    m = np.where((kc >= start) & (kc < start + WIN), 0.0, -1e30).astype(np.float32)
    return np.broadcast_to(m.transpose(1, 0, 2)[None], (ROWS, QC, NT, KC)).reshape(P, NT * KC)


def router_constants():
    row = lambda v, n: np.repeat(np.asarray(v, np.float32), n)
    rc = np.concatenate([row(T * np.arange(TOPK), E), row(P * np.arange(NT) - FAR, E), np.arange(NOV, dtype=np.float32)])
    p = np.arange(P)
    tri = np.concatenate([1.0 * (p[:, None] < p[None, :]), np.ones((P, P))], axis=1)
    selb = np.zeros((P, E, P))
    for part in range(3):
        selb[E * part + np.arange(E), np.arange(E), :] = 1.0
    b16 = lambda v: (v.astype(np.float32).view(np.uint32) >> 16).astype(np.uint16)
    return {"c_router": np.tile(rc[None], (P, 1)), "c_tri": b16(tri), "c_selb": b16(selb.reshape(P, E * P)),
            "c_prow": b16(np.tile(p[:, None], (1, 2))), "c_iota": np.arange(T, dtype=np.float32)}


def build(nc, ext, out):
    nrows = vec_rows()[1]
    with ExitStack() as ctx:
        sb = lambda name, shape, dt=F32, c=ctx: c.enter_context(nc.sbuf_tensor(name, shape, dt))
        psum = [ctx.enter_context(nc.psum_tensor(f"bank{i}", [P, 512], F32)) for i in range(8)]
        vpad = nc.dram_tensor("v_padded", [ROWS * PGRID, C], F32).ap()
        keep = {"x": sb("x", [P, NT, D]), "ident": sb("ident", [P, P]), "vec": sb("vec", [P, nrows])}
        with ExitStack() as mixer:
            keep["PTb"] = sb("proj_rwkv", [P, NTILE - N_ATT_TILES, T], c=mixer)
            keep["att"] = sb("att", [P, NT, C], c=mixer)
            keep["rk"] = sb("rk", [P, NT, C], c=mixer)
            keep["VN"] = sb("v_nat_rwkv", [P, NT, C], c=mixer)
            keep["coef"] = sb("bonus_coef", [P, NT, NH], c=mixer)
            with ExitStack() as first:
                keep["PTa"] = sb("proj_att", [P, N_ATT_TILES, T], c=first)
                in_projection(nc, psum, ext, keep)
                attention(nc, psum, ext, {**keep}, vpad)
            rwkv(nc, psum, ext, keep)
            mixed_output(nc, psum, ext, keep)
        hn_dram = nc.dram_tensor("hn_rows", [T, D], F32).ap()
        c_dram = nc.dram_tensor("contribution_rows", [TOPK * T, D], F32).ap()
        for name, shape, dt in (("gates", [P, NT, TOPK], F32), ("posm", [P, NT, E], F32), ("meta", [P, NT, E, 2], BF16),
                                ("over", [P, 2 * NOV + 1], I32), ("biasb", [P, 3 * F], BF16), ("iota", [P, T], F32),
                                ("selb", [P, E, P], BF16), ("prow", [P, 2], BF16)):
            keep[name] = sb(name, shape, dt)
        router(nc, psum, ext, keep, hn_dram)
        experts(nc, psum, ext, keep, hn_dram, c_dram)
        final_norm(nc, psum, ext, keep, c_dram, out)


def lay_out(a):
    lines = lambda v: np.ascontiguousarray(v).reshape(-1, P)
    ext = {n: a[n][0] for n in ("x", "w_in", "w_o", "router_w", "router_b", "expert_w_up", "expert_b_up",
                                "expert_w_down", "expert_b_down")}
    ext.update({n: lines(a[n]) for n in ("norm1_w", "norm2_w", "attn_norm_w")})
    ext.update({n: lines(a["rwkv_" + n]) for n in ("mu_prev", "mu_next", "w0", "a0", "k_k", "k_a", "r_k")})
    ext.update({n: a["rwkv_" + n].reshape(P, C) for n in ("w2", "a2", "g2")})
    ext.update({n: a["rwkv_" + n].reshape(C) for n in ("ln_w", "ln_b")})
    ext["norm2_row"] = a["norm2_w"].reshape(D)
    ext["final_norm_w"] = a["final_norm_w"]
    wide = np.pad(a["attn_rpb"][0], ((0, 0), (0, 0), (QC, QC)))
    ext["rpb"] = np.stack([wide[:, :, QC + WIN // 2 - 1 - c:][:, :, :KC] for c in range(QC)])
    ext["c_ident"] = np.eye(P, dtype=np.float32)
    ext["c_att_mask"] = attention_mask()
    ext["c_rwkv"] = rwkv_constants()
    ext.update(router_constants())
    return {n: np.ascontiguousarray(v) for n, v in ext.items()}


def kernel(**inputs):
    import concourse.bacc as bacc
    from concourse.bass_utils import run_bass_kernel_spmd

    nc = bacc.Bacc("TRN2", target_bir_lowering=False, num_devices=1)
    arrays, ext = {}, {}
    for name, a in lay_out({k: np.asarray(v) for k, v in inputs.items()}).items():
        arrays[f"in_{name}"] = a
        ext[name] = nc.dram_tensor(f"in_{name}", a.shape, mybir.dt.from_np(a.dtype), kind="ExternalInput").ap()
    out = nc.dram_tensor("out", (T, D), F32, kind="ExternalOutput").ap()
    build(nc, ext, out)
    r = run_bass_kernel_spmd(nc, [arrays], core_ids=[0])
    return r.results[0]["out"].reshape(1, T, D)
```
